# Optimizing a Trainium2 kernel written in Bass

```python
import jax, jax.numpy as jnp
from jax import lax
import numpy as np

D_MODEL = 2048
BATCH = 1
SEQ = 256
DEPTH = 2

N_A = DEPTH // 2
N_B = DEPTH - N_A
GLA_HEADS = 4
GLA_DK = D_MODEL // 2 // GLA_HEADS
GLA_DV = D_MODEL // GLA_HEADS
GLA_QK = GLA_HEADS * GLA_DK
GLA_V = GLA_HEADS * GLA_DV
GLA_GATE_RANK = 16
GLA_TAU = 16.0
GLA_CHUNK = 64
MLA_HEADS = 16
MLA_NOPE = 128
MLA_ROPE = 64
MLA_V = 128
MLA_QK = MLA_NOPE + MLA_ROPE
Q_LORA = 512
KV_LORA = 512
ROPE_THETA = 10000.0
Q_BLOCK = 128
D_FF = -(-8 * D_MODEL // (3 * 256)) * 256
EPS = 1e-6

kernel_name = 'yoco_gla_mla_adaln_hybrid'

def rms_norm(x, gain):
    x32 = x.astype(jnp.float32)
    y = x32 * lax.rsqrt(jnp.mean(x32 * x32, axis=-1, keepdims=True) + EPS)
    return (y * gain.astype(jnp.float32)).astype(x.dtype)

def modulate(x, gain, shift, scale):
    return rms_norm(x, gain) * (1 + scale[:, None, :]) + shift[:, None, :]

def rope(x, cos, sin):
    half = MLA_ROPE // 2
    x32 = x.astype(jnp.float32)
    x1, x2 = x32[..., :half], x32[..., half:]
    return jnp.concatenate([x1 * cos - x2 * sin, x2 * cos + x1 * sin], axis=-1).astype(x.dtype)

def swiglu(h, w_gu, w_down):
    g, u = jnp.split(h @ w_gu, 2, axis=-1)
    return (jax.nn.silu(g) * u) @ w_down

def gla_mixer(h, w_in, w_alpha, b_alpha, onorm, w_out):
    B, S, _ = h.shape
    nc = S // GLA_CHUNK
    proj = h @ w_in
    q, k, v, g, a_lr = jnp.split(proj, [GLA_QK, 2 * GLA_QK, 2 * GLA_QK + GLA_V, 2 * GLA_QK + 2 * GLA_V], axis=-1)
    log_alpha = jax.nn.log_sigmoid((a_lr @ w_alpha + b_alpha).astype(jnp.float32)) / GLA_TAU

    def to_chunks(t, d):
        return t.astype(jnp.float32).reshape(B, nc, GLA_CHUNK, GLA_HEADS, d).transpose(1, 0, 3, 2, 4)

    qc = to_chunks(q, GLA_DK) * (GLA_DK ** -0.5)
    kc = to_chunks(k, GLA_DK)
    vc = to_chunks(v, GLA_DV)
    bcum = jnp.cumsum(to_chunks(log_alpha, GLA_DK), axis=3)
    b_last = bcum[:, :, :, -1:, :]
    q_dec = qc * jnp.exp(bcum)
    k_intra = kc * jnp.exp(-bcum)
    k_state = kc * jnp.exp(b_last - bcum)
    causal = jnp.tril(jnp.ones((GLA_CHUNK, GLA_CHUNK), dtype=bool))
    att = jnp.einsum('nbhik,nbhjk->nbhij', q_dec, k_intra)
    att = jnp.where(causal, att, 0.0)
    o_intra = jnp.einsum('nbhij,nbhjv->nbhiv', att, vc)

    def step(state, inp):
        q_n, k_n, v_n, dec_n = inp
        o_n = jnp.einsum('bhck,bhkv->bhcv', q_n, state)
        state = dec_n[..., None] * state + jnp.einsum('bhck,bhcv->bhkv', k_n, v_n)
        return state, o_n

    s0 = jnp.zeros((B, GLA_HEADS, GLA_DK, GLA_DV), jnp.float32)
    _, o_inter = lax.scan(step, s0, (q_dec, k_state, vc, jnp.exp(b_last[:, :, :, 0, :])))
    o = (o_intra + o_inter).transpose(1, 0, 3, 2, 4).reshape(B, S, GLA_HEADS, GLA_DV)
    o = rms_norm(o, onorm).astype(h.dtype)
    o = o * jax.nn.silu(g).reshape(B, S, GLA_HEADS, GLA_DV)
    return o.reshape(B, S, GLA_V) @ w_out

def shared_kv(x_mid, c, ada_w, ada_b, norm, w_dkv, lat_norm, w_ukv, k_norm, cos, sin):
    B, S, _ = x_mid.shape
    shift, scale = jnp.split(jax.nn.silu(c) @ ada_w + ada_b, 2, axis=-1)
    h = modulate(x_mid, norm, shift, scale)
    ckv = h @ w_dkv
    c_lat = rms_norm(ckv[..., :KV_LORA], lat_norm)
    k_pe = rope(ckv[..., KV_LORA:], cos, sin)
    kv = (c_lat @ w_ukv).reshape(B, S, MLA_HEADS, MLA_NOPE + MLA_V)
    k_nope, v = kv[..., :MLA_NOPE], kv[..., MLA_NOPE:]
    k = jnp.concatenate([k_nope, jnp.broadcast_to(k_pe[:, :, None, :], (B, S, MLA_HEADS, MLA_ROPE))], axis=-1)
    k = rms_norm(k, k_norm)
    return k, v

def mla_mixer(h, k, v, w_dq, q_lat_norm, w_uq, q_norm, w_out, cos, sin):
    B, S, _ = h.shape
    cq = rms_norm(h @ w_dq, q_lat_norm)
    q = (cq @ w_uq).reshape(B, S, MLA_HEADS, MLA_QK)
    q = jnp.concatenate([q[..., :MLA_NOPE], rope(q[..., MLA_NOPE:], cos[:, :, None, :], sin[:, :, None, :])], axis=-1)
    q = rms_norm(q, q_norm)
    nb = S // Q_BLOCK
    qb = q.reshape(B, nb, Q_BLOCK, MLA_HEADS, MLA_QK).transpose(1, 0, 2, 3, 4)
    key_idx = jnp.arange(S)
    sm_scale = MLA_QK ** -0.5

    def attend(args):
        q_blk, blk = args
        s = jnp.einsum('bqhd,bkhd->bhqk', q_blk, k).astype(jnp.float32) * sm_scale
        q_idx = blk * Q_BLOCK + jnp.arange(Q_BLOCK)
        s = jnp.where(key_idx[None, :] <= q_idx[:, None], s, -jnp.inf)
        p = jax.nn.softmax(s, axis=-1).astype(v.dtype)
        return jnp.einsum('bhqk,bkhd->bqhd', p, v)

    o = lax.map(attend, (qb, jnp.arange(nb)))
    o = o.transpose(1, 0, 2, 3, 4).reshape(B, S, MLA_HEADS * MLA_V)
    return o @ w_out

def setup_inputs(seed: int = 0) -> dict:
    key = jax.random.key(seed)
    ks = jax.random.split(key, 32)
    f32 = jnp.float32
    D = D_MODEL

    def nrm(k, shape, std):
        return jax.random.normal(k, shape, f32) * std

    def gain(k, shape):
        return 1.0 + 0.02 * jax.random.normal(k, shape, f32)

    offset = jax.random.randint(ks[2], (BATCH, 1), 0, 1024, dtype=jnp.int32)
    positions = offset + jnp.arange(SEQ, dtype=jnp.int32)[None, :]
    return {
        'x': nrm(ks[0], (BATCH, SEQ, D), 1.0),
        'c': nrm(ks[1], (BATCH, D), 1.0),
        'positions': positions,
        'ada_w': nrm(ks[3], (DEPTH, D, 6 * D), 0.5 * D ** -0.5),
        'ada_b': nrm(ks[4], (DEPTH, 6 * D), 0.01),
        'norm_mix': gain(ks[5], (DEPTH, D)),
        'norm_ffn': gain(ks[6], (DEPTH, D)),
        'gla_w_in': nrm(ks[7], (N_A, D, 2 * GLA_QK + 2 * GLA_V + GLA_GATE_RANK), D ** -0.5),
        'gla_w_alpha': nrm(ks[8], (N_A, GLA_GATE_RANK, GLA_QK), GLA_GATE_RANK ** -0.5),
        'gla_b_alpha': nrm(ks[9], (N_A, GLA_QK), 0.01),
        'gla_onorm': gain(ks[10], (N_A, GLA_DV)),
        'gla_w_out': nrm(ks[11], (N_A, GLA_V, D), GLA_V ** -0.5),
        'mla_w_dq': nrm(ks[12], (N_B, D, Q_LORA), D ** -0.5),
        'mla_q_lat_norm': gain(ks[13], (N_B, Q_LORA)),
        'mla_w_uq': nrm(ks[14], (N_B, Q_LORA, MLA_HEADS * MLA_QK), Q_LORA ** -0.5),
        'mla_q_norm': gain(ks[15], (N_B, MLA_QK)),
        'mla_w_out': nrm(ks[16], (N_B, MLA_HEADS * MLA_V, D), (MLA_HEADS * MLA_V) ** -0.5),
        'kv_ada_w': nrm(ks[17], (D, 2 * D), 0.5 * D ** -0.5),
        'kv_ada_b': nrm(ks[18], (2 * D,), 0.01),
        'kv_norm': gain(ks[19], (D,)),
        'kv_w_dkv': nrm(ks[20], (D, KV_LORA + MLA_ROPE), D ** -0.5),
        'kv_lat_norm': gain(ks[21], (KV_LORA,)),
        'kv_w_ukv': nrm(ks[22], (KV_LORA, MLA_HEADS * (MLA_NOPE + MLA_V)), KV_LORA ** -0.5),
        'kv_k_norm': gain(ks[23], (MLA_QK,)),
        'ffn_w_gu': nrm(ks[24], (DEPTH, D, 2 * D_FF), D ** -0.5),
        'ffn_w_down': nrm(ks[25], (DEPTH, D_FF, D), D_FF ** -0.5),
    }

def reference(x, c, positions, ada_w, ada_b, norm_mix, norm_ffn, gla_w_in, gla_w_alpha, gla_b_alpha,
              gla_onorm, gla_w_out, mla_w_dq, mla_q_lat_norm, mla_w_uq, mla_q_norm, mla_w_out,
              kv_ada_w, kv_ada_b, kv_norm, kv_w_dkv, kv_lat_norm, kv_w_ukv, kv_k_norm,
              ffn_w_gu, ffn_w_down):
    half = MLA_ROPE // 2
    inv_freq = ROPE_THETA ** (-jnp.arange(half, dtype=jnp.float32) / half)
    ang = positions.astype(jnp.float32)[..., None] * inv_freq
    cos, sin = jnp.cos(ang), jnp.sin(ang)
    k_sh, v_sh = None, None
    for layer in range(DEPTH):
        mod = jax.nn.silu(c) @ ada_w[layer] + ada_b[layer]
        shift_m, scale_m, gate_m, shift_f, scale_f, gate_f = jnp.split(mod, 6, axis=-1)
        if layer < N_A:
            h = modulate(x, norm_mix[layer], shift_m, scale_m)
            mix = gla_mixer(h, gla_w_in[layer], gla_w_alpha[layer], gla_b_alpha[layer],
                            gla_onorm[layer], gla_w_out[layer])
        else:
            j = layer - N_A
            if j == 0:
                k_sh, v_sh = shared_kv(x, c, kv_ada_w, kv_ada_b, kv_norm, kv_w_dkv, kv_lat_norm,
                                       kv_w_ukv, kv_k_norm, cos, sin)
            h = modulate(x, norm_mix[layer], shift_m, scale_m)
            mix = mla_mixer(h, k_sh, v_sh, mla_w_dq[j], mla_q_lat_norm[j], mla_w_uq[j],
                            mla_q_norm[j], mla_w_out[j], cos, sin)
        x = x + gate_m[:, None, :] * mix
        h = modulate(x, norm_ffn[layer], shift_f, scale_f)
        x = x + gate_f[:, None, :] * swiglu(h, ffn_w_gu[layer], ffn_w_down[layer])
    return x


_drawn_inputs = setup_inputs


def setup_inputs(seed=0):
    import zlib

    import numpy as np

    out = dict(_drawn_inputs(seed))
    spreads = {}
    factors = {'ada_b': 3.737,
     'norm_mix': 6.863,
     'norm_ffn': 6.602,
     'gla_b_alpha': 8.0,
     'gla_onorm': 8.0,
     'mla_q_lat_norm': 8.0,
     'mla_q_norm': 8.0,
     'kv_ada_b': 8.0,
     'kv_norm': 8.0,
     'kv_lat_norm': 23.96,
     'kv_k_norm': 8.0}
    for name, (base, spread) in spreads.items():
        noise = np.random.default_rng([zlib.crc32(name.encode()), seed]).standard_normal(out[name].shape)
        drawn = base * np.exp(spread * noise) if base else spread * noise
        out[name] = __import__('jax').numpy.asarray(drawn.astype(out[name].dtype))
    for name, factor in factors.items():
        out[name] = (out[name] * factor).astype(out[name].dtype)
    return out
```

```python
from contextlib import ExitStack

import numpy as np

import concourse.bass as bass
from concourse import mybir

F32 = mybir.dt.float32
F32R = mybir.dt.float32r
I32 = mybir.dt.int32
ALU = mybir.AluOpType
ACT = mybir.ActivationFunctionType
AX = mybir.AxisListType

P = 128
D = 2048
T = 256
NB = D // P
KQ = NB // 4
HEADS_A = 4
DK, DV = D // 2 // HEADS_A, D // HEADS_A
QK_A = HEADS_A * DK
RANK = 16
TAU = 16.0
CH = 64
NCH = T // CH
HEADS_B = 16
NOPE, ROPE, VD = 128, 64, 128
QKD = NOPE + ROPE
HALF = ROPE // 2
LORA = 512
LB = LORA // P
FF = 5632
FFC = (8, 8, 6)
EPS = 1e-6
THETA = 10000.0
GW = 512
NEG = -1e30
TWO_PI = 2.0 * np.pi
PI_A = 6.28125
PI_B = 0.00193500518798828125
PI_C = float(TWO_PI - PI_A - PI_B)
MAGIC = 12582912.0

MOD0, MODKV, MOD1 = 0, 24, 32
C_C, C_NMIX, C_NFFN, C_KVN, C_ON, C_BA, C_QL, C_KL, C_QN, C_KN, C_QT, C_KT, C_END = \
    224, 240, 272, 304, 320, 324, 332, 336, 340, 341, 342, 343, 344

T_LOW, T_GLA, T_WOA, T_FFN0 = 0, 1, 49, 65
T_DKV, T_KPE, T_DQ, T_MLA, T_WOB, T_FFN1, T_END = 201, 205, 206, 210, 226, 242, 378
G_LOW, G_GLA, G_WOA, G_FFN0, G_DKV, G_KPE, G_DQ, G_MLA, G_WOB, G_FFN1, G_END = 0, 1, 13, 17, 51, 52, 53, 54, 70, 74, 108
O_N0, O_GLA, O_NF0, O_FFN0, O_NKV, O_NMX, O_LKV, O_LQ, O_MLA, O_NF1, O_FFN1 = 0, 8, 16, 24, 46, 54, 62, 64, 66, 74, 82
E_N0, E_GLA, E_NF0, E_NKV, E_LKV, E_LQ, E_NF1 = 0, 8, 16, 24, 32, 34, 36
S_N0, S_GLA, S_NF0, S_NKV, S_LKV, S_LQ, S_NF1 = 0, 1, 5, 6, 7, 8, 9
FMA = {O_N0: 0, O_NF0: 8, O_NKV: 16, O_NMX: 24, O_LKV: 32, O_LQ: 34, O_NF1: 36}
U_GLA, U_FFN0, U_MLA, U_WOB, U_FFN1, U_END = 8, 20, 40, 48, 52, 56


def steps(eng, n, peel=False):
    m = n - 1 if peel else n
    if m > 1:
        with eng.Fori(0, m) as i:
            yield i
    else:
        yield from range(m)
    if peel:
        yield n - 1


def ffn_plan(layer):
    t, g, o, u = (T_FFN0, G_FFN0, O_FFN0, U_FFN0) if layer == 0 else (T_FFN1, G_FFN1, O_FFN1, U_FFN1)
    att = {0: ((0,), (0,), (0,), (0,), (0, 1), (0,)), 1: ((0,), (), (), (), (), ())}[layer]
    out, b = [], 0
    for c, n in enumerate(FFC):
        a = att[2 * c]
        out.append(("up", t, g, o, n // 2, u, a, c, b))
        t, g, o, u = t + 4 * n, g + n, o + n, u + len(a) * (n // 2)
        a = att[2 * c + 1]
        out.append(("down", t, g, o - n, 2, u, a, c, b))
        t, g, u = t + 16, g + 4, u + len(a) * 2
        b += 2 * n
    return out


def trunk(nc, x, c, positions, ada_w, ada_b, norm_mix, norm_ffn, gla_w_in, gla_w_alpha, gla_b_alpha, gla_onorm,
          gla_w_out, mla_w_dq, mla_q_lat_norm, mla_w_uq, mla_q_norm, mla_w_out, kv_ada_w, kv_ada_b, kv_norm,
          kv_w_dkv, kv_lat_norm, kv_w_ukv, kv_k_norm, ffn_w_gu, ffn_w_down, out):
    with ExitStack() as ctx:
        def sb(name, shape, dt=F32):
            return ctx.enter_context(nc.sbuf_tensor(name, shape, dt))

        def ps(name, shape):
            return ctx.enter_context(nc.psum_tensor(name, shape, F32))

        def sem(name):
            return ctx.enter_context(nc.semaphore(name))

        raw = sb("raw", [P, 4, 2048])
        whi = sb("whi", [P, 2, 2048], F32R)
        wlo = sb("wlo", [P, 2, 2048], F32R)
        adar = sb("adar", [P, 2, 4, GW])
        acc = sb("acc", [P, GW])
        xt = sb("xt", [P, NB, T])
        hhi = sb("hhi", [P, NB, T], F32R)
        hlo = sb("hlo", [P, NB, T], F32R)
        ahi = sb("ahi", [P, NB, T], F32R)
        alo = sb("alo", [P, NB, T], F32R)
        work = sb("work", [P, 6144])
        cols = sb("cols", [P, C_END])
        mods = sb("mods", [P, 224])
        avec = sb("avec", [P, NB])
        scol = sb("scol", [P, NB])
        ones = sb("ones", [P, P])
        ident = sb("ident", [P, P])
        one256 = sb("one256", [P, T])
        alrt = sb("alrt", [RANK, T])
        wah = sb("wah", [RANK, DK])
        rstd = sb("rstd", [P, T])
        sq = sb("sq", [P, 2, 2 * T])
        ht = sb("ht", [P, 2, 2 * T])
        mask = sb("mask", [P, 3, P])
        csin = sb("csin", [P, 2, 2, HALF])
        kpe = sb("kpe", [P, 2, ROPE])
        nrow = sb("nrow", [P, 64])
        posi = sb("posi", [P, 2], I32)
        cst = sb("cst", [P, 4])
        invf = sb("invf", [P, HALF])
        EPSC, ONEC, HPIC = cst[:, 0:1], cst[:, 1:2], cst[:, 2:3]
        COS, SIN = csin[:, 0], csin[:, 1]

        def wview(lo, hi, **dims):
            pat = {1: "p (a n) -> p a n", 2: "p (a b n) -> p a b n"}[len(dims)]
            return work[:, lo:hi].rearrange(pat, **dims)

        xio = wview(0, 4096, a=2)
        vrow = wview(4096, 4480, a=3)
        a_qk = wview(0, 1024, a=4)
        a_v = wview(1024, 2048, a=2)
        a_sg = wview(2048, 3072, a=4)
        a_c = wview(3072, 3584, a=2)
        a_e = wview(3584, 4864, a=2)
        a_qd = wview(4864, 5376, a=2)
        a_att = wview(5376, 5888, a=2)
        a_l = a_e[:, :, 0:T]
        a_m = a_e[:, :, T:2 * T]
        a_lr = wview(5888, 5920, a=2)
        a_cs = nrow[:, 0:16].rearrange("p (s b n) -> p s b n", s=2, b=2)
        KOFF = [0, 64, 192, 384]
        f_s = wview(0, 1024, a=2)
        f_a = wview(1024, 2048, a=2)
        b_q = wview(0, 768, a=2)
        b_kv = wview(768, 1792, a=2)
        b_qt = wview(1792, 2304, a=2)
        b_kt = wview(2304, 2816, a=2)
        b_rt = wview(2816, 3328, a=2)
        b_kp = wview(3328, 3584, a=2, b=2)
        b_qp = wview(5888, 6144, a=2, b=2)
        b_p = wview(3584, 4352, a=2)
        b_pt = wview(4352, 5120, a=2)
        b_sq = work[:, 5120:5888]
        b_o = work[:, 5120:5632]
        latk = wview(0, 1024, a=4)
        latq = wview(1024, 2048, a=4)
        ang = wview(2048, 2112, a=2)
        angk = wview(2112, 2176, a=2)
        anga = wview(2176, 2240, a=2)
        posf = work[:, 2272:2274]
        krw = wview(2304, 2432, a=2)
        krt = wview(2432, 2688, a=4, b=2)
        b_st = nrow[:, 16:24]
        b_mx, b_sm = nrow[:, 24:28], nrow[:, 28:32]
        kss = nrow[:, 32:34]

        pg = ps("pg", [P, 2, 4, T])
        pt = pg[:, :, :, :].rearrange("p s (t b) n -> p s t (b n)", t=2)
        xo = ps("xo", [P, 2, 512])
        x2 = ps("x2", [P, 512])
        x3 = ps("x3", [P, 512])

        raw_ld = [sem(f"raw_ld{i}") for i in range(4)]
        ada_ld = [sem(f"ada_ld{i}") for i in range(2)]
        par_ld, x_ld, pos_ld, wah_ld, out_st = sem("par_ld"), sem("x_ld"), sem("pos_ld"), sem("wah_ld"), sem("out_st")
        hi_done, lo_done, mm_done, pg_free = sem("hi_done"), sem("lo_done"), sem("mm_done"), sem("pg_free")
        ada_used, modp_ready, mods_done = sem("ada_used"), sem("modp_ready"), sem("mods_done")
        cst_done, dcst_done = sem("cst_done"), sem("dcst_done")
        tr_ready, tr_evac, s_silu = sem("tr_ready"), sem("tr_evac"), sem("s_silu")
        sq_done, ssq_mm, std_done, rstd_done = sem("sq_done"), sem("ssq_mm"), sem("std_done"), sem("rstd_done")
        a_done, n_mul, n_fma, o_hi, o_lo = sem("a_done"), sem("n_mul"), sem("n_fma"), sem("o_hi"), sem("o_lo")
        lr_tr, lr_ready, oa_norm = sem("lr_tr"), sem("lr_ready"), sem("oa_norm")
        la_ready, la_act, la_used, la_dve, kexp, kq_ready = (sem("la_ready"), sem("la_act"), sem("la_used"),
                                                             sem("la_dve"), sem("kexp"), sem("kq_ready"))
        att_ready, att_evac, att_msk, sg_act, oa_ready, og_mul = (sem("att_ready"), sem("att_evac"), sem("att_msk"),
                                                                  sem("sg_act"), sem("oa_ready"), sem("og_mul"))
        f_silu = sem("f_silu")
        rot_c, rot_a, kp_rot, kp_ss = sem("rot_c"), sem("rot_a"), sem("kp_rot"), sem("kp_ss")
        q_rot, bsq, bst, bstd, brs, bqk = sem("q_rot"), sem("bsq"), sem("bst"), sem("bstd"), sem("brs"), sem("bqk")
        tq_ready, tk_ready, te_act, te_dve = sem("tq_ready"), sem("tk_ready"), sem("te_act"), sem("te_dve")
        s_ready, s_mx, s_exp, s_dve = sem("s_ready"), sem("s_mx"), sem("s_exp"), sem("s_dve")
        p_ready, pt_ready, pt_evac, ob_ready, ob_act = (sem("p_ready"), sem("pt_ready"), sem("pt_evac"),
                                                        sem("ob_ready"), sem("ob_act"))
        y_tr, y_ev = sem("y_tr"), sem("y_ev")

        def rows(w):
            return w.rearrange("(k p) n -> p k n", p=P)

        w_in, w_outa = rows(gla_w_in[0]), rows(gla_w_out[0])
        w_dq, w_uq, w_outb = rows(mla_w_dq[0]), rows(mla_w_uq[0]), rows(mla_w_out[0])
        w_dkv, w_ukv = rows(kv_w_dkv), rows(kv_w_ukv)
        w_gu = [rows(ffn_w_gu[i]) for i in range(2)]
        w_dn = [rows(ffn_w_down[i]) for i in range(2)]
        w_ada = {0: rows(ada_w[0]), 1: rows(kv_ada_w), 2: rows(ada_w[1])}

        def ada_src(unit0, rel):
            m, base = (0, MOD0) if unit0 < MODKV else (1, MODKV) if unit0 < MOD1 else (2, MOD1)
            return w_ada[m], (unit0 - base + rel) * GW

        def tile(buf, s, k, n):
            return buf[:, s, 0:k * n].rearrange("p (k n) -> p k n", k=k)

        def y_bank(g):
            return pt[:, g % 4 // 2, g % 2]

        def lines(v):
            return v.rearrange("(a n) -> a n", n=P)

        rowsets = [lines(ada_b[0]), lines(kv_ada_b), lines(ada_b[1]), lines(c[0]), lines(norm_mix[0]),
                   lines(norm_mix[1]), lines(norm_ffn[0]), lines(norm_ffn[1]), lines(kv_norm), lines(gla_onorm[0]),
                   lines(gla_b_alpha[0]), lines(mla_q_lat_norm[0]), lines(kv_lat_norm), lines(mla_q_norm[0][0:NOPE]),
                   lines(kv_k_norm[0:NOPE])]
        pieces, r = [], 0
        for v in rowsets:
            k = 0
            while k < v.shape[0]:
                m = min(v.shape[0] - k, P - r % P)
                pieces.append((v, k, m, r))
                k, r = k + m, r + m
        assert r == C_QT
        par_dmas = len(pieces) + 4

        block = ctx.enter_context(nc.Block())

        @block.sync
        def _(sp):
            def g_tile(t, s, pieces, first=False):
                if not first:
                    sp.wait_ge(lo_done, t - 3)
                for dst, src in pieces:
                    sp.dma_start(dst, src).then_inc(raw_ld[s], 16)

            def by_k(s, w, k0, k, n, col):
                d = tile(raw, s, k, n)
                h = (k + 1) // 2
                return [(d[:, 0:h], w[:, k0:k0 + h, bass.ds(col, n)]),
                        (d[:, h:k], w[:, k0 + h:k0 + k, bass.ds(col, n)])]

            def by_half(s, w, k0, col_a, col_b):
                d = tile(raw, s, 4, GW)
                return [(d[:, :, 0:256], w[:, k0:k0 + 4, bass.ds(col_a, 256)]),
                        (d[:, :, 256:512], w[:, k0:k0 + 4, bass.ds(col_b, 256)])]

            def a_tile(unit, src, j, first=False):
                w, col = src
                if not first:
                    sp.wait_ge(ada_used, (unit * 4 + j - 1) * 4)
                for h in range(2):
                    k0 = 4 * j + 2 * h
                    sp.dma_start(adar[:, j % 2, 2 * h:2 * h + 2, :], w[:, k0:k0 + 2, bass.ds(col, GW)]) \
                        .then_inc(ada_ld[j % 2], 16)

            sp.dma_start(xio, x[0].rearrange("(t p) n -> p t n", p=P)).then_inc(x_ld, 16)
            for u in range(8):
                for j in range(4):
                    a_tile(u, ada_src(0, u), j, first=(u == 0 and j < 2))
                if u == 0:
                    g_tile(0, 0, by_k(0, w_in, 0, NB, RANK, 2 * QK_A + 2 * D), first=True)
            for n in range(3):
                g_tile(1 + n, 1 + n, by_half(1 + n, w_in, 4 * n, 0, QK_A), first=True)
                a_tile(8, ada_src(8, 0), n)
            g_tile(4, 0, by_half(0, w_in, 12, 0, QK_A))
            a_tile(8, ada_src(8, 0), 3)
            for g in (1, 2):
                for j in range(4):
                    t = 1 + 4 * g + j
                    g_tile(t, t % 4, by_k(t % 4, w_in, 4 * j, 4, GW, 2 * QK_A + (g - 1) * D))
                    a_tile(8 + g, ada_src(8, g), j)
            with sp.Fori(1, HEADS_A) as h:
                for g in range(3):
                    for j in range(4):
                        t, s = h * 12 + (1 + 4 * g + j), (1 + j) % 4
                        if g == 0:
                            g_tile(t, s, by_half(s, w_in, 4 * j, h * DK, h * DK + QK_A))
                        else:
                            g_tile(t, s, by_k(s, w_in, 4 * j, 4, GW, h * DV + (2 * QK_A + (g - 1) * D)))
                        a_tile(h * 3 + (8 + g), ada_src(8, h * 3 + g), j)

            def square(w, t0, n):
                for i in steps(sp, n):
                    for u in range(2):
                        for j in range(4):
                            s = (t0 + j) % 4
                            g_tile(i * 8 + (t0 + 4 * u + j), s, by_k(s, w, 4 * j, 4, GW, (i * 2 + u) * GW))

            square(w_outa, T_WOA, 2)

            def ffn(layer):
                for kind, t0, g0, o0, n, u0, att, ch, b0 in ffn_plan(layer):
                    for i in steps(sp, n):
                        for u in range(2):
                            for j in range(4):
                                s = (t0 + j) % 4
                                t = i * 8 + (t0 + 4 * u + j)
                                if kind == "up":
                                    col = (i * 2 + u) * 256 + b0 * P
                                    g_tile(t, s, by_half(s, w_gu[layer], 4 * j, col, col + FF))
                                else:
                                    k = FFC[ch] // 2
                                    g_tile(t, s, by_k(s, w_dn[layer], b0 + k * j, k, GW, (i * 2 + u) * GW))
                                if u in att:
                                    rel = i * len(att) + att.index(u)
                                    a_tile(u0 + rel, ada_src(u0, rel), j)

            ffn(0)
            for j in range(4):
                s = (T_DKV + j) % 4
                g_tile(T_DKV + j, s, by_k(s, w_dkv, 4 * j, 4, GW, 0))
            s = T_KPE % 4
            g_tile(T_KPE, s, by_k(s, w_dkv, 0, NB, ROPE, LORA))
            for j in range(4):
                s = (T_DQ + j) % 4
                g_tile(T_DQ + j, s, by_k(s, w_dq, 4 * j, 4, GW, 0))
            with sp.Fori(0, HEADS_B // 4) as i:
                for u in range(2):
                    pr = i * 2 + u
                    for m in range(2):
                        s = (T_MLA + 2 * u + m) % 4
                        w, n = ((w_uq, 2 * QKD), (w_ukv, 2 * (NOPE + VD)))[m]
                        g_tile(i * 4 + (T_MLA + 2 * u + m), s, by_k(s, w, 0, LB, n, pr * n))
                        for j in (2 * m, 2 * m + 1):
                            a_tile(i * 2 + (40 + u), ada_src(40, i * 2 + u), j)
            for i in steps(sp, 2):
                for u in range(2):
                    for j in range(4):
                        s = (T_WOB + j) % 4
                        g_tile(i * 8 + (T_WOB + 4 * u + j), s, by_k(s, w_outb, 4 * j, 4, GW, (i * 2 + u) * GW))
                        a_tile(i * 2 + (48 + u), ada_src(48, i * 2 + u), j)
            ffn(1)
            sp.wait_ge(y_ev, 8)
            sp.dma_start(out[0].rearrange("(t p) n -> p t n", p=P), xio).then_inc(out_st, 16)
            sp.wait_ge(out_st, 16)

        @block.gpsimd
        def _(pool):
            pool.memset(ident[:], 0.0).then_inc(cst_done, 1)
            pool.memset(mask[:], 0.0).then_inc(cst_done, 1)
            pool.memset(a_att, 0.0).then_inc(cst_done, 1)
            for f in range(HALF):
                ins = pool.memset(invf[:, f:f + 1], float(np.float32(THETA) ** np.float32(-np.float32(f) / HALF)))
            ins.then_inc(cst_done, 1)
            pool.wait_ge(cst_done, 4)
            pool.affine_select(out=ident[:], in_=ident[:], compare_op=ALU.not_equal, fill=1.0, base=0,
                               pattern=[[-1, P]], channel_multiplier=1).then_inc(cst_done, 1)
            for b in (0, 2):
                ins = pool.affine_select(out=mask[:, b, :], in_=mask[:, b, :], compare_op=ALU.is_ge, fill=NEG, base=0,
                                         pattern=[[-1, P]], channel_multiplier=1)
            ins.then_inc(cst_done, 1)

            def lo_part(o, dst, src, hi):
                pool.wait_ge(o_hi, o + 1)
                pool.tensor_tensor(dst, src, hi.bitcast(F32), ALU.subtract).then_inc(o_lo, 1)

            def norm_lo(o0, n, hi, lo, b0=0):
                for j in range(n):
                    b = b0 + 2 * j
                    lo_part(o0 + j, lo[:, b:b + 2, :], ht[:, j % 2, :].rearrange("p (b n) -> p b n", b=2),
                            hi[:, b:b + 2, :])

            pool.dma_start(wah[:], gla_w_alpha[0][:, 0:DK]).then_inc(wah_ld, 16)
            norm_lo(O_N0, 8, hhi, hlo)

            def gla_mask_and_lo(h):
                pool.wait_ge(tr_evac, 5)
                pool.wait_ge(att_evac, h + 1)
                pool.affine_select(out=a_att[:, 0, 0:P], in_=a_att[:, 0, 0:P], compare_op=ALU.is_ge, fill=0.0, base=0,
                                   pattern=[[1, P]], channel_multiplier=-1)
                pool.affine_select(out=a_att[:, 1, P:T], in_=a_att[:, 1, P:T], compare_op=ALU.is_ge, fill=0.0, base=0,
                                   pattern=[[1, P]], channel_multiplier=-1).then_inc(att_msk, 1)
                for e in range(2):
                    lo_part(h * 2 + (O_GLA + e), alo[:, bass.ds(h * 4 + 2 * e, 2), :],
                            ht[:, e, :].rearrange("p (b n) -> p b n", b=2), ahi[:, bass.ds(h * 4 + 2 * e, 2), :])

            with pool.Fori(0, HEADS_A - 1) as h:
                pool.wait_ge(la_ready, h + 1)
                pool.dma_start(wah[:], gla_w_alpha[0][:, bass.ds(h * DK + DK, DK)]).then_inc(wah_ld, 16)
                gla_mask_and_lo(h)
            gla_mask_and_lo(HEADS_A - 1)

            def ffn(layer):
                for kind, t0, g0, o0, n, u0, att, ch, b0 in ffn_plan(layer):
                    if kind == "up":
                        for i in steps(pool, n):
                            for u in range(2):
                                lo_part(i * 2 + (o0 + u), alo[:, bass.ds(i * 4 + 2 * u, 2), :],
                                        f_a[:, u, :].rearrange("p (b n) -> p b n", b=2),
                                        ahi[:, bass.ds(i * 4 + 2 * u, 2), :])

            norm_lo(O_NF0, 8, hhi, hlo)
            ffn(0)
            norm_lo(O_NKV, 8, hhi, hlo)
            norm_lo(O_NMX, 8, hhi, hlo)

            def rotate(r1, r2, cos, sin, tmp, done, base):
                for k, (a, b) in enumerate(((r1, cos), (r2, sin), (r2, cos), (r1, sin))):
                    ins = pool.tensor_tensor(tmp[k], a, b, ALU.mult)
                ins.then_inc(done, 1)
                pool.wait_ge(done, base + 1)
                pool.tensor_tensor(r1, tmp[0], tmp[1], ALU.subtract)
                pool.tensor_tensor(r2, tmp[2], tmp[3], ALU.add).then_inc(done, 1)

            pool.wait_ge(pg_free, G_KPE + 1)
            pool.wait_ge(rot_a, 3)
            rotate(kpe[:, :, 0:HALF], kpe[:, :, HALF:ROPE], COS, SIN, [krt[:, k] for k in range(4)], kp_rot, 0)
            norm_lo(O_LKV, 2, ahi, alo, 0)
            norm_lo(O_LQ, 2, ahi, alo, LB)

            with pool.Fori(0, HEADS_B // 4) as i:
                for u in range(2):
                    pr = i * 2 + u
                    pool.wait_ge(pg_free, i * 4 + (G_MLA + 2 * u + 1))
                    q4 = b_q.rearrange("p t (h n) -> p t h n", h=2)
                    cs = [z[:, :, None, :].broadcast_to([P, 2, 2, HALF]) for z in (COS, SIN)]
                    tmp = [ht[:, k // 2, (k % 2) * 128:(k % 2) * 128 + 128].rearrange("p (t h n) -> p t h n", t=2, h=2)
                           for k in range(4)]
                    pool.wait_ge(o_lo, pr + O_MLA)
                    rotate(q4[:, :, :, NOPE:NOPE + HALF], q4[:, :, :, NOPE + HALF:QKD], cs[0], cs[1], tmp,
                           q_rot, pr * 2)
                    lo_part(pr + O_MLA, hlo[:, bass.ds(pr * 2, 2), :], b_o.rearrange("p (b n) -> p b n", b=2),
                            hhi[:, bass.ds(pr * 2, 2), :])
            norm_lo(O_NF1, 8, hhi, hlo)
            ffn(1)

        @block.scalar
        def _(act):
            def hi(t, s4, s2, n4, free=True, n=2048):
                act.wait_ge(raw_ld[s4], n4 * 32 + 32)
                if free:
                    act.wait_ge(mm_done, t - 1)
                act.activation(whi[:, s2, 0:n], raw[:, s4, 0:n], ACT.Copy).then_inc(hi_done, 1)

            def his(t0, per, i, first, count):
                for k in range(first, first + count):
                    hi(i * per + (t0 + k), (t0 + k) % 4, (t0 + k) % 2, i * (per // 4) + (t0 + k) // 4)

            for t in range(2):
                act.dma_start(posi[:, t:t + 1], positions[0, t * P:(t + 1) * P].rearrange("(p a) -> p a", a=1)) \
                    .then_inc(pos_ld, 16)
            for v, k, m, r in pieces:
                act.dma_start(vrow[r % P:r % P + m, r // P, :], v[k:k + m, :]).then_inc(par_ld, 16)
            for r, v in ((C_QT, mla_q_norm[0]), (C_KT, kv_k_norm)):
                for h in range(2):
                    act.dma_start(vrow[r % P:r % P + 1, r // P, ROPE * h:ROPE * (h + 1)],
                                  v[NOPE:QKD].rearrange("(a n) -> a n", a=1)).then_inc(par_ld, 16)
            act.wait_ge(tr_evac, 1)
            act.activation(scol[:], cols[:, C_C:C_C + NB], ACT.Silu).then_inc(s_silu, 1)

            def squares(e0, src, n):
                for j in range(n):
                    if e0 + j >= 2:
                        act.wait_ge(ssq_mm, e0 + j - 1)
                    act.activation(sq[:, j % 2, :].rearrange("p (b n) -> p b n", b=2), src[:, 2 * j:2 * j + 2, :],
                                   ACT.Square).then_inc(sq_done, 1)

            def std(e, depth):
                act.wait_ge(ssq_mm, e)
                act.activation(rstd[:], x2[:, 0:T], ACT.Sqrt, bias=EPSC, scale=1.0 / depth).then_inc(std_done, 1)

            def norm_hi(o0, n, dst, b0=0):
                for j in range(n):
                    act.wait_ge(n_fma, FMA[o0] + j + 1)
                    act.activation(dst[:, b0 + 2 * j:b0 + 2 * j + 2, :],
                                   ht[:, j % 2, :].rearrange("p (b n) -> p b n", b=2), ACT.Copy).then_inc(o_hi, 1)

            act.wait_ge(tr_evac, 5)
            act.wait_ge(dcst_done, 3)
            squares(E_N0, xt, 8)
            std(E_N0 + 8, D)
            hi(0, 0, 0, 0, free=False, n=NB * RANK)
            norm_hi(O_N0, 8, hhi)
            hi(1, 1, 1, 0, free=False)

            with act.Fori(0, HEADS_A) as h:
                his(T_GLA, 12, h, 1, 1)
                act.wait_ge(la_ready, h + 1)
                for b in range(2):
                    ins = act.activation(a_l[:, b, :], x2[:, b * T:(b + 1) * T], ACT.Identity,
                                         bias=cols[:, bass.ds(h * 2 + (C_BA + b), 1)])
                ins.then_inc(la_act, 1)
                act.wait_ge(la_act, h * 4 + 1)
                act.activation(a_m, a_l, ACT.Abs).then_inc(la_act, 1)
                act.wait_ge(la_act, h * 4 + 2)
                act.activation(a_m, a_m, ACT.Exp, scale=-1.0).then_inc(la_act, 1)
                act.wait_ge(la_act, h * 4 + 3)
                act.activation(a_m, a_m, ACT.Ln, bias=ONEC).then_inc(la_act, 1)
                his(T_GLA, 12, h, 2, 3)
                act.wait_ge(la_dve, h * 4 + 4)
                for n in range(NCH):
                    for b in range(2):
                        act.activation(a_e[:, b, KOFF[n]:KOFF[n] + CH * (n + 1)], a_c[:, b, 0:CH * (n + 1)], ACT.Exp,
                                       bias=a_cs[:, 0, b, n:n + 1], scale=1.0 / TAU)
                        ins = act.activation(a_qd[:, b, CH * n:CH * (n + 1)], a_c[:, b, CH * n:CH * (n + 1)], ACT.Exp,
                                             bias=a_cs[:, 1, b, n:n + 1], scale=-1.0 / TAU)
                ins.then_inc(kexp, 1)
                his(T_GLA, 12, h, 5, 8)
                act.wait_ge(mm_done, h * 12 + (T_GLA + 12))
                act.activation(a_sg, pg[:, 0], ACT.Sigmoid).then_inc(sg_act, 1)
                act.wait_ge(oa_ready, h + 1)
                for e in range(2):
                    act.wait_ge(ssq_mm, h * 2 + (E_GLA + e - 1))
                    act.activation(sq[:, e, :], xo[:, e, :], ACT.Square).then_inc(sq_done, 1)
                std(h * 2 + (E_GLA + 2), DV)
                for e in range(2):
                    act.wait_ge(og_mul, h * 2 + e + 1)
                    act.activation(ahi[:, bass.ds(h * 4 + 2 * e, 2), :],
                                   ht[:, e, :].rearrange("p (b n) -> p b n", b=2), ACT.Copy).then_inc(o_hi, 1)

            def plain(t0, n):
                for i in steps(act, n):
                    his(t0, 8, i, 1, 8)

            def ffn(layer):
                last_down = T_WOA + 16 if layer == 0 else T_WOB + 16
                for kind, t0, g0, o0, n, u0, att, ch, b0 in ffn_plan(layer):
                    if kind == "down":
                        if layer == 1 and ch == 2:
                            for i in steps(act, n, peel=True):
                                his(t0, 8, i, 1, 7 if isinstance(i, int) and i == n - 1 else 8)
                        else:
                            plain(t0, n)
                        last_down = t0 + 16
                        continue
                    act.wait_ge(mm_done, last_down)
                    for i in steps(act, n):
                        for u in range(2):
                            his(t0 + 4 * u, 8, i, 1, 4)
                            act.wait_ge(mm_done, i * 8 + (t0 + 4 * u + 4))
                            act.activation(f_s[:, u, :].rearrange("p (b n) -> p b n", b=2),
                                           pg[:, (g0 + u) % 2, 0:2], ACT.Silu).then_inc(f_silu, 1)
                            act.wait_ge(pg_free, i * 2 + (g0 + u + 1))
                            act.activation(ahi[:, bass.ds(i * 4 + 2 * u, 2), :],
                                           f_a[:, u, :].rearrange("p (b n) -> p b n", b=2), ACT.Copy).then_inc(o_hi, 1)

            plain(T_WOA, 2)
            act.wait_ge(pg_free, G_FFN0)
            squares(E_NF0, xt, 8)
            std(E_NF0 + 8, D)
            norm_hi(O_NF0, 8, hhi)
            ffn(0)
            act.wait_ge(pg_free, G_DKV)
            squares(E_NKV, xt, 8)
            std(E_NKV + 8, D)
            norm_hi(O_NKV, 8, hhi)
            his(T_DKV, 4, 0, 1, 4)
            his(T_KPE, 4, 0, 1, 1)
            act.wait_ge(rot_c, 8)
            act.activation(SIN, ang, ACT.Sin).then_inc(rot_a, 1)
            act.activation(anga, ang, ACT.Abs).then_inc(rot_a, 1)
            act.wait_ge(rot_a, 2)
            act.activation(COS, anga, ACT.Sin, bias=HPIC, scale=-1.0).then_inc(rot_a, 1)
            act.wait_ge(mm_done, T_DQ)
            norm_hi(O_NMX, 8, hhi)
            act.wait_ge(pg_free, G_DKV + 1)
            squares(E_LKV, latk, 2)
            std(E_LKV + 2, LORA)
            norm_hi(O_LKV, 2, ahi, 0)
            his(T_DQ, 4, 0, 1, 4)
            act.wait_ge(pg_free, G_DQ + 1)
            squares(E_LQ, latq, 2)
            std(E_LQ + 2, LORA)
            norm_hi(O_LQ, 2, ahi, LB)

            with act.Fori(0, HEADS_B // 4) as i:
                for u in range(2):
                    pr = i * 2 + u
                    his(T_MLA + 2 * u, 4, i, 1, 2)
                    act.wait_ge(q_rot, pr * 2 + 2)
                    act.wait_ge(o_lo, pr + O_MLA)
                    act.activation(b_sq, work[:, 0:768], ACT.Square).then_inc(bsq, 1)
                    act.wait_ge(pg_free, i * 4 + (G_MLA + 2 * u + 2))
                    act.wait_ge(bst, pr * 3 + 1)
                    act.activation(b_sq[:, 0:512].rearrange("p (t h n) -> p t h n", t=2, h=2),
                                   b_kv.rearrange("p t (h n) -> p t h n", h=2)[:, :, :, 0:NOPE], ACT.Square) \
                        .then_inc(bsq, 1)
                    act.wait_ge(bst, pr * 3 + 3)
                    act.activation(b_st, b_st, ACT.Sqrt, bias=EPSC, scale=1.0 / QKD).then_inc(bstd, 1)
                    act.wait_ge(tq_ready, pr + 1)
                    act.activation(b_qt.rearrange("p h n -> p (h n)"), xo[:, 0, :], ACT.Copy, scale=cols[:, C_QN:C_QN + 1])
                    act.wait_ge(tk_ready, pr + 1)
                    act.activation(b_kt.rearrange("p h n -> p (h n)"), x3[:], ACT.Copy, scale=cols[:, C_KN:C_KN + 1]) \
                        .then_inc(te_act, 1)
                    for h in range(2):
                        act.wait_ge(s_mx, pr * 2 + h + 1)
                        for q, (a, b) in enumerate(((0, P), (P, 3 * P))):
                            ins = act.activation(b_p[:, h, a:b], b_p[:, h, a:b], ACT.Exp,
                                                 bias=b_mx[:, 2 * h + q:2 * h + q + 1],
                                                 accum_out=b_sm[:, 2 * h + q:2 * h + q + 1])
                        ins.then_inc(s_exp, 1)
                    for h in range(2):
                        act.wait_ge(pt_ready, pr * 2 + h + 1)
                        act.activation(b_pt[:, h, :], xo[:, 1 - h, 0:3 * P], ACT.Copy).then_inc(pt_evac, 1)
                    act.wait_ge(ob_ready, pr + 1)
                    act.activation(b_o, x3[:], ACT.Copy).then_inc(ob_act, 1)
                    act.wait_ge(ob_act, pr + 1)
                    act.activation(hhi[:, bass.ds(pr * 2, 2), :], b_o.rearrange("p (b n) -> p b n", b=2), ACT.Copy) \
                        .then_inc(o_hi, 1)
            plain(T_WOB, 2)
            act.wait_ge(pg_free, G_FFN1)
            squares(E_NF1, xt, 8)
            std(E_NF1 + 8, D)
            norm_hi(O_NF1, 8, hhi)
            ffn(1)

        @block.vector
        def _(dve):
            def lo(t, s4, s2, n=2048):
                dve.wait_ge(hi_done, t + 1)
                dve.tensor_tensor(wlo[:, s2, 0:n], raw[:, s4, 0:n], whi[:, s2, 0:n].bitcast(F32), ALU.subtract) \
                    .then_inc(lo_done, 1)

            def ada(unit, j, n2=None, first=False):
                dve.wait_ge(ada_ld[j % 2], (unit * 2 + j // 2) * 32 + 32)
                for q in range(4):
                    k = 4 * j + q
                    if k == 0:
                        if not first:
                            dve.wait_ge(modp_ready, unit)
                        dve.tensor_scalar(acc[:], adar[:, 0, 0, :], scol[:, 0:1], None, ALU.mult).then_inc(ada_used, 1)
                    else:
                        dve.wait_ge(ada_used, unit * 16 + k)
                        dve.scalar_tensor_tensor(out=acc[:], in0=adar[:, j % 2, q, :], scalar=scol[:, k:k + 1],
                                                 in1=acc[:], op0=ALU.mult, op1=ALU.add).then_inc(ada_used, 1)

            def mod(unit):
                dve.wait_ge(modp_ready, unit + 1)
                dve.tensor_tensor(mods[:, bass.ds(unit * 4, 4)], x2[:, 508:512], cols[:, bass.ds(unit * 4, 4)],
                                  ALU.add).then_inc(mods_done, 1)

            def los(t0, per, i, first, count, unit=None):
                for n, k in enumerate(range(first, first + count)):
                    lo(i * per + (t0 + k), (t0 + k) % 4, (t0 + k) % 2)
                    if unit is not None:
                        ada(unit, n)

            dve.memset(ones[:], 1.0).then_inc(dcst_done, 1)
            dve.memset(one256[:], 1.0)
            dve.memset(cst[:, 0:1], EPS)
            dve.memset(cst[:, 1:2], 1.0)
            dve.memset(cst[:, 2:3], float(np.pi / 2)).then_inc(dcst_done, 1)
            dve.memset(nrow[:], 0.0).then_inc(dcst_done, 1)
            dve.wait_ge(tr_ready, 1)
            dve.tensor_copy(cols[:], x3[:, 0:C_END]).then_inc(tr_evac, 1)
            for g in range(4):
                dve.wait_ge(tr_ready, g + 2)
                dve.tensor_copy(xt[:, 4 * g:4 * g + 4, :], pg[:, g % 2]).then_inc(tr_evac, 1)

            def gain(n, unit0, gcol):
                dve.scalar_tensor_tensor(out=avec[:], in0=mods[:, 4 * unit0:4 * unit0 + NB], scalar=1.0,
                                         in1=cols[:, gcol:gcol + NB], op0=ALU.add, op1=ALU.mult).then_inc(a_done, 1)
                dve.wait_ge(a_done, n + 1)

            def recip(s):
                dve.wait_ge(std_done, s + 1)
                dve.reciprocal(rstd[:], rstd[:]).then_inc(rstd_done, 1)
                dve.wait_ge(rstd_done, s + 1)

            def norm_apply(o0, n, src, a, shift):
                for j in range(n):
                    o, m = o0 + j, FMA[o0] + j
                    if o >= 2:
                        dve.wait_ge(o_lo, o - 1)
                    v = ht[:, j % 2, :].rearrange("p (b n) -> p b n", b=2)
                    dve.tensor_tensor(v, src[:, 2 * j:2 * j + 2, :], rstd[:, None, :].broadcast_to([P, 2, T]),
                                      ALU.mult).then_inc(n_mul, 1)
                    dve.wait_ge(n_mul, m + 1)
                    for b in range(2):
                        k = 2 * j + b
                        if shift is None:
                            ins = dve.tensor_scalar(v[:, b, :], v[:, b, :], a[:, k:k + 1], None, ALU.mult)
                        else:
                            ins = dve.tensor_scalar(v[:, b, :], v[:, b, :], a[:, k:k + 1], shift[:, k:k + 1],
                                                    ALU.mult, ALU.add)
                    ins.then_inc(n_fma, 1)

            dve.wait_ge(s_silu, 1)
            for u in range(8):
                for j in range(4):
                    ada(u, j, first=(u == 0))
                mod(u)
            dve.wait_ge(mods_done, 8)
            gain(0, 4, C_NMIX)
            recip(S_N0)
            lo(0, 0, 0, NB * RANK)
            norm_apply(O_N0, 8, xt, avec, mods[:, 0:NB])
            lo(1, 1, 1)
            dve.wait_ge(mm_done, 1)
            dve.tensor_copy(a_lr, pt[:, 1, :, 0:RANK]).then_inc(pg_free, 1)
            dve.wait_ge(lr_tr, 1)
            dve.tensor_copy(alrt[:], x3[0:RANK, 0:T]).then_inc(lr_ready, 1)

            with dve.Fori(0, HEADS_A) as h:
                unit = h * 3 + 8
                los(T_GLA, 12, h, 1, 1)
                ada(unit, 0)
                dve.wait_ge(la_act, h * 4 + 4)
                dve.tensor_scalar(a_l, a_l, -1.0, 0.0, ALU.mult, ALU.max).then_inc(la_used, 1)
                dve.wait_ge(la_used, h + 1)
                dve.tensor_tensor(a_l, a_l, a_m, ALU.add).then_inc(la_dve, 1)
                dve.wait_ge(la_dve, h * 4 + 1)
                for b in range(2):
                    dve.tensor_tensor_scan(a_c[:, b, :], one256[:], a_l[:, b, :], 0.0, ALU.mult, ALU.add) \
                        .then_inc(la_dve, 1)
                dve.wait_ge(la_dve, h * 4 + 3)
                for s in range(2):
                    ins = dve.tensor_scalar(a_cs[:, s, :, 1:NCH], a_c[:, :, CH - 1:T - CH:CH],
                                            (-1.0 / TAU, 1.0 / TAU)[s], None, ALU.mult)
                ins.then_inc(la_dve, 1)
                for j in range(1, 4):
                    los(T_GLA, 12, h, 1 + j, 1)
                    ada(unit, j)
                dve.wait_ge(mm_done, h * 12 + (T_GLA + 4))
                dve.tensor_copy(a_qk, pg[:, 0]).then_inc(pg_free, 1)
                mod(unit)
                los(T_GLA, 12, h, 5, 1)
                ada(unit + 1, 0)
                dve.wait_ge(kexp, h + 1)
                dve.wait_ge(pg_free, h * 3 + 2)
                for n in range(NCH):
                    v = a_e[:, :, KOFF[n]:KOFF[n] + CH * (n + 1)]
                    dve.tensor_tensor(v, v, a_qk[:, 2:4, 0:CH * (n + 1)], ALU.mult)
                dve.scalar_tensor_tensor(out=a_qd, in0=a_qk[:, 0:2, :], scalar=float(DK) ** -0.5, in1=a_qd,
                                         op0=ALU.mult, op1=ALU.mult).then_inc(kq_ready, 1)
                for j in range(1, 4):
                    los(T_GLA, 12, h, 5 + j, 1)
                    ada(unit + 1, j)
                dve.wait_ge(mm_done, h * 12 + (T_GLA + 8))
                dve.tensor_copy(a_v, pt[:, 1]).then_inc(pg_free, 1)
                mod(unit + 1)
                los(T_GLA, 12, h, 9, 1)
                ada(unit + 2, 0)
                dve.wait_ge(att_ready, h + 1)
                dve.tensor_copy(a_att[0:CH, 0, 0:CH], x3[0:CH, 0:CH])
                dve.tensor_copy(a_att[:, 0, CH:T], x3[:, CH:T])
                dve.tensor_copy(a_att[0:CH, 1, P:P + CH], x3[0:CH, T + P:T + P + CH])
                dve.tensor_copy(a_att[:, 1, P + CH:T], x3[:, T + P + CH:2 * T]).then_inc(att_evac, 1)
                for j in range(1, 4):
                    los(T_GLA, 12, h, 9 + j, 1)
                    ada(unit + 2, j)
                dve.wait_ge(sg_act, h + 1)
                dve.tensor_tensor(a_sg, a_sg, pg[:, 0], ALU.mult).then_inc(pg_free, 1)
                mod(unit + 2)
                recip_h = h + (S_GLA + 1)
                dve.wait_ge(std_done, recip_h)
                dve.reciprocal(rstd[:], rstd[:]).then_inc(rstd_done, 1)
                dve.wait_ge(rstd_done, recip_h)
                dve.wait_ge(pg_free, h * 3 + (G_GLA + 3))
                for e in range(2):
                    dve.wait_ge(o_lo, h * 2 + (O_GLA + e - 1))
                    for b in range(2):
                        k = 2 * e + b
                        ins = dve.scalar_tensor_tensor(out=ht[:, e, b * T:(b + 1) * T], in0=xo[:, e, b * T:(b + 1) * T],
                                                       scalar=cols[:, C_ON + k:C_ON + k + 1], in1=rstd[:],
                                                       op0=ALU.mult, op1=ALU.mult)
                    ins.then_inc(oa_norm, 1)
                    dve.wait_ge(oa_norm, h * 2 + e + 1)
                    dve.tensor_tensor(ht[:, e, :], ht[:, e, :],
                                      a_sg[:, 2 * e:2 * e + 2, :].rearrange("p b n -> p (b n)"), ALU.mult) \
                        .then_inc(og_mul, 1)

            def residual(t, g, set_, blk, gate):
                dve.wait_ge(mm_done, t)
                for b in range(4):
                    ins = dve.scalar_tensor_tensor(out=xt[:, bass.ds(blk + b, 1), :].rearrange("p b n -> p (b n)"),
                                                   in0=pg[:, set_, b, :], scalar=mods[:, bass.ds(gate + b, 1)],
                                                   in1=xt[:, bass.ds(blk + b, 1), :].rearrange("p b n -> p (b n)"),
                                                   op0=ALU.mult, op1=ALU.add)
                ins.then_inc(pg_free, 1)

            def down(t0, g0, n, set0, gate_unit, att=(), u0=0, peel=False):
                dve.wait_ge(pg_free, g0)
                dve.wait_ge(mods_done, gate_unit + 4)
                for i in steps(dve, n, peel):
                    for u in range(2):
                        unit = i * len(att) + (u0 + att.index(u)) if u in att else None
                        last = peel and isinstance(i, int) and i == n - 1 and u == 1
                        los(t0 + 4 * u, 8, i, 1, 3 if last else 4, unit)
                        residual(i * 8 + (t0 + 4 * u + 4), None, (set0 + u) % 2, i * 8 + 4 * u,
                                 i * 8 + (4 * gate_unit + 4 * u))
                        if unit is not None:
                            mod(unit)

            def ffn(layer):
                base = MOD0 if layer == 0 else MOD1
                for kind, t0, g0, o0, n, u0, att, ch, b0 in ffn_plan(layer):
                    set0 = g0 % 2
                    if kind == "down":
                        down(t0, g0, n, set0, base + 20, att, u0, peel=(layer == 1 and ch == 2))
                        continue
                    for i in steps(dve, n):
                        for u in range(2):
                            unit = i * len(att) + (u0 + att.index(u)) if u in att else None
                            los(t0 + 4 * u, 8, i, 1, 4, unit)
                            dve.wait_ge(f_silu, i * 2 + (o0 + u + 1 - (O_FFN0, O_FFN1 - FF // T)[layer]))
                            dve.wait_ge(o_lo, i * 2 + (o0 + u - 1))
                            dve.tensor_tensor(f_a[:, u, :].rearrange("p (b n) -> p b n", b=2),
                                              f_s[:, u, :].rearrange("p (b n) -> p b n", b=2),
                                              pg[:, (set0 + u) % 2, 2:4], ALU.mult).then_inc(pg_free, 1)
                            if unit is not None:
                                mod(unit)

            down(T_WOA, G_WOA, 2, 1, MOD0 + 8)
            dve.wait_ge(mods_done, 20)
            gain(1, 16, C_NFFN)
            recip(S_NF0)
            norm_apply(O_NF0, 8, xt, avec, mods[:, 12 * 4:12 * 4 + NB])
            ffn(0)
            dve.wait_ge(mods_done, U_MLA)
            gain(2, MODKV + 4, C_KVN)
            recip(S_NKV)
            norm_apply(O_NKV, 8, xt, avec, mods[:, 4 * MODKV:4 * MODKV + NB])
            los(T_DKV, 4, 0, 1, 1)
            dve.wait_ge(pos_ld, 32)
            dve.wait_ge(cst_done, 6)
            dve.tensor_copy(posf, posi[:]).then_inc(rot_c, 1)
            dve.wait_ge(rot_c, 1)
            for t in range(2):
                ins = dve.tensor_scalar(ang[:, t, :], invf[:, 0:HALF], posf[:, t:t + 1], None, ALU.mult)
            ins.then_inc(rot_c, 1)
            dve.wait_ge(rot_c, 2)
            dve.tensor_scalar(angk, ang, float(1.0 / TWO_PI), MAGIC, ALU.mult, ALU.add).then_inc(rot_c, 1)
            dve.wait_ge(rot_c, 3)
            dve.tensor_scalar(angk, angk, MAGIC, None, ALU.subtract).then_inc(rot_c, 1)
            for k, part in enumerate((PI_A, PI_B, PI_C)):
                dve.wait_ge(rot_c, 4 + k)
                dve.scalar_tensor_tensor(out=ang, in0=angk, scalar=-part, in1=ang, op0=ALU.mult, op1=ALU.add) \
                    .then_inc(rot_c, 1)
            dve.wait_ge(rot_c, 7)
            dve.tensor_scalar(ang, ang, 3.1415925, -3.1415925, ALU.min, ALU.max).then_inc(rot_c, 1)
            los(T_DKV, 4, 0, 2, 3)
            dve.wait_ge(mm_done, T_DKV + 4)
            dve.tensor_copy(latk, pg[:, 1]).then_inc(pg_free, 1)
            los(T_KPE, 4, 0, 1, 1)
            dve.wait_ge(mm_done, T_KPE + 1)
            dve.tensor_copy(kpe[:], pt[:, 0, :, 0:ROPE]).then_inc(pg_free, 1)
            gain(3, MOD1 + 4, C_NMIX + NB)
            norm_apply(O_NMX, 8, xt, avec, mods[:, 4 * MOD1:4 * MOD1 + NB])
            recip(S_LKV)
            norm_apply(O_LKV, 2, latk, cols[:, C_KL:C_KL + LB], None)
            dve.wait_ge(kp_rot, 2)
            dve.tensor_tensor(krw, kpe[:], kpe[:], ALU.mult).then_inc(kp_ss, 1)
            dve.wait_ge(kp_ss, 1)
            dve.tensor_reduce(kss, krw, AX.X, ALU.add).then_inc(kp_ss, 1)
            los(T_DQ, 4, 0, 1, 4)
            dve.wait_ge(mm_done, T_DQ + 4)
            dve.tensor_copy(latq, pg[:, 1]).then_inc(pg_free, 1)
            recip(S_LQ)
            norm_apply(O_LQ, 2, latq, cols[:, C_QL:C_QL + LB], None)
            dve.wait_ge(kp_ss, 2)

            with dve.Fori(0, HEADS_B // 4) as i:
                for u in range(2):
                    pr = i * 2 + u
                    t0 = T_MLA + 2 * u
                    unit = i * 2 + (40 + u)
                    los(t0, 4, i, 1, 1)
                    ada(unit, 0)
                    ada(unit, 1)
                    dve.wait_ge(mm_done, i * 4 + (t0 + 1))
                    dve.wait_ge(o_hi, pr + O_MLA)
                    dve.tensor_copy(b_q, pt[:, 0, :, 0:2 * QKD]).then_inc(pg_free, 1)
                    los(t0, 4, i, 2, 1)
                    ada(unit, 2)
                    ada(unit, 3)
                    dve.wait_ge(mm_done, i * 4 + (t0 + 2))
                    dve.tensor_copy(b_kv, pt[:, 1]).then_inc(pg_free, 1)
                    mod(unit)
                    dve.wait_ge(bsq, pr * 2 + 1)
                    dve.tensor_reduce(b_st[:, 0:4], b_sq.rearrange("p (a n) -> p a n", a=4), AX.X, ALU.add) \
                        .then_inc(bst, 1)
                    dve.wait_ge(bsq, pr * 2 + 2)
                    dve.tensor_reduce(b_st[:, 4:8], b_sq[:, 0:512].rearrange("p (a n) -> p a n", a=4), AX.X, ALU.add) \
                        .then_inc(bst, 1)
                    dve.wait_ge(bst, pr * 3 + 2)
                    k_st = b_st[:, 4:8].rearrange("p (t h) -> p t h", t=2)
                    dve.tensor_tensor(k_st, k_st, kss[:, :, None].broadcast_to([P, 2, 2]), ALU.add).then_inc(bst, 1)
                    dve.wait_ge(bstd, pr + 1)
                    dve.reciprocal(b_st, b_st).then_inc(brs, 1)
                    dve.wait_ge(brs, pr + 1)
                    q4 = b_q.rearrange("p t (h n) -> p t h n", h=2)
                    k4 = b_kv.rearrange("p t (h n) -> p t h n", h=2)[:, :, :, 0:NOPE]
                    r4 = b_st.rearrange("p (a t h) -> p a t h", a=2, t=2)
                    dve.tensor_tensor(b_qp, q4[:, :, :, NOPE:QKD], r4[:, 0, :, :, None].broadcast_to([P, 2, 2, ROPE]),
                                      ALU.mult)
                    q4 = q4[:, :, :, 0:NOPE]
                    dve.tensor_tensor(q4, q4, r4[:, 0, :, :, None].broadcast_to([P, 2, 2, NOPE]), ALU.mult) \
                        .then_inc(bqk, 1)
                    dve.tensor_tensor(k4, k4, r4[:, 1, :, :, None].broadcast_to([P, 2, 2, NOPE]), ALU.mult)
                    dve.tensor_tensor(b_kp, kpe[:, :, None, :].broadcast_to([P, 2, 2, ROPE]),
                                      r4[:, 1, :, :, None].broadcast_to([P, 2, 2, ROPE]), ALU.mult).then_inc(bqk, 1)
                    dve.wait_ge(tk_ready, pr + 1)
                    dve.tensor_scalar(b_rt[:, 0, :], xo[:, 1, 0:T], cols[:, C_QT:C_QT + 1], None, ALU.mult)
                    dve.tensor_scalar(b_rt[:, 1, :], xo[:, 1, T:2 * T], cols[:, C_KT:C_KT + 1], None, ALU.mult) \
                        .then_inc(te_dve, 1)
                    for h in range(2):
                        s = (xo[:, 0, 0:3 * P], x3[:, 0:3 * P])[h]
                        d0 = (pr * 2 + h) * 3
                        dve.wait_ge(s_ready, pr * 2 + h + 1)
                        dve.scalar_tensor_tensor(out=b_p[:, h, :], in0=s, scalar=float(QKD) ** -0.5,
                                                 in1=mask[:].rearrange("p b n -> p (b n)"), op0=ALU.mult,
                                                 op1=ALU.add).then_inc(s_dve, 1)
                        dve.wait_ge(s_dve, d0 + 1)
                        dve.tensor_reduce(b_mx[:, 2 * h:2 * h + 1], b_p[:, h, 0:P], AX.X, ALU.max)
                        dve.tensor_reduce(b_mx[:, 2 * h + 1:2 * h + 2], b_p[:, h, P:3 * P], AX.X, ALU.max) \
                            .then_inc(s_dve, 1)
                        dve.wait_ge(s_dve, d0 + 2)
                        dve.tensor_scalar(b_mx[:, 2 * h:2 * h + 2], b_mx[:, 2 * h:2 * h + 2], -1.0, None, ALU.mult) \
                            .then_inc(s_mx, 1)
                        dve.wait_ge(s_exp, pr * 2 + h + 1)
                        dve.reciprocal(b_sm[:, 2 * h:2 * h + 2], b_sm[:, 2 * h:2 * h + 2]).then_inc(s_dve, 1)
                        dve.wait_ge(s_dve, d0 + 3)
                        dve.tensor_scalar(b_p[:, h, 0:P], b_p[:, h, 0:P], b_sm[:, 2 * h:2 * h + 1], None, ALU.mult)
                        dve.tensor_scalar(b_p[:, h, P:3 * P], b_p[:, h, P:3 * P], b_sm[:, 2 * h + 1:2 * h + 2], None,
                                          ALU.mult).then_inc(p_ready, 1)
            down(T_WOB, G_WOB, 2, 0, MOD1 + 8, (0, 1), 48)
            dve.wait_ge(mods_done, 52)
            gain(4, MOD1 + 16, C_NFFN + NB)
            recip(S_NF1)
            norm_apply(O_NF1, 8, xt, avec, mods[:, 4 * (MOD1 + 12):4 * (MOD1 + 12) + NB])
            ffn(1)
            for g in range(8):
                dve.wait_ge(y_tr, g + 1)
                dve.tensor_copy(xio[:, g // 4, (g % 4) * 512:(g % 4 + 1) * 512], y_bank(g)).then_inc(y_ev, 1)

        @block.tensor
        def _(pe):
            def split3(dst, w, x_, start, stop):
                (w_h, w_l), (x_h, x_l) = w, x_
                pe.matmul(dst, w_h, x_h, start=start, stop=False, skip_group_check=True)
                pe.matmul(dst, w_h, x_l, start=False, stop=False, skip_group_check=True)
                return pe.matmul(dst, w_l, x_h, start=False, stop=stop, skip_group_check=True)

            def feature_tile(t, s2, set_, kts, k0, right, j, last_j, dst_cols=4):
                pe.wait_ge(lo_done, t + 1)
                r_hi, r_lo = right
                for k in range(kts):
                    for b in range(4):
                        c0 = k * GW + b * P
                        ins = split3(pg[:, set_, b, :], (whi[:, s2, c0:c0 + P], wlo[:, s2, c0:c0 + P]),
                                     (r_hi[:, k0 + k, :], r_lo[:, k0 + k, :]),
                                     start=(j == 0 and k == 0 and b % 2 == 0), stop=(j == last_j and k == kts - 1))
                ins.then_inc(mm_done, 1)

            def token_tile(t, s2, set_, kts, n, k0, left, first, last):
                pe.wait_ge(lo_done, t + 1)
                l_hi, l_lo = left
                for k in range(kts):
                    for tt in range(2):
                        w_h, w_l = whi[:, s2, k * n:(k + 1) * n], wlo[:, s2, k * n:(k + 1) * n]
                        a_h = l_hi[:, k0 + k, tt * P:(tt + 1) * P]
                        a_lw = l_lo[:, k0 + k, tt * P:(tt + 1) * P]
                        ins = split3(pt[:, set_, tt, 0:n], (a_h, a_lw), (w_h, w_l),
                                     start=(first and k == 0), stop=(last and k == kts - 1))
                ins.then_inc(mm_done, 1)

            def reduce_unit(unit, std):
                pe.wait_ge(ada_used, unit * 16 + 16)
                if not isinstance(unit, int) or unit:
                    pe.wait_ge(mods_done, unit)
                if std is not None:
                    pe.wait_ge(std_done, std)
                for b in range(4):
                    ins = pe.matmul(x2[:, 508 + b:509 + b], acc[:, b * P:(b + 1) * P], ones[:, 0:1], start=True, stop=True)
                ins.then_inc(modp_ready, 1)

            def sumsq(e0, n, units, s):
                if units:
                    pe.wait_ge(mods_done, units)
                    pe.wait_ge(std_done, s)
                for j in range(n):
                    pe.wait_ge(sq_done, e0 + j + 1)
                    for b in range(2):
                        ins = pe.matmul(x2[:, 0:T], ones[:], sq[:, j % 2, b * T:(b + 1) * T],
                                        start=(j == 0 and b == 0), stop=(j == n - 1 and b == 1))
                    ins.then_inc(ssq_mm, 1)

            pe.wait_ge(cst_done, 6)
            pe.wait_ge(par_ld, par_dmas * 16)
            for k in range(3):
                n = min(P, C_END - k * P)
                ins = pe.matmul(x3[:, k * P:k * P + n], vrow[0:n, k, :], ident[0:n, 0:n], start=True, stop=True)
            ins.then_inc(tr_ready, 1)
            pe.wait_ge(x_ld, 16)
            for g in range(4):
                if g >= 2:
                    pe.wait_ge(tr_evac, g)
                for b in range(4):
                    for tt in range(2):
                        ins = pe.matmul(pg[:, g % 2, b, tt * P:(tt + 1) * P],
                                        xio[:, tt, (4 * g + b) * P:(4 * g + b + 1) * P], ident[:], start=True, stop=True)
                ins.then_inc(tr_ready, 1)
            pe.wait_ge(dcst_done, 1)
            sumsq(E_N0, 8, 0, 0)
            for u in range(8):
                reduce_unit(u, 1)

            h2 = (hhi, hlo)
            a2 = (ahi, alo)
            pe.wait_ge(tr_evac, 5)
            pe.wait_ge(o_lo, O_N0 + 8)
            token_tile(0, 0, 1, NB, RANK, 0, h2, True, True)
            pe.wait_ge(pg_free, G_LOW + 1)
            for tt in range(2):
                ins = pe.matmul(x3[0:RANK, tt * P:(tt + 1) * P], a_lr[:, tt, :], ident[:], start=True, stop=True)
            ins.then_inc(lr_tr, 1)
            pe.wait_ge(lr_ready, 1)

            with pe.Fori(0, HEADS_A) as h:
                pe.wait_ge(wah_ld, h * 16 + 16)
                pe.wait_ge(std_done, h + S_GLA)
                pe.wait_ge(mods_done, h * 3 + 8)
                for b in range(2):
                    ins = pe.matmul(x2[:, b * T:(b + 1) * T], wah[:, b * P:(b + 1) * P], alrt[:], start=True, stop=True)
                ins.then_inc(la_ready, 1)
                pe.wait_ge(pg_free, h * 3 + G_GLA)
                for j in range(4):
                    feature_tile(h * 12 + (T_GLA + j), (T_GLA + j) % 2, 0, 4, 4 * j, h2, j, 3)
                pe.wait_ge(la_act, h * 4 + 4)
                reduce_unit(h * 3 + 8, None)
                pe.wait_ge(pg_free, h * 3 + G_GLA)
                for j in range(4):
                    token_tile(h * 12 + (T_GLA + 4 + j), (T_GLA + j) % 2, 1, 4, GW, 4 * j, h2, j == 0, j == 3)
                reduce_unit(h * 3 + 9, None)
                pe.wait_ge(kq_ready, h + 1)
                for n in range(NCH):
                    for kt in range((n + 2) // 2):
                        m = min(P, CH * (n + 1) - kt * P)
                        for b in range(2):
                            c0 = KOFF[n] + kt * P
                            ins = pe.matmul(x3[0:m, kt * T + CH * n:kt * T + CH * (n + 1)], a_e[:, b, c0:c0 + m],
                                            a_qd[:, b, CH * n:CH * (n + 1)], start=(b == 0), stop=(b == 1))
                ins.then_inc(att_ready, 1)
                pe.wait_ge(pg_free, h * 3 + (G_GLA + 1))
                for j in range(4):
                    feature_tile(h * 12 + (T_GLA + 8 + j), (T_GLA + j) % 2, 0, 4, 4 * j, h2, j, 3)
                reduce_unit(h * 3 + 10, None)
                pe.wait_ge(att_msk, h + 1)
                pe.wait_ge(o_hi, h * 2 + O_GLA)
                for b in range(4):
                    v = [a_v[:, kt, b * P:(b + 1) * P] for kt in range(2)]
                    o = xo[:, b // 2, (b % 2) * T:(b % 2 + 1) * T]
                    pe.matmul(o, v[0], a_att[:, 0, :], start=True, stop=False, skip_group_check=True)
                    ins = pe.matmul(o[:, P:T], v[1], a_att[:, 1, P:T], start=False, stop=True, skip_group_check=True)
                ins.then_inc(oa_ready, 1)
                pe.wait_ge(mods_done, h * 3 + 11)
                for e in range(2):
                    pe.wait_ge(sq_done, h * 2 + (E_GLA + e + 1))
                    for b in range(2):
                        ins = pe.matmul(x2[:, 0:T], ones[:], sq[:, e, b * T:(b + 1) * T],
                                        start=(e == 0 and b == 0), stop=(e == 1 and b == 1))
                    ins.then_inc(ssq_mm, 1)

            def product(t0, g0, n, set0, right, kts=4, o_wait=None, att=(), u0=0, std=None):
                for i in steps(pe, n):
                    for u in range(2):
                        pe.wait_ge(pg_free, i * 2 + (g0 + u - 1))
                        for j in range(4):
                            if u == 0 and o_wait is not None:
                                pe.wait_ge(o_lo, o_wait + ((j + 1) * kts + 1) // 2)
                            feature_tile(i * 8 + (t0 + 4 * u + j), (t0 + j) % 2, (set0 + u) % 2, kts, kts * j, right,
                                         j, 3)
                        if u in att:
                            reduce_unit(i * len(att) + (u0 + att.index(u)), std)

            def ffn(layer):
                o_n = O_NF0 if layer == 0 else O_NF1
                for kind, t0, g0, o0, n, u0, att, ch, b0 in ffn_plan(layer):
                    set0 = g0 % 2
                    std = (S_NF0 if layer == 0 else S_NF1) + 1
                    if kind == "up":
                        product(t0, g0, n, set0, h2, 4, o_n, att, u0, std)
                    else:
                        product(t0, g0, n, set0, a2, FFC[ch] // 2, o0, att, u0, std)

            product(T_WOA, G_WOA, 2, 1, a2, 4, O_GLA)
            sumsq(E_NF0, 8, U_FFN0, S_NF0)
            ffn(0)
            sumsq(E_NKV, 8, U_MLA, S_NKV)
            pe.wait_ge(pg_free, G_DKV)
            for j in range(4):
                pe.wait_ge(o_lo, O_NKV + 2 * (j + 1))
                feature_tile(T_DKV + j, (T_DKV + j) % 2, 1, 4, 4 * j, h2, j, 3)
            token_tile(T_KPE, T_KPE % 2, 0, NB, ROPE, 0, h2, True, True)
            sumsq(E_LKV, 2, U_MLA, S_LKV)
            for j in range(4):
                pe.wait_ge(o_lo, O_NMX + 2 * (j + 1))
                feature_tile(T_DQ + j, (T_DQ + j) % 2, 1, 4, 4 * j, h2, j, 3)
            sumsq(E_LQ, 2, U_MLA, S_LQ)
            pe.wait_ge(o_lo, O_LQ + 2)

            with pe.Fori(0, HEADS_B // 4) as i:
                for u in range(2):
                    pr = i * 2 + u
                    t0 = T_MLA + 2 * u
                    pe.wait_ge(pg_free, i * 4 + (G_MLA + 2 * u - 1))
                    token_tile(i * 4 + t0, t0 % 2, 0, LB, 2 * QKD, LB, a2, True, True)
                    pe.wait_ge(pg_free, i * 4 + (G_MLA + 2 * u))
                    token_tile(i * 4 + (t0 + 1), (t0 + 1) % 2, 1, LB, 2 * (NOPE + VD), 0, a2, True, True)
                    reduce_unit(i * 2 + (40 + u), S_LQ + 1)
                    pe.wait_ge(bqk, pr * 2 + 1)
                    for hh in range(2):
                        for tt in range(2):
                            pe.matmul(xo[:, 0, hh * T + tt * P:hh * T + (tt + 1) * P],
                                      b_q[:, tt, hh * QKD:hh * QKD + NOPE], ident[:], start=True, stop=True)
                    for tt in range(2):
                        ins = pe.matmul(xo[:, 1, tt * P:(tt + 1) * P], b_qp[:, tt].rearrange("p h n -> p (h n)"), ident[:],
                                        start=True, stop=True)
                    ins.then_inc(tq_ready, 1)
                    pe.wait_ge(bqk, pr * 2 + 2)
                    pe.wait_ge(o_hi, pr + O_MLA)
                    for hh in range(2):
                        for tt in range(2):
                            pe.matmul(x3[:, hh * T + tt * P:hh * T + (tt + 1) * P],
                                      b_kv[:, tt, hh * 256:hh * 256 + NOPE], ident[:], start=True, stop=True)
                    for tt in range(2):
                        ins = pe.matmul(xo[:, 1, T + tt * P:T + (tt + 1) * P], b_kp[:, tt].rearrange("p h n -> p (h n)"), ident[:],
                                        start=True, stop=True)
                    ins.then_inc(tk_ready, 1)
                    pe.wait_ge(te_act, pr + 1)
                    pe.wait_ge(te_dve, pr + 1)
                    for hh in range(2):
                        dst = (xo[:, 0, :], x3[:, :])[hh]
                        r0 = hh * ROPE
                        for qt, (c0, n) in enumerate(((0, P), (P, T))):
                            pe.matmul(dst[:, c0:c0 + n], b_qt[:, hh, qt * P:(qt + 1) * P], b_kt[:, hh, 0:n],
                                      start=True, stop=False)
                            ins = pe.matmul(dst[:, c0:c0 + n], b_rt[r0:r0 + ROPE, 0, qt * P:(qt + 1) * P],
                                            b_rt[r0:r0 + ROPE, 1, 0:n], start=False, stop=True)
                        ins.then_inc(s_ready, 1)
                    for hh in range(2):
                        pe.wait_ge(p_ready, pr * 2 + hh + 1)
                        for b in range(3):
                            ins = pe.matmul(xo[:, 1 - hh, b * P:(b + 1) * P], b_p[:, hh, b * P:(b + 1) * P], ident[:],
                                            start=True, stop=True)
                        ins.then_inc(pt_ready, 1)
                    for hh in range(2):
                        pe.wait_ge(pt_evac, pr * 2 + hh + 1)
                        v = [b_kv[:, kt, hh * 256 + NOPE:hh * 256 + NOPE + VD] for kt in range(2)]
                        pe.matmul(x3[:, hh * T:(hh + 1) * T], v[0], b_pt[:, hh, 0:T], start=True, stop=False,
                                  skip_group_check=True)
                        ins = pe.matmul(x3[:, hh * T + P:(hh + 1) * T], v[1], b_pt[:, hh, T:3 * P], start=False,
                                        stop=True, skip_group_check=True)
                    ins.then_inc(ob_ready, 1)
            product(T_WOB, G_WOB, 2, 0, h2, 4, O_MLA, (0, 1), 48, S_LQ + 1)
            sumsq(E_NF1, 8, U_FFN1, S_NF1)
            ffn(1)
            pe.wait_ge(pg_free, G_END)
            for g in range(8):
                if g >= 4:
                    pe.wait_ge(y_ev, g - 3)
                for b in range(4):
                    ins = pe.matmul(y_bank(g)[:, b * P:(b + 1) * P],
                                    xt[:, 4 * (g % 4) + b, (g // 4) * P:(g // 4 + 1) * P], ident[:], start=True, stop=True)
                ins.then_inc(y_tr, 1)


_INS = ["x", "c", "positions", "ada_w", "ada_b", "norm_mix", "norm_ffn", "gla_w_in", "gla_w_alpha", "gla_b_alpha",
        "gla_onorm", "gla_w_out", "mla_w_dq", "mla_q_lat_norm", "mla_w_uq", "mla_q_norm", "mla_w_out", "kv_ada_w",
        "kv_ada_b", "kv_norm", "kv_w_dkv", "kv_lat_norm", "kv_w_ukv", "kv_k_norm", "ffn_w_gu", "ffn_w_down"]


def kernel(**inputs):
    import concourse.bacc as bacc
    from concourse.bass_utils import run_bass_kernel_spmd

    nc = bacc.Bacc("TRN2", target_bir_lowering=False, num_devices=1)
    arrays, args = {}, []
    for name in _INS:
        a = np.ascontiguousarray(inputs[name])
        arrays["in_" + name] = a
        args.append(nc.dram_tensor("in_" + name, a.shape, mybir.dt.from_np(a.dtype), kind="ExternalInput").ap())
    args.append(nc.dram_tensor("out_0", (1, T, D), F32, kind="ExternalOutput").ap())
    trunk(nc, *args)
    r = run_bass_kernel_spmd(nc, [arrays], core_ids=[0])
    return r.results[0]["out_0"]
```

```python
from contextlib import ExitStack

import numpy as np

import concourse.bass as bass
from concourse import mybir

F32 = mybir.dt.float32
F32R = mybir.dt.float32r
I32 = mybir.dt.int32
ALU = mybir.AluOpType
ACT = mybir.ActivationFunctionType
AX = mybir.AxisListType

P = 128
D = 2048
T = 256
NB = D // P
KQ = NB // 4
HEADS_A = 4
DK, DV = D // 2 // HEADS_A, D // HEADS_A
QK_A = HEADS_A * DK
RANK = 16
TAU = 16.0
CH = 64
NCH = T // CH
HEADS_B = 16
NOPE, ROPE, VD = 128, 64, 128
QKD = NOPE + ROPE
HALF = ROPE // 2
PAIRS = HEADS_B // 2
LORA = 512
LB = LORA // P
FF = 5632
FFC = (8, 8, 6)
EPS = 1e-6
THETA = 10000.0
GW = 512
NEG = -1e30
TWO_PI = 2.0 * np.pi
PI_A = 6.28125
PI_B = 0.00193500518798828125
PI_C = float(TWO_PI - PI_A - PI_B)
MAGIC = 12582912.0

MOD0, MODKV, MOD1 = 0, 24, 32
C_C, C_NMIX, C_NFFN, C_KVN, C_ON, C_BA, C_QL, C_KL, C_QN, C_KN, C_QT, C_KT, C_END = \
    224, 240, 272, 304, 320, 324, 332, 336, 340, 341, 342, 343, 344

T_LOW, T_GLA, T_WOA, T_FFN0 = 0, 1, 49, 65
T_DKV, T_KPE, T_DQ, T_MLA, T_WOB, T_FFN1, T_END = 201, 205, 206, 210, 226, 242, 378
G_LOW, G_GLA, G_WOA, G_FFN0, G_DKV, G_KPE, G_DQ, G_MLA, G_WOB, G_FFN1, G_END = 0, 1, 13, 17, 51, 52, 53, 54, 70, 74, 108
O_N0, O_GLA, O_NF0, O_FFN0, O_NKV, O_NMX, O_LKV, O_LQ, O_MLA, O_NF1, O_FFN1 = 0, 8, 16, 24, 46, 54, 62, 64, 66, 74, 82
E_N0, E_GLA, E_NF0, E_NKV, E_LKV, E_LQ, E_NF1 = 0, 8, 16, 24, 32, 34, 36
S_N0, S_GLA, S_NF0, S_NKV, S_LKV, S_LQ, S_NF1 = 0, 1, 5, 6, 7, 8, 9
FMA = {O_N0: 0, O_NF0: 8, O_NKV: 16, O_NMX: 24, O_LKV: 32, O_LQ: 34, O_NF1: 36}
U_GLA, U_WOA, U_FFN0, U_DKV, U_PAIR, U_WOB, U_FFN1, U_END = 8, 16, 20, 40, 41, 48, 52, 56


def whole(tiles):
    return tiles * 2


def tile_shape(t0, k, per):
    t = t0 + k
    if t == T_KPE:
        return NB, ROPE
    if T_MLA <= t < T_WOB and t % 2 == T_MLA % 2:
        return LB, 2 * QKD
    return 4, GW


def halves(k):
    return (0, (k + 1) // 2), ((k + 1) // 2, k)


def steps(eng, n, peel=False):
    m = n - 1 if peel else n
    if m > 1:
        with eng.Fori(0, m) as i:
            yield i
    else:
        yield from range(m)
    if peel:
        yield n - 1


def pairs(eng):
    with eng.Fori(0, PAIRS // 2 - 1) as i:
        for u in range(2):
            yield i * 2 + u, i, u
    for u in range(2):
        yield PAIRS - 2 + u, PAIRS // 2 - 1, u


def a_of(rate, u, j):
    if rate == 2:
        return u, j
    if rate == 1 and j % 2 == 0:
        return 0, 2 * u + j // 2
    return None


def a_of_head(pos):
    return None if pos % 3 == 2 else (pos // 6, pos % 6 - pos % 6 // 3)


def ffn_plan(layer):
    t, g, o, u = (T_FFN0, G_FFN0, O_FFN0, U_FFN0) if layer == 0 else (T_FFN1, G_FFN1, O_FFN1, U_FFN1)
    rates = ((1, 1, 1, 1, 2, 1), (1, 0, 0, 0, 0, 0))[layer]
    out, b = [], 0
    for c, n in enumerate(FFC):
        a = rates[2 * c]
        out.append(("up", t, g, o, n // 2, u, a, c, b))
        t, g, o, u = t + 4 * n, g + n, o + n, u + a * (n // 2)
        a = rates[2 * c + 1]
        out.append(("down", t, g, o - n, 2, u, a, c, b))
        t, g, u = t + 16, g + 4, u + a * 2
        b += 2 * n
    return out


def trunk(nc, x, c, positions, ada_w, ada_b, norm_mix, norm_ffn, gla_w_in, gla_w_alpha, gla_b_alpha, gla_onorm,
          gla_w_out, mla_w_dq, mla_q_lat_norm, mla_w_uq, mla_q_norm, mla_w_out, kv_ada_w, kv_ada_b, kv_norm,
          kv_w_dkv, kv_lat_norm, kv_w_ukv, kv_k_norm, ffn_w_gu, ffn_w_down, out):
    with ExitStack() as ctx:
        def sb(name, shape, dt=F32):
            return ctx.enter_context(nc.sbuf_tensor(name, shape, dt))

        def ps(name, shape):
            return ctx.enter_context(nc.psum_tensor(name, shape, F32))

        def sem(name):
            return ctx.enter_context(nc.semaphore(name))

        raw = sb("raw", [P, 4, 2048])
        whi = sb("whi", [P, 2, 2048], F32R)
        wlo = sb("wlo", [P, 2, 2048], F32R)
        adar = sb("adar", [P, 2, 4, GW])
        acc = sb("acc", [P, 2, GW])
        xt = sb("xt", [P, NB, T])
        hhi = sb("hhi", [P, NB, T], F32R)
        hlo = sb("hlo", [P, NB, T], F32R)
        ahi = sb("ahi", [P, NB, T], F32R)
        alo = sb("alo", [P, NB, T], F32R)
        work = sb("work", [P, 6912])
        cols = sb("cols", [P, C_END])
        mods = sb("mods", [P, 224])
        avec = sb("avec", [P, NB])
        scol = sb("scol", [P, NB])
        ones = sb("ones", [P, P])
        ident = sb("ident", [P, P])
        rstd = sb("rstd", [P, T])
        sq = sb("sq", [P, 2, 2 * T])
        ht = sb("ht", [P, 2, 2 * T])
        mask = sb("mask", [P, 3, P])
        csin = sb("csin", [P, 2, 2, HALF])
        kpe = sb("kpe", [P, 2, ROPE])
        nrow = sb("nrow", [P, 64])
        posi = sb("posi", [P, 2], I32)
        cst = sb("cst", [P, 4])
        invf = sb("invf", [P, HALF])
        EPSC, ONEC, HPIC = cst[:, 0:1], cst[:, 1:2], cst[:, 2:3]
        COS, SIN = csin[:, 0], csin[:, 1]

        def wview(lo, hi, **dims):
            pat = {1: "p (a n) -> p a n", 2: "p (a b n) -> p a b n"}[len(dims)]
            return work[:, lo:hi].rearrange(pat, **dims)

        xio = wview(0, 4096, a=2)
        vrow = wview(4096, 4480, a=3)
        a_qk = wview(0, 1024, a=4)
        a_v = wview(1024, 2048, a=2)
        a_sg = wview(2048, 3072, a=4)
        a_c = wview(3072, 3584, a=2)
        a_e = wview(3584, 4864, a=2)
        a_qd = wview(4864, 5376, a=2)
        a_att = wview(5376, 5888, a=2)
        a_l = a_e[:, :, 0:T]
        a_m = a_e[:, :, T:2 * T]
        a_lr = wview(5888, 5920, a=2)
        alrt = work[0:RANK, 5920:6176]
        wah = work[0:RANK, 6176:6432]
        a_cs = nrow[:, 0:16].rearrange("p (s b n) -> p s b n", s=2, b=2)
        KOFF = [0, 64, 192, 384]
        f_s = wview(0, 1024, a=2)
        f_a = wview(1024, 2048, a=2)
        b_q = [v.rearrange("p (a n) -> p a n", a=2)
               for v in (work[:, 0:768], work[:, 6144:6912])]
        b_kv = [v.rearrange("p (a n) -> p a n", a=2)
                for v in (work[:, 768:1792], sq[:].rearrange("p a n -> p (a n)"))]
        b_qt = wview(1792, 2304, a=2)
        b_kt = wview(2304, 2816, a=2)
        b_rt = wview(2816, 3328, a=2)
        b_kp = wview(3328, 3584, a=2, b=2)
        b_qp = wview(5888, 6144, a=2, b=2)
        b_p = wview(3584, 4352, a=2)
        b_pt = wview(4352, 5120, a=2)
        b_sq = work[:, 5120:5888]
        b_o = ht[:, 1, :]
        latk = wview(0, 1024, a=4)
        latq = wview(1024, 2048, a=4)
        ang = wview(2048, 2112, a=2)
        angk = wview(2112, 2176, a=2)
        anga = wview(2176, 2240, a=2)
        posf = work[:, 2272:2274]
        krw = wview(2304, 2432, a=2)
        krt = wview(2432, 2688, a=4, b=2)
        b_st = nrow[:, 16:24]
        b_mx, b_sm = nrow[:, 24:28], nrow[:, 28:32]
        kss = nrow[:, 32:34]

        pg = ps("pg", [P, 2, 4, T])
        pt = pg[:, :, :, :].rearrange("p s (t b) n -> p s t (b n)", t=2)
        xo = ps("xo", [P, 2, 512])
        x2 = ps("x2", [P, 512])
        x3 = ps("x3", [P, 512])

        raw_ld = [sem(f"raw_ld{i}") for i in range(4)]
        ada_ld = [sem(f"ada_ld{i}") for i in range(4)]
        par_ld, x_ld, pos_ld, wah_ld, out_st = sem("par_ld"), sem("x_ld"), sem("pos_ld"), sem("wah_ld"), sem("out_st")
        hi_done, lo_done, mm_done, pg_free = sem("hi_done"), sem("lo_done"), sem("mm_done"), sem("pg_free")
        ada_used, modp_ready, mods_done = sem("ada_used"), sem("modp_ready"), sem("mods_done")
        cst_done, dcst_done = sem("cst_done"), sem("dcst_done")
        tr_ready, tr_evac, s_silu = sem("tr_ready"), sem("tr_evac"), sem("s_silu")
        sq_done, ssq_mm, std_done, rstd_done = sem("sq_done"), sem("ssq_mm"), sem("std_done"), sem("rstd_done")
        a_done, n_mul, n_fma, o_hi, o_lo = sem("a_done"), sem("n_mul"), sem("n_fma"), sem("o_hi"), sem("o_lo")
        lr_tr, lr_ready, oa_norm = sem("lr_tr"), sem("lr_ready"), sem("oa_norm")
        la_ready, la_act, la_used, la_dve, kexp, kq_ready = (sem("la_ready"), sem("la_act"), sem("la_used"),
                                                             sem("la_dve"), sem("kexp"), sem("kq_ready"))
        att_ready, att_evac, att_msk, sg_act, oa_ready, og_mul = (sem("att_ready"), sem("att_evac"), sem("att_msk"),
                                                                  sem("sg_act"), sem("oa_ready"), sem("og_mul"))
        f_silu = sem("f_silu")
        rot_c, rot_a, kp_rot, kp_ss = sem("rot_c"), sem("rot_a"), sem("kp_rot"), sem("kp_ss")
        q_rot, bsq, bst, bstd, brs, bqk = sem("q_rot"), sem("bsq"), sem("bst"), sem("bstd"), sem("brs"), sem("bqk")
        tq_ready, tk_ready, te_act, te_dve = sem("tq_ready"), sem("tk_ready"), sem("te_act"), sem("te_dve")
        s_ready, s_mx, s_exp, s_dve = sem("s_ready"), sem("s_mx"), sem("s_exp"), sem("s_dve")
        p_ready, pt_ready, pt_evac, ob_ready, ob_act = (sem("p_ready"), sem("pt_ready"), sem("pt_evac"),
                                                        sem("ob_ready"), sem("ob_act"))
        y_tr, y_ev = sem("y_tr"), sem("y_ev")

        def rows(w):
            return w.rearrange("(k p) n -> p k n", p=P)

        w_in, w_outa = rows(gla_w_in[0]), rows(gla_w_out[0])
        w_dq, w_uq, w_outb = rows(mla_w_dq[0]), rows(mla_w_uq[0]), rows(mla_w_out[0])
        w_dkv, w_ukv = rows(kv_w_dkv), rows(kv_w_ukv)
        w_gu = [rows(ffn_w_gu[i]) for i in range(2)]
        w_dn = [rows(ffn_w_down[i]) for i in range(2)]
        w_ada = {0: rows(ada_w[0]), 1: rows(kv_ada_w), 2: rows(ada_w[1])}

        def ada_src(unit0, rel):
            m, base = (0, MOD0) if unit0 < MODKV else (1, MODKV) if unit0 < MOD1 else (2, MOD1)
            return w_ada[m], (unit0 - base + rel) * GW

        def tile(buf, s, k, n):
            return buf[:, s, 0:k * n].rearrange("p (k n) -> p k n", k=k)

        def a_slot(j):
            return adar[:, j] if j < 2 else tile(raw, j, 4, GW)

        def y_bank(g):
            return pt[:, g % 4 // 2, g % 2]

        def lines(v):
            return v.rearrange("(a n) -> a n", n=P)

        rowsets = [lines(ada_b[0]), lines(kv_ada_b), lines(ada_b[1]), lines(c[0]), lines(norm_mix[0]),
                   lines(norm_mix[1]), lines(norm_ffn[0]), lines(norm_ffn[1]), lines(kv_norm), lines(gla_onorm[0]),
                   lines(gla_b_alpha[0]), lines(mla_q_lat_norm[0]), lines(kv_lat_norm), lines(mla_q_norm[0][0:NOPE]),
                   lines(kv_k_norm[0:NOPE])]
        pieces, r = [], 0
        for v in rowsets:
            k = 0
            while k < v.shape[0]:
                m = min(v.shape[0] - k, P - r % P)
                pieces.append((v, k, m, r))
                k, r = k + m, r + m
        assert r == C_QT
        par_dmas = len(pieces) + 4

        block = ctx.enter_context(nc.Block())

        @block.sync
        def _(sp):
            def g_tile(t, s, pieces, first=False):
                if not first:
                    sp.wait_ge(lo_done, whole(t - 3))
                for dst, src in pieces:
                    sp.dma_start(dst, src).then_inc(raw_ld[s], 16)

            def by_k(s, w, k0, k, n, col):
                d = tile(raw, s, k, n)
                h = (k + 1) // 2
                return [(d[:, 0:h], w[:, k0:k0 + h, bass.ds(col, n)]),
                        (d[:, h:k], w[:, k0 + h:k0 + k, bass.ds(col, n)])]

            def by_half(s, w, k0, col_a, col_b):
                d = tile(raw, s, 4, GW)
                return [(d[:, :, 0:256], w[:, k0:k0 + 4, bass.ds(col_a, 256)]),
                        (d[:, :, 256:512], w[:, k0:k0 + 4, bass.ds(col_b, 256)])]

            def a_tile_start(unit, j):
                w, col = ada_src(0, unit)
                if unit:
                    sp.wait_ge(ada_used, unit * 16 + 4 * j - 12)
                for h in range(2):
                    k0 = 4 * j + 2 * h
                    sp.dma_start(a_slot(j)[:, 2 * h:2 * h + 2, :], w[:, k0:k0 + 2, col:col + GW]) \
                        .then_inc(ada_ld[j], 16)

            def a_tile(unit, src, j):
                w, col = src
                sp.wait_ge(ada_used, (unit * 4 + j - 1) * 4)
                for h in range(2):
                    k0 = 4 * j + 2 * h
                    sp.dma_start(adar[:, j % 2, 2 * h:2 * h + 2, :], w[:, k0:k0 + 2, bass.ds(col, GW)]) \
                        .then_inc(ada_ld[j % 2], 16)

            sp.dma_start(xio, x[0].rearrange("(t p) n -> p t n", p=P)).then_inc(x_ld, 16)
            for u in range(8):
                for j in range(4):
                    a_tile_start(u, j)
                if u == 0:
                    g_tile(0, 0, by_k(0, w_in, 0, NB, RANK, 2 * QK_A + 2 * D), first=True)
            def a_with(u0, i, rate, hit):
                if hit is not None:
                    rel = i * rate + hit[0]
                    a_tile(rel + u0, ada_src(u0, rel), hit[1])

            for n in range(3):
                if n:
                    sp.wait_ge(ada_used, 8 * 16 - 8 + 4 * n)
                g_tile(1 + n, 1 + n, by_half(1 + n, w_in, 4 * n, 0, QK_A), first=True)
                a_with(U_GLA, 0, 2, a_of_head(n))
            g_tile(4, 0, by_half(0, w_in, 12, 0, QK_A))
            a_with(U_GLA, 0, 2, a_of_head(3))
            for g in (1, 2):
                for j in range(4):
                    t = 1 + 4 * g + j
                    g_tile(t, t % 4, by_k(t % 4, w_in, 4 * j, 4, GW, 2 * QK_A + (g - 1) * D))
                    a_with(U_GLA, 0, 2, a_of_head(4 * g + j))
            with sp.Fori(1, HEADS_A) as h:
                for g in range(3):
                    for j in range(4):
                        t, s = h * 12 + (1 + 4 * g + j), (1 + j) % 4
                        if g == 0:
                            g_tile(t, s, by_half(s, w_in, 4 * j, h * DK, h * DK + QK_A))
                        else:
                            g_tile(t, s, by_k(s, w_in, 4 * j, 4, GW, h * DV + (2 * QK_A + (g - 1) * D)))
                        a_with(U_GLA, h, 2, a_of_head(4 * g + j))

            def square(w, t0, n, u0, rate):
                for i in steps(sp, n):
                    for u in range(2):
                        for j in range(4):
                            s = (t0 + j) % 4
                            g_tile(i * 8 + (t0 + 4 * u + j), s, by_k(s, w, 4 * j, 4, GW, (i * 2 + u) * GW))
                            a_with(u0, i, rate, a_of(rate, u, j))

            square(w_outa, T_WOA, 2, U_WOA, 2)

            def ffn(layer):
                for kind, t0, g0, o0, n, u0, rate, ch, b0 in ffn_plan(layer):
                    for i in steps(sp, n):
                        for u in range(2):
                            for j in range(4):
                                s = (t0 + j) % 4
                                t = i * 8 + (t0 + 4 * u + j)
                                if kind == "up":
                                    col = (i * 2 + u) * 256 + b0 * P
                                    g_tile(t, s, by_half(s, w_gu[layer], 4 * j, col, col + FF))
                                else:
                                    k = FFC[ch] // 2
                                    g_tile(t, s, by_k(s, w_dn[layer], b0 + k * j, k, GW, (i * 2 + u) * GW))
                                a_with(u0, i, rate, a_of(rate, u, j))

            ffn(0)
            for j in range(4):
                s = (T_DKV + j) % 4
                g_tile(T_DKV + j, s, by_k(s, w_dkv, 4 * j, 4, GW, 0))
                a_tile(U_DKV, ada_src(U_DKV, 0), j)
            s = T_KPE % 4
            g_tile(T_KPE, s, by_k(s, w_dkv, 0, NB, ROPE, LORA))
            for j in range(4):
                s = (T_DQ + j) % 4
                g_tile(T_DQ + j, s, by_k(s, w_dq, 4 * j, 4, GW, 0))
            def mla_tile(i, k):
                s = (T_MLA + k) % 4
                w, n = ((w_uq, 2 * QKD), (w_ukv, 2 * (NOPE + VD)))[k % 2]
                g_tile(i * 4 + (T_MLA + k), s, by_k(s, w, 0, LB, n, (i * 2 + k // 2) * n))

            for k in range(4):
                mla_tile(0, k)
            for pr, i, u in pairs(sp):
                for m in range(2):
                    if not isinstance(pr, int):
                        mla_tile(i, 4 + 2 * u + m)
                    if not isinstance(pr, int) or pr < PAIRS - 1:
                        for j in (2 * m, 2 * m + 1):
                            a_tile(pr + U_PAIR, ada_src(U_PAIR, pr), j)
            square(w_outb, T_WOB, 2, U_WOB, 2)
            ffn(1)
            sp.wait_ge(y_ev, 8)
            sp.dma_start(out[0].rearrange("(t p) n -> p t n", p=P), xio).then_inc(out_st, 16)
            sp.wait_ge(out_st, 16)

        @block.gpsimd
        def _(pool):
            pool.memset(ident[:], 0.0).then_inc(cst_done, 1)
            pool.memset(mask[:], 0.0).then_inc(cst_done, 1)
            pool.memset(a_att, 0.0).then_inc(cst_done, 1)
            for f in range(HALF):
                ins = pool.memset(invf[:, f:f + 1], float(np.float32(THETA) ** np.float32(-np.float32(f) / HALF)))
            ins.then_inc(cst_done, 1)
            pool.wait_ge(cst_done, 4)
            pool.affine_select(out=ident[:], in_=ident[:], compare_op=ALU.not_equal, fill=1.0, base=0,
                               pattern=[[-1, P]], channel_multiplier=1).then_inc(cst_done, 1)
            for b in (0, 2):
                ins = pool.affine_select(out=mask[:, b, :], in_=mask[:, b, :], compare_op=ALU.is_ge, fill=NEG, base=0,
                                         pattern=[[-1, P]], channel_multiplier=1)
            ins.then_inc(cst_done, 1)

            def lo_part(o, dst, src, hi):
                pool.wait_ge(o_hi, o + 1)
                pool.tensor_tensor(dst, src, hi.bitcast(F32), ALU.subtract).then_inc(o_lo, 1)

            def norm_lo(o0, n, hi, lo, b0=0):
                for j in range(n):
                    b = b0 + 2 * j
                    lo_part(o0 + j, lo[:, b:b + 2, :], ht[:, j % 2, :].rearrange("p (b n) -> p b n", b=2),
                            hi[:, b:b + 2, :])

            pool.dma_start(wah, gla_w_alpha[0][:, 0:DK]).then_inc(wah_ld, 16)
            norm_lo(O_N0, 8, hhi, hlo)

            def gla_mask_and_lo(h):
                pool.wait_ge(tr_evac, 5)
                pool.wait_ge(att_evac, h + 1)
                pool.affine_select(out=a_att[:, 0, 0:P], in_=a_att[:, 0, 0:P], compare_op=ALU.is_ge, fill=0.0, base=0,
                                   pattern=[[1, P]], channel_multiplier=-1)
                pool.affine_select(out=a_att[:, 1, P:T], in_=a_att[:, 1, P:T], compare_op=ALU.is_ge, fill=0.0, base=0,
                                   pattern=[[1, P]], channel_multiplier=-1).then_inc(att_msk, 1)
                for e in range(2):
                    lo_part(h * 2 + (O_GLA + e), alo[:, bass.ds(h * 4 + 2 * e, 2), :],
                            ht[:, e, :].rearrange("p (b n) -> p b n", b=2), ahi[:, bass.ds(h * 4 + 2 * e, 2), :])

            with pool.Fori(0, HEADS_A - 1) as h:
                pool.wait_ge(la_ready, h + 1)
                pool.dma_start(wah, gla_w_alpha[0][:, bass.ds(h * DK + DK, DK)]).then_inc(wah_ld, 16)
                gla_mask_and_lo(h)
            gla_mask_and_lo(HEADS_A - 1)

            def ffn(layer):
                for kind, t0, g0, o0, n, u0, rate, ch, b0 in ffn_plan(layer):
                    if kind == "up":
                        for i in steps(pool, n):
                            for u in range(2):
                                lo_part(i * 2 + (o0 + u), alo[:, bass.ds(i * 4 + 2 * u, 2), :],
                                        f_a[:, u, :].rearrange("p (b n) -> p b n", b=2),
                                        ahi[:, bass.ds(i * 4 + 2 * u, 2), :])

            norm_lo(O_NF0, 8, hhi, hlo)
            ffn(0)
            norm_lo(O_NKV, 8, hhi, hlo)
            norm_lo(O_NMX, 8, hhi, hlo)

            def rotate(r1, r2, cos, sin, tmp, done, base):
                for k, (a, b) in enumerate(((r1, cos), (r2, sin), (r2, cos), (r1, sin))):
                    ins = pool.tensor_tensor(tmp[k], a, b, ALU.mult)
                ins.then_inc(done, 1)
                pool.wait_ge(done, base + 1)
                pool.tensor_tensor(r1, tmp[0], tmp[1], ALU.subtract)
                pool.tensor_tensor(r2, tmp[2], tmp[3], ALU.add).then_inc(done, 1)

            pool.wait_ge(pg_free, G_KPE + 1)
            pool.wait_ge(rot_a, 3)
            rotate(kpe[:, :, 0:HALF], kpe[:, :, HALF:ROPE], COS, SIN, [krt[:, k] for k in range(4)], kp_rot, 0)
            norm_lo(O_LKV, 2, ahi, alo, 0)
            norm_lo(O_LQ, 2, ahi, alo, LB)

            def rotate_q(pr, par):
                pool.wait_ge(pg_free, pr * 2 + (G_MLA + 1))
                q4 = b_q[par].rearrange("p t (h n) -> p t h n", h=2)
                cs = [z[:, :, None, :].broadcast_to([P, 2, 2, HALF]) for z in (COS, SIN)]
                tmp = [ht[:, 0, k * 128:(k + 1) * 128].rearrange("p (t h n) -> p t h n", t=2, h=2)
                       for k in range(4)]
                rotate(q4[:, :, :, NOPE:NOPE + HALF], q4[:, :, :, NOPE + HALF:QKD], cs[0], cs[1], tmp, q_rot, pr * 2)

            pool.wait_ge(o_lo, O_MLA)
            rotate_q(0, 0)
            for pr, i, u in pairs(pool):
                if not isinstance(pr, int) or pr < PAIRS - 1:
                    pool.wait_ge(q_rot, pr * 2 + 2)
                    rotate_q(pr + 1, (u + 1) % 2)
                lo_part(pr + O_MLA, hlo[:, bass.ds(pr * 2, 2), :], b_o.rearrange("p (b n) -> p b n", b=2),
                        hhi[:, bass.ds(pr * 2, 2), :])
            norm_lo(O_NF1, 8, hhi, hlo)
            ffn(1)

        @block.scalar
        def _(act):
            def hi(t, s4, s2, n4, free=True, k=4, n=GW):
                act.wait_ge(raw_ld[s4], n4 * 32 + 32)
                for h, (a, b) in enumerate(halves(k)):
                    if free:
                        act.wait_ge(mm_done, whole(t - 2) + (h + 1))
                    act.activation(whi[:, s2, h * 1024:h * 1024 + (b - a) * n], raw[:, s4, a * n:b * n], ACT.Copy).then_inc(hi_done, 1)

            def his(t0, per, i, first, count):
                for k in range(first, first + count):
                    hi(i * per + (t0 + k), (t0 + k) % 4, (t0 + k) % 2, i * (per // 4) + (t0 + k) // 4,
                       True, *tile_shape(t0, k, per))

            for t in range(2):
                act.dma_start(posi[:, t:t + 1], positions[0, t * P:(t + 1) * P].rearrange("(p a) -> p a", a=1)) \
                    .then_inc(pos_ld, 16)
            for v, k, m, r in pieces:
                act.dma_start(vrow[r % P:r % P + m, r // P, :], v[k:k + m, :]).then_inc(par_ld, 16)
            for r, v in ((C_QT, mla_q_norm[0]), (C_KT, kv_k_norm)):
                for h in range(2):
                    act.dma_start(vrow[r % P:r % P + 1, r // P, ROPE * h:ROPE * (h + 1)],
                                  v[NOPE:QKD].rearrange("(a n) -> a n", a=1)).then_inc(par_ld, 16)
            act.wait_ge(tr_evac, 1)
            act.activation(scol[:], cols[:, C_C:C_C + NB], ACT.Silu).then_inc(s_silu, 1)

            def squares(e0, src, n):
                for j in range(n):
                    if e0 + j >= 2:
                        act.wait_ge(ssq_mm, e0 + j - 1)
                    act.activation(sq[:, j % 2, :].rearrange("p (b n) -> p b n", b=2), src[:, 2 * j:2 * j + 2, :],
                                   ACT.Square).then_inc(sq_done, 1)

            def std(e, depth):
                act.wait_ge(ssq_mm, e)
                act.activation(rstd[:], x2[:, 0:T], ACT.Sqrt, bias=EPSC, scale=1.0 / depth).then_inc(std_done, 1)

            def norm_hi(o0, n, dst, b0=0):
                for j in range(n):
                    act.wait_ge(n_fma, FMA[o0] + j + 1)
                    act.activation(dst[:, b0 + 2 * j:b0 + 2 * j + 2, :],
                                   ht[:, j % 2, :].rearrange("p (b n) -> p b n", b=2), ACT.Copy).then_inc(o_hi, 1)

            act.wait_ge(tr_evac, 5)
            act.wait_ge(dcst_done, 3)
            squares(E_N0, xt, 8)
            std(E_N0 + 8, D)
            hi(0, 0, 0, 0, free=False, k=NB, n=RANK)
            norm_hi(O_N0, 8, hhi)
            hi(1, 1, 1, 0, free=False)

            with act.Fori(0, HEADS_A) as h:
                his(T_GLA, 12, h, 1, 1)
                act.wait_ge(la_ready, h + 1)
                for b in range(2):
                    ins = act.activation(a_l[:, b, :], x2[:, b * T:(b + 1) * T], ACT.Identity,
                                         bias=cols[:, bass.ds(h * 2 + (C_BA + b), 1)])
                ins.then_inc(la_act, 1)
                act.wait_ge(la_act, h * 4 + 1)
                act.activation(a_m, a_l, ACT.Abs).then_inc(la_act, 1)
                act.wait_ge(la_act, h * 4 + 2)
                act.activation(a_m, a_m, ACT.Exp, scale=-1.0).then_inc(la_act, 1)
                act.wait_ge(la_act, h * 4 + 3)
                act.activation(a_m, a_m, ACT.Ln, bias=ONEC).then_inc(la_act, 1)
                his(T_GLA, 12, h, 2, 3)
                act.wait_ge(la_dve, h * 4 + 4)
                for n in range(NCH):
                    for b in range(2):
                        act.activation(a_e[:, b, KOFF[n]:KOFF[n] + CH * (n + 1)], a_c[:, b, 0:CH * (n + 1)], ACT.Exp,
                                       bias=a_cs[:, 0, b, n:n + 1], scale=1.0 / TAU)
                        ins = act.activation(a_qd[:, b, CH * n:CH * (n + 1)], a_c[:, b, CH * n:CH * (n + 1)], ACT.Exp,
                                             bias=a_cs[:, 1, b, n:n + 1], scale=-1.0 / TAU)
                ins.then_inc(kexp, 1)
                his(T_GLA, 12, h, 5, 8)
                act.wait_ge(mm_done, whole(h * 12 + (T_GLA + 12)))
                act.activation(a_sg, pg[:, 0], ACT.Sigmoid).then_inc(sg_act, 1)
                act.wait_ge(oa_ready, h + 1)
                for e in range(2):
                    act.wait_ge(ssq_mm, h * 2 + (E_GLA + e - 1))
                    act.activation(sq[:, e, :], xo[:, e, :], ACT.Square).then_inc(sq_done, 1)
                std(h * 2 + (E_GLA + 2), DV)
                for e in range(2):
                    act.wait_ge(og_mul, h * 2 + e + 1)
                    act.activation(ahi[:, bass.ds(h * 4 + 2 * e, 2), :],
                                   ht[:, e, :].rearrange("p (b n) -> p b n", b=2), ACT.Copy).then_inc(o_hi, 1)

            def plain(t0, n):
                for i in steps(act, n):
                    his(t0, 8, i, 1, 8)

            def ffn(layer):
                last_down = T_WOA + 16 if layer == 0 else T_WOB + 16
                for kind, t0, g0, o0, n, u0, rate, ch, b0 in ffn_plan(layer):
                    if kind == "down":
                        if layer == 1 and ch == 2:
                            for i in steps(act, n, peel=True):
                                his(t0, 8, i, 1, 7 if isinstance(i, int) and i == n - 1 else 8)
                        else:
                            plain(t0, n)
                        last_down = t0 + 16
                        continue
                    act.wait_ge(mm_done, whole(last_down))
                    for i in steps(act, n):
                        for u in range(2):
                            his(t0 + 4 * u, 8, i, 1, 4)
                            act.wait_ge(mm_done, whole(i * 8 + (t0 + 4 * u + 4)))
                            act.activation(f_s[:, u, :].rearrange("p (b n) -> p b n", b=2),
                                           pg[:, (g0 + u) % 2, 0:2], ACT.Silu).then_inc(f_silu, 1)
                            act.wait_ge(pg_free, i * 2 + (g0 + u + 1))
                            act.activation(ahi[:, bass.ds(i * 4 + 2 * u, 2), :],
                                           f_a[:, u, :].rearrange("p (b n) -> p b n", b=2), ACT.Copy).then_inc(o_hi, 1)

            plain(T_WOA, 2)
            act.wait_ge(pg_free, G_FFN0)
            squares(E_NF0, xt, 8)
            std(E_NF0 + 8, D)
            norm_hi(O_NF0, 8, hhi)
            ffn(0)
            act.wait_ge(pg_free, G_DKV)
            squares(E_NKV, xt, 8)
            std(E_NKV + 8, D)
            norm_hi(O_NKV, 8, hhi)
            his(T_DKV, 4, 0, 1, 4)
            his(T_KPE, 4, 0, 1, 1)
            act.wait_ge(rot_c, 8)
            act.activation(SIN, ang, ACT.Sin).then_inc(rot_a, 1)
            act.activation(anga, ang, ACT.Abs).then_inc(rot_a, 1)
            act.wait_ge(rot_a, 2)
            act.activation(COS, anga, ACT.Sin, bias=HPIC, scale=-1.0).then_inc(rot_a, 1)
            act.wait_ge(mm_done, whole(T_DQ))
            norm_hi(O_NMX, 8, hhi)
            act.wait_ge(pg_free, G_DKV + 1)
            squares(E_LKV, latk, 2)
            std(E_LKV + 2, LORA)
            norm_hi(O_LKV, 2, ahi, 0)
            his(T_DQ, 4, 0, 1, 4)
            act.wait_ge(pg_free, G_DQ + 1)
            squares(E_LQ, latq, 2)
            std(E_LQ + 2, LORA)
            norm_hi(O_LQ, 2, ahi, LB)

            def square_q(pr, par):
                act.wait_ge(q_rot, pr * 2 + 2)
                act.activation(b_sq, b_q[par].rearrange("p t n -> p (t n)"), ACT.Square).then_inc(bsq, 1)

            def square_k(pr, par):
                act.wait_ge(pg_free, pr * 2 + (G_MLA + 2))
                act.wait_ge(bst, pr * 3 + 1)
                act.activation(b_sq[:, 0:512].rearrange("p (t h n) -> p t h n", t=2, h=2),
                               b_kv[par].rearrange("p t (h n) -> p t h n", h=2)[:, :, :, 0:NOPE], ACT.Square) \
                    .then_inc(bsq, 1)
                act.wait_ge(bst, pr * 3 + 3)
                act.activation(b_st, b_st, ACT.Sqrt, bias=EPSC, scale=1.0 / QKD).then_inc(bstd, 1)

            his(T_MLA, 4, 0, 1, 2)
            act.wait_ge(o_lo, O_MLA)
            square_q(0, 0)
            square_k(0, 0)
            his(T_MLA, 4, 0, 3, 1)
            for pr, i, u in pairs(act):
                nxt = not isinstance(pr, int) or pr < PAIRS - 1
                act.wait_ge(tq_ready, pr + 1)
                act.activation(b_qt.rearrange("p h n -> p (h n)"), xo[:, 0, :], ACT.Copy, scale=cols[:, C_QN:C_QN + 1])
                act.wait_ge(tk_ready, pr + 1)
                act.activation(b_kt.rearrange("p h n -> p (h n)"), x3[:], ACT.Copy, scale=cols[:, C_KN:C_KN + 1]) \
                    .then_inc(te_act, 1)
                if not isinstance(pr, int):
                    his(T_MLA + 2 * u, 4, i, 4, 1)
                elif not nxt:
                    his(T_WOB, 4, 0, 0, 1)
                for h in range(2):
                    act.wait_ge(s_mx, pr * 2 + h + 1)
                    for q, (a, b) in enumerate(((0, P), (P, 3 * P))):
                        ins = act.activation(b_p[:, h, a:b], b_p[:, h, a:b], ACT.Exp,
                                             bias=b_mx[:, 2 * h + q:2 * h + q + 1],
                                             accum_out=b_sm[:, 2 * h + q:2 * h + q + 1])
                    ins.then_inc(s_exp, 1)
                if nxt:
                    square_q(pr + 1, (u + 1) % 2)
                for h in range(2):
                    act.wait_ge(pt_ready, pr * 2 + h + 1)
                    act.activation(b_pt[:, h, :], xo[:, 1 - h, 0:3 * P], ACT.Copy).then_inc(pt_evac, 1)
                if nxt:
                    square_k(pr + 1, (u + 1) % 2)
                act.wait_ge(ob_ready, pr + 1)
                act.wait_ge(o_lo, pr + O_MLA)
                act.activation(b_o, x3[:], ACT.Copy).then_inc(ob_act, 1)
                act.wait_ge(ob_act, pr + 1)
                act.activation(hhi[:, bass.ds(pr * 2, 2), :], b_o.rearrange("p (b n) -> p b n", b=2), ACT.Copy) \
                    .then_inc(o_hi, 1)
                if not isinstance(pr, int):
                    his(T_MLA + 2 * u, 4, i, 5, 1)
            plain(T_WOB, 2)
            act.wait_ge(pg_free, G_FFN1)
            squares(E_NF1, xt, 8)
            std(E_NF1 + 8, D)
            norm_hi(O_NF1, 8, hhi)
            ffn(1)

        @block.vector
        def _(dve):
            def lo(t, s4, s2, k=4, n=GW):
                for h, (a, b) in enumerate(halves(k)):
                    dve.wait_ge(hi_done, whole(t) + (h + 1))
                    c0, c1 = h * 1024, h * 1024 + (b - a) * n
                    dve.tensor_tensor(wlo[:, s2, c0:c1], raw[:, s4, a * n:b * n], whi[:, s2, c0:c1].bitcast(F32),
                                      ALU.subtract).then_inc(lo_done, 1)

            def ada(unit, j, start=False, first=False):
                if start:
                    buf = a_slot(j)
                    dve.wait_ge(ada_ld[j], unit * 32 + 32)
                else:
                    buf = adar[:, j % 2]
                    dve.wait_ge(ada_ld[j % 2], (unit * 2 + j // 2 - 8) * 32 + 32)
                for q in range(4):
                    k = 4 * j + q
                    if k < 2:
                        if not first and k == 0:
                            dve.wait_ge(modp_ready, unit)
                        dve.tensor_scalar(acc[:, k, :], buf[:, q, :], scol[:, k:k + 1], None, ALU.mult) \
                            .then_inc(ada_used, 1)
                    else:
                        dve.wait_ge(ada_used, unit * 16 + (k - 1))
                        dve.scalar_tensor_tensor(out=acc[:, k % 2, :], in0=buf[:, q, :], scalar=scol[:, k:k + 1],
                                                 in1=acc[:, k % 2, :], op0=ALU.mult, op1=ALU.add) \
                            .then_inc(ada_used, 1)

            def mod(unit):
                dve.wait_ge(modp_ready, unit + 1)
                dve.tensor_tensor(mods[:, bass.ds(unit * 4, 4)], x2[:, 508:512], cols[:, bass.ds(unit * 4, 4)],
                                  ALU.add).then_inc(mods_done, 1)

            def los(t0, per, i, first, count, hits=(None,) * 4):
                for n, k in enumerate(range(first, first + count)):
                    lo(i * per + (t0 + k), (t0 + k) % 4, (t0 + k) % 2, *tile_shape(t0, k, per))
                    if hits[n] is not None:
                        ada(*hits[n])

            def a_hits(u0, i, rate, u):
                hits = [a_of(rate, u, j) for j in range(4)]
                return [hit and (i * rate + (u0 + hit[0]), hit[1]) for hit in hits]

            def mod_at(u0, i, rate, u):
                if rate == 2 or (rate == 1 and u == 1):
                    mod(i * rate + (u0 + (u if rate == 2 else 0)))

            dve.memset(ones[:], 1.0).then_inc(dcst_done, 1)
            dve.memset(cst[:, 0:1], EPS)
            dve.memset(cst[:, 1:2], 1.0)
            dve.memset(cst[:, 2:3], float(np.pi / 2)).then_inc(dcst_done, 1)
            dve.memset(nrow[:], 0.0).then_inc(dcst_done, 1)
            dve.wait_ge(tr_ready, 1)
            dve.tensor_copy(cols[:], x3[:, 0:C_END]).then_inc(tr_evac, 1)
            for g in range(4):
                dve.wait_ge(tr_ready, g + 2)
                dve.tensor_copy(xt[:, 4 * g:4 * g + 4, :], pg[:, g % 2]).then_inc(tr_evac, 1)

            def gain(n, unit0, gcol):
                dve.scalar_tensor_tensor(out=avec[:], in0=mods[:, 4 * unit0:4 * unit0 + NB], scalar=1.0,
                                         in1=cols[:, gcol:gcol + NB], op0=ALU.add, op1=ALU.mult).then_inc(a_done, 1)
                dve.wait_ge(a_done, n + 1)

            def recip(s):
                dve.wait_ge(std_done, s + 1)
                dve.reciprocal(rstd[:], rstd[:]).then_inc(rstd_done, 1)
                dve.wait_ge(rstd_done, s + 1)

            def norm_apply(o0, n, src, a, shift):
                for j in range(n):
                    o, m = o0 + j, FMA[o0] + j
                    if o >= 2:
                        dve.wait_ge(o_lo, o - 1)
                    v = ht[:, j % 2, :].rearrange("p (b n) -> p b n", b=2)
                    dve.tensor_tensor(v, src[:, 2 * j:2 * j + 2, :], rstd[:, None, :].broadcast_to([P, 2, T]),
                                      ALU.mult).then_inc(n_mul, 1)
                    dve.wait_ge(n_mul, m + 1)
                    for b in range(2):
                        k = 2 * j + b
                        if shift is None:
                            ins = dve.tensor_scalar(v[:, b, :], v[:, b, :], a[:, k:k + 1], None, ALU.mult)
                        else:
                            ins = dve.tensor_scalar(v[:, b, :], v[:, b, :], a[:, k:k + 1], shift[:, k:k + 1],
                                                    ALU.mult, ALU.add)
                    ins.then_inc(n_fma, 1)

            dve.wait_ge(s_silu, 1)
            for u in range(8):
                for j in range(4):
                    ada(u, j, start=True, first=(u == 0))
                mod(u)
            dve.wait_ge(mods_done, 8)
            gain(0, 4, C_NMIX)
            recip(S_N0)
            lo(0, 0, 0, NB, RANK)
            norm_apply(O_N0, 8, xt, avec, mods[:, 0:NB])
            lo(1, 1, 1)
            dve.wait_ge(mm_done, whole(1))
            dve.tensor_copy(a_lr, pt[:, 1, :, 0:RANK]).then_inc(pg_free, 1)
            dve.wait_ge(lr_tr, 1)
            dve.tensor_copy(alrt, x3[0:RANK, 0:T]).then_inc(lr_ready, 1)

            with dve.Fori(0, HEADS_A) as h:
                def los_head(first, count):
                    for pos in range(first, first + count):
                        hit = a_of_head(pos)
                        los(T_GLA, 12, h, pos + 1, 1, (hit and (h * 2 + (U_GLA + hit[0]), hit[1]),))

                los_head(0, 1)
                dve.wait_ge(la_act, h * 4 + 4)
                dve.tensor_scalar(a_l, a_l, -1.0, 0.0, ALU.mult, ALU.max).then_inc(la_used, 1)
                dve.wait_ge(la_used, h + 1)
                dve.tensor_tensor(a_l, a_l, a_m, ALU.add).then_inc(la_dve, 1)
                dve.wait_ge(la_dve, h * 4 + 1)
                for b in range(2):
                    dve.tensor_tensor_scan(a_c[:, b, :], ones[:, 0:1].broadcast_to([P, T]), a_l[:, b, :], 0.0, ALU.mult, ALU.add) \
                        .then_inc(la_dve, 1)
                dve.wait_ge(la_dve, h * 4 + 3)
                for s in range(2):
                    ins = dve.tensor_scalar(a_cs[:, s, :, 1:NCH], a_c[:, :, CH - 1:T - CH:CH],
                                            (-1.0 / TAU, 1.0 / TAU)[s], None, ALU.mult)
                ins.then_inc(la_dve, 1)
                los_head(1, 3)
                dve.wait_ge(mm_done, whole(h * 12 + (T_GLA + 4)))
                dve.tensor_copy(a_qk, pg[:, 0]).then_inc(pg_free, 1)
                los_head(4, 1)
                dve.wait_ge(kexp, h + 1)
                dve.wait_ge(pg_free, h * 3 + 2)
                for n in range(NCH):
                    v = a_e[:, :, KOFF[n]:KOFF[n] + CH * (n + 1)]
                    dve.tensor_tensor(v, v, a_qk[:, 2:4, 0:CH * (n + 1)], ALU.mult)
                dve.scalar_tensor_tensor(out=a_qd, in0=a_qk[:, 0:2, :], scalar=float(DK) ** -0.5, in1=a_qd,
                                         op0=ALU.mult, op1=ALU.mult).then_inc(kq_ready, 1)
                los_head(5, 3)
                dve.wait_ge(mm_done, whole(h * 12 + (T_GLA + 8)))
                dve.tensor_copy(a_v, pt[:, 1]).then_inc(pg_free, 1)
                mod(h * 2 + U_GLA)
                los_head(8, 1)
                dve.wait_ge(att_ready, h + 1)
                dve.tensor_copy(a_att[0:CH, 0, 0:CH], x3[0:CH, 0:CH])
                dve.tensor_copy(a_att[:, 0, CH:T], x3[:, CH:T])
                dve.tensor_copy(a_att[0:CH, 1, P:P + CH], x3[0:CH, T + P:T + P + CH])
                dve.tensor_copy(a_att[:, 1, P + CH:T], x3[:, T + P + CH:2 * T]).then_inc(att_evac, 1)
                los_head(9, 3)
                dve.wait_ge(sg_act, h + 1)
                dve.tensor_tensor(a_sg, a_sg, pg[:, 0], ALU.mult).then_inc(pg_free, 1)
                mod(h * 2 + (U_GLA + 1))
                recip_h = h + (S_GLA + 1)
                dve.wait_ge(std_done, recip_h)
                dve.reciprocal(rstd[:], rstd[:]).then_inc(rstd_done, 1)
                dve.wait_ge(rstd_done, recip_h)
                dve.wait_ge(pg_free, h * 3 + (G_GLA + 3))
                for e in range(2):
                    dve.wait_ge(o_lo, h * 2 + (O_GLA + e - 1))
                    for b in range(2):
                        k = 2 * e + b
                        ins = dve.scalar_tensor_tensor(out=ht[:, e, b * T:(b + 1) * T], in0=xo[:, e, b * T:(b + 1) * T],
                                                       scalar=cols[:, C_ON + k:C_ON + k + 1], in1=rstd[:],
                                                       op0=ALU.mult, op1=ALU.mult)
                    ins.then_inc(oa_norm, 1)
                    dve.wait_ge(oa_norm, h * 2 + e + 1)
                    dve.tensor_tensor(ht[:, e, :], ht[:, e, :],
                                      a_sg[:, 2 * e:2 * e + 2, :].rearrange("p b n -> p (b n)"), ALU.mult) \
                        .then_inc(og_mul, 1)

            def residual(t, g, set_, blk, gate):
                dve.wait_ge(mm_done, whole(t))
                for b in range(4):
                    ins = dve.scalar_tensor_tensor(out=xt[:, bass.ds(blk + b, 1), :].rearrange("p b n -> p (b n)"),
                                                   in0=pg[:, set_, b, :], scalar=mods[:, bass.ds(gate + b, 1)],
                                                   in1=xt[:, bass.ds(blk + b, 1), :].rearrange("p b n -> p (b n)"),
                                                   op0=ALU.mult, op1=ALU.add)
                ins.then_inc(pg_free, 1)

            def down(t0, g0, n, set0, gate_unit, rate=0, u0=0, peel=False):
                dve.wait_ge(pg_free, g0)
                dve.wait_ge(mods_done, gate_unit + 4)
                for i in steps(dve, n, peel):
                    for u in range(2):
                        last = peel and isinstance(i, int) and i == n - 1 and u == 1
                        los(t0 + 4 * u, 8, i, 1, 3 if last else 4, a_hits(u0, i, rate, u))
                        residual(i * 8 + (t0 + 4 * u + 4), None, (set0 + u) % 2, i * 8 + 4 * u,
                                 i * 8 + (4 * gate_unit + 4 * u))
                        mod_at(u0, i, rate, u)

            def ffn(layer):
                base = MOD0 if layer == 0 else MOD1
                for kind, t0, g0, o0, n, u0, rate, ch, b0 in ffn_plan(layer):
                    set0 = g0 % 2
                    if kind == "down":
                        down(t0, g0, n, set0, base + 20, rate, u0, peel=(layer == 1 and ch == 2))
                        continue
                    for i in steps(dve, n):
                        for u in range(2):
                            los(t0 + 4 * u, 8, i, 1, 4, a_hits(u0, i, rate, u))
                            dve.wait_ge(f_silu, i * 2 + (o0 + u + 1 - (O_FFN0, O_FFN1 - FF // T)[layer]))
                            dve.wait_ge(o_lo, i * 2 + (o0 + u - 1))
                            dve.tensor_tensor(f_a[:, u, :].rearrange("p (b n) -> p b n", b=2),
                                              f_s[:, u, :].rearrange("p (b n) -> p b n", b=2),
                                              pg[:, (set0 + u) % 2, 2:4], ALU.mult).then_inc(pg_free, 1)
                            mod_at(u0, i, rate, u)

            down(T_WOA, G_WOA, 2, 1, MOD0 + 8, 2, U_WOA)
            dve.wait_ge(mods_done, 20)
            gain(1, 16, C_NFFN)
            recip(S_NF0)
            norm_apply(O_NF0, 8, xt, avec, mods[:, 12 * 4:12 * 4 + NB])
            ffn(0)
            dve.wait_ge(mods_done, U_DKV)
            gain(2, MODKV + 4, C_KVN)
            recip(S_NKV)
            norm_apply(O_NKV, 8, xt, avec, mods[:, 4 * MODKV:4 * MODKV + NB])
            los(T_DKV, 4, 0, 1, 1, [(U_DKV, 0)])
            dve.wait_ge(pos_ld, 32)
            dve.wait_ge(cst_done, 6)
            dve.tensor_copy(posf, posi[:]).then_inc(rot_c, 1)
            dve.wait_ge(rot_c, 1)
            for t in range(2):
                ins = dve.tensor_scalar(ang[:, t, :], invf[:, 0:HALF], posf[:, t:t + 1], None, ALU.mult)
            ins.then_inc(rot_c, 1)
            dve.wait_ge(rot_c, 2)
            dve.tensor_scalar(angk, ang, float(1.0 / TWO_PI), MAGIC, ALU.mult, ALU.add).then_inc(rot_c, 1)
            dve.wait_ge(rot_c, 3)
            dve.tensor_scalar(angk, angk, MAGIC, None, ALU.subtract).then_inc(rot_c, 1)
            for k, part in enumerate((PI_A, PI_B, PI_C)):
                dve.wait_ge(rot_c, 4 + k)
                dve.scalar_tensor_tensor(out=ang, in0=angk, scalar=-part, in1=ang, op0=ALU.mult, op1=ALU.add) \
                    .then_inc(rot_c, 1)
            dve.wait_ge(rot_c, 7)
            dve.tensor_scalar(ang, ang, 3.1415925, -3.1415925, ALU.min, ALU.max).then_inc(rot_c, 1)
            los(T_DKV, 4, 0, 2, 3, [(U_DKV, j) for j in range(1, 4)])
            dve.wait_ge(mm_done, whole(T_DKV + 4))
            dve.tensor_copy(latk, pg[:, 1]).then_inc(pg_free, 1)
            mod(U_DKV)
            los(T_KPE, 4, 0, 1, 1)
            dve.wait_ge(mm_done, whole(T_KPE + 1))
            dve.tensor_copy(kpe[:], pt[:, 0, :, 0:ROPE]).then_inc(pg_free, 1)
            gain(3, MOD1 + 4, C_NMIX + NB)
            norm_apply(O_NMX, 8, xt, avec, mods[:, 4 * MOD1:4 * MOD1 + NB])
            recip(S_LKV)
            norm_apply(O_LKV, 2, latk, cols[:, C_KL:C_KL + LB], None)
            dve.wait_ge(kp_rot, 2)
            dve.tensor_tensor(krw, kpe[:], kpe[:], ALU.mult).then_inc(kp_ss, 1)
            dve.wait_ge(kp_ss, 1)
            dve.tensor_reduce(kss, krw, AX.X, ALU.add).then_inc(kp_ss, 1)
            los(T_DQ, 4, 0, 1, 4)
            dve.wait_ge(mm_done, whole(T_DQ + 4))
            dve.tensor_copy(latq, pg[:, 1]).then_inc(pg_free, 1)
            recip(S_LQ)
            norm_apply(O_LQ, 2, latq, cols[:, C_QL:C_QL + LB], None)
            dve.wait_ge(kp_ss, 2)

            def bring_q(pr, par):
                dve.wait_ge(mm_done, whole(pr * 2 + (T_MLA + 1)))
                dve.tensor_copy(b_q[par], pt[:, 0, :, 0:2 * QKD]).then_inc(pg_free, 1)

            def bring_kv(pr, par):
                dve.wait_ge(mm_done, whole(pr * 2 + (T_MLA + 2)))
                dve.tensor_copy(b_kv[par], pt[:, 1]).then_inc(pg_free, 1)

            def sum_q(pr):
                dve.wait_ge(bsq, pr * 2 + 1)
                dve.tensor_reduce(b_st[:, 0:4], b_sq.rearrange("p (a n) -> p a n", a=4), AX.X, ALU.add) \
                    .then_inc(bst, 1)

            def sum_k(pr):
                dve.wait_ge(bsq, pr * 2 + 2)
                dve.tensor_reduce(b_st[:, 4:8], b_sq[:, 0:512].rearrange("p (a n) -> p a n", a=4), AX.X, ALU.add) \
                    .then_inc(bst, 1)
                dve.wait_ge(bst, pr * 3 + 2)
                k_st = b_st[:, 4:8].rearrange("p (t h) -> p t h", t=2)
                dve.tensor_tensor(k_st, k_st, kss[:, :, None].broadcast_to([P, 2, 2]), ALU.add).then_inc(bst, 1)

            def scale_qk(pr, par):
                dve.wait_ge(bstd, pr + 1)
                dve.reciprocal(b_st, b_st).then_inc(brs, 1)
                dve.wait_ge(brs, pr + 1)
                q4 = b_q[par].rearrange("p t (h n) -> p t h n", h=2)
                k4 = b_kv[par].rearrange("p t (h n) -> p t h n", h=2)[:, :, :, 0:NOPE]
                r4 = b_st.rearrange("p (a t h) -> p a t h", a=2, t=2)
                dve.tensor_tensor(b_qp, q4[:, :, :, NOPE:QKD], r4[:, 0, :, :, None].broadcast_to([P, 2, 2, ROPE]),
                                  ALU.mult)
                q4 = q4[:, :, :, 0:NOPE]
                dve.tensor_tensor(q4, q4, r4[:, 0, :, :, None].broadcast_to([P, 2, 2, NOPE]), ALU.mult) \
                    .then_inc(bqk, 1)
                dve.tensor_tensor(k4, k4, r4[:, 1, :, :, None].broadcast_to([P, 2, 2, NOPE]), ALU.mult)
                dve.tensor_tensor(b_kp, kpe[:, :, None, :].broadcast_to([P, 2, 2, ROPE]),
                                  r4[:, 1, :, :, None].broadcast_to([P, 2, 2, ROPE]), ALU.mult).then_inc(bqk, 1)

            los(T_MLA, 4, 0, 1, 1)
            bring_q(0, 0)
            los(T_MLA, 4, 0, 2, 1)
            ada(U_PAIR, 0)
            bring_kv(0, 0)
            sum_q(0)
            sum_k(0)
            ada(U_PAIR, 1)
            scale_qk(0, 0)
            los(T_MLA, 4, 0, 3, 1)
            for pr, i, u in pairs(dve):
                nxt = not isinstance(pr, int) or pr < PAIRS - 1
                dve.wait_ge(tk_ready, pr + 1)
                dve.tensor_scalar(b_rt[:, 0, :], xo[:, 1, 0:T], cols[:, C_QT:C_QT + 1], None, ALU.mult)
                dve.tensor_scalar(b_rt[:, 1, :], xo[:, 1, T:2 * T], cols[:, C_KT:C_KT + 1], None, ALU.mult) \
                    .then_inc(te_dve, 1)
                if nxt:
                    ada(pr + U_PAIR, 2)
                    bring_q(pr + 1, (u + 1) % 2)
                    ada(pr + U_PAIR, 3)
                for h in range(2):
                    s = (xo[:, 0, 0:3 * P], x3[:, 0:3 * P])[h]
                    d0 = pr * 6 + 2 * h
                    dve.wait_ge(s_ready, pr * 2 + h + 1)
                    dve.scalar_tensor_tensor(out=b_p[:, h, :], in0=s, scalar=float(QKD) ** -0.5,
                                             in1=mask[:].rearrange("p b n -> p (b n)"), op0=ALU.mult,
                                             op1=ALU.add).then_inc(s_dve, 1)
                    dve.wait_ge(s_dve, d0 + 1)
                    dve.tensor_reduce(b_mx[:, 2 * h:2 * h + 1], b_p[:, h, 0:P], AX.X, ALU.max)
                    dve.tensor_reduce(b_mx[:, 2 * h + 1:2 * h + 2], b_p[:, h, P:3 * P], AX.X, ALU.max) \
                        .then_inc(s_dve, 1)
                    dve.wait_ge(s_dve, d0 + 2)
                    dve.tensor_scalar(b_mx[:, 2 * h:2 * h + 2], b_mx[:, 2 * h:2 * h + 2], -1.0, None, ALU.mult) \
                        .then_inc(s_mx, 1)
                if not isinstance(pr, int):
                    los(T_MLA + 2 * u, 4, i, 4, 1)
                elif not nxt:
                    los(T_WOB, 4, 0, 0, 1)
                for h in range(2):
                    dve.wait_ge(s_exp, pr * 2 + h + 1)
                    dve.reciprocal(b_sm[:, 2 * h:2 * h + 2], b_sm[:, 2 * h:2 * h + 2]).then_inc(s_dve, 1)
                    dve.wait_ge(s_dve, pr * 6 + (5 + h))
                    dve.tensor_scalar(b_p[:, h, 0:P], b_p[:, h, 0:P], b_sm[:, 2 * h:2 * h + 1], None, ALU.mult)
                    dve.tensor_scalar(b_p[:, h, P:3 * P], b_p[:, h, P:3 * P], b_sm[:, 2 * h + 1:2 * h + 2], None,
                                      ALU.mult).then_inc(p_ready, 1)
                if nxt:
                    mod(pr + U_PAIR)
                    sum_q(pr + 1)
                    bring_kv(pr + 1, (u + 1) % 2)
                    if not isinstance(pr, int):
                        ada(pr + (U_PAIR + 1), 0)
                    sum_k(pr + 1)
                    if not isinstance(pr, int):
                        ada(pr + (U_PAIR + 1), 1)
                    scale_qk(pr + 1, (u + 1) % 2)
                if not isinstance(pr, int):
                    los(T_MLA + 2 * u, 4, i, 5, 1)
            down(T_WOB, G_WOB, 2, 0, MOD1 + 8, 2, U_WOB)
            dve.wait_ge(mods_done, 52)
            gain(4, MOD1 + 16, C_NFFN + NB)
            recip(S_NF1)
            norm_apply(O_NF1, 8, xt, avec, mods[:, 4 * (MOD1 + 12):4 * (MOD1 + 12) + NB])
            ffn(1)
            for g in range(8):
                dve.wait_ge(y_tr, g + 1)
                dve.tensor_copy(xio[:, g // 4, (g % 4) * 512:(g % 4 + 1) * 512], y_bank(g)).then_inc(y_ev, 1)

        @block.tensor
        def _(pe):
            def split3(dst, w, x_, start, stop):
                (w_h, w_l), (x_h, x_l) = w, x_
                pe.matmul(dst, w_h, x_h, start=start, stop=False, skip_group_check=True)
                pe.matmul(dst, w_h, x_l, start=False, stop=False, skip_group_check=True)
                return pe.matmul(dst, w_l, x_h, start=False, stop=stop, skip_group_check=True)

            def feature_tile(t, s2, set_, kts, k0, right, j, last_j, dst_cols=4):
                r_hi, r_lo = right
                for h, (ka, kb) in enumerate(halves(kts)):
                    pe.wait_ge(lo_done, whole(t) + (h + 1))
                    for k in range(ka, kb):
                        for b in range(4):
                            c0 = h * 1024 + (k - ka) * GW + b * P
                            ins = split3(pg[:, set_, b, :], (whi[:, s2, c0:c0 + P], wlo[:, s2, c0:c0 + P]),
                                         (r_hi[:, k0 + k, :], r_lo[:, k0 + k, :]),
                                         start=(j == 0 and k == 0 and b % 2 == 0), stop=(j == last_j and k == kts - 1))
                    ins.then_inc(mm_done, 1)

            def token_tile(t, s2, set_, kts, n, k0, left, first, last):
                l_hi, l_lo = left
                for h, (ka, kb) in enumerate(halves(kts)):
                    pe.wait_ge(lo_done, whole(t) + (h + 1))
                    for k in range(ka, kb):
                        c0 = h * 1024 + (k - ka) * n
                        for tt in range(2):
                            w_h, w_l = whi[:, s2, c0:c0 + n], wlo[:, s2, c0:c0 + n]
                            a_h = l_hi[:, k0 + k, tt * P:(tt + 1) * P]
                            a_lw = l_lo[:, k0 + k, tt * P:(tt + 1) * P]
                            ins = split3(pt[:, set_, tt, 0:n], (a_h, a_lw), (w_h, w_l),
                                         start=(first and k == 0), stop=(last and k == kts - 1))
                    ins.then_inc(mm_done, 1)

            def reduce_unit(unit, std):
                pe.wait_ge(ada_used, unit * 16 + 16)
                if not isinstance(unit, int) or unit:
                    pe.wait_ge(mods_done, unit)
                if std is not None:
                    pe.wait_ge(std_done, std)
                for b in range(4):
                    for e in range(2):
                        ins = pe.matmul(x2[:, 508 + b:509 + b], acc[:, e, b * P:(b + 1) * P], ones[:, 0:1],
                                        start=(e == 0), stop=(e == 1))
                ins.then_inc(modp_ready, 1)

            def sumsq(e0, n, units, s):
                if units:
                    pe.wait_ge(mods_done, units)
                    pe.wait_ge(std_done, s)
                for j in range(n):
                    pe.wait_ge(sq_done, e0 + j + 1)
                    for b in range(2):
                        ins = pe.matmul(x2[:, 0:T], ones[:], sq[:, j % 2, b * T:(b + 1) * T],
                                        start=(j == 0 and b == 0), stop=(j == n - 1 and b == 1))
                    ins.then_inc(ssq_mm, 1)

            pe.wait_ge(cst_done, 6)
            pe.wait_ge(par_ld, par_dmas * 16)
            for k in range(3):
                n = min(P, C_END - k * P)
                ins = pe.matmul(x3[:, k * P:k * P + n], vrow[0:n, k, :], ident[0:n, 0:n], start=True, stop=True)
            ins.then_inc(tr_ready, 1)
            pe.wait_ge(x_ld, 16)
            for g in range(4):
                if g >= 2:
                    pe.wait_ge(tr_evac, g)
                for b in range(4):
                    for tt in range(2):
                        ins = pe.matmul(pg[:, g % 2, b, tt * P:(tt + 1) * P],
                                        xio[:, tt, (4 * g + b) * P:(4 * g + b + 1) * P], ident[:], start=True, stop=True)
                ins.then_inc(tr_ready, 1)
            pe.wait_ge(dcst_done, 1)
            sumsq(E_N0, 8, 0, 0)
            for u in range(8):
                reduce_unit(u, 1)

            h2 = (hhi, hlo)
            a2 = (ahi, alo)
            pe.wait_ge(tr_evac, 5)
            pe.wait_ge(o_lo, O_N0 + 8)
            token_tile(0, 0, 1, NB, RANK, 0, h2, True, True)
            pe.wait_ge(pg_free, G_LOW + 1)
            for tt in range(2):
                ins = pe.matmul(x3[0:RANK, tt * P:(tt + 1) * P], a_lr[:, tt, :], ident[:], start=True, stop=True)
            ins.then_inc(lr_tr, 1)
            pe.wait_ge(lr_ready, 1)

            with pe.Fori(0, HEADS_A) as h:
                pe.wait_ge(wah_ld, h * 16 + 16)
                pe.wait_ge(std_done, h + S_GLA)
                pe.wait_ge(mods_done, h * 2 + U_GLA)
                for b in range(2):
                    ins = pe.matmul(x2[:, b * T:(b + 1) * T], wah[:, b * P:(b + 1) * P], alrt, start=True, stop=True)
                ins.then_inc(la_ready, 1)
                pe.wait_ge(pg_free, h * 3 + G_GLA)
                for j in range(4):
                    feature_tile(h * 12 + (T_GLA + j), (T_GLA + j) % 2, 0, 4, 4 * j, h2, j, 3)
                pe.wait_ge(pg_free, h * 3 + G_GLA)
                for j in range(4):
                    token_tile(h * 12 + (T_GLA + 4 + j), (T_GLA + j) % 2, 1, 4, GW, 4 * j, h2, j == 0, j == 3)
                pe.wait_ge(la_act, h * 4 + 1)
                reduce_unit(h * 2 + U_GLA, None)
                pe.wait_ge(kq_ready, h + 1)
                for n in range(NCH):
                    for kt in range((n + 2) // 2):
                        m = min(P, CH * (n + 1) - kt * P)
                        for b in range(2):
                            c0 = KOFF[n] + kt * P
                            ins = pe.matmul(x3[0:m, kt * T + CH * n:kt * T + CH * (n + 1)], a_e[:, b, c0:c0 + m],
                                            a_qd[:, b, CH * n:CH * (n + 1)], start=(b == 0), stop=(b == 1))
                ins.then_inc(att_ready, 1)
                pe.wait_ge(pg_free, h * 3 + (G_GLA + 1))
                for j in range(4):
                    feature_tile(h * 12 + (T_GLA + 8 + j), (T_GLA + j) % 2, 0, 4, 4 * j, h2, j, 3)
                reduce_unit(h * 2 + (U_GLA + 1), None)
                pe.wait_ge(att_msk, h + 1)
                pe.wait_ge(o_hi, h * 2 + O_GLA)
                for b in range(4):
                    v = [a_v[:, kt, b * P:(b + 1) * P] for kt in range(2)]
                    o = xo[:, b // 2, (b % 2) * T:(b % 2 + 1) * T]
                    pe.matmul(o, v[0], a_att[:, 0, :], start=True, stop=False, skip_group_check=True)
                    ins = pe.matmul(o[:, P:T], v[1], a_att[:, 1, P:T], start=False, stop=True, skip_group_check=True)
                ins.then_inc(oa_ready, 1)
                pe.wait_ge(mods_done, h * 2 + (U_GLA + 2))
                for e in range(2):
                    pe.wait_ge(sq_done, h * 2 + (E_GLA + e + 1))
                    for b in range(2):
                        ins = pe.matmul(x2[:, 0:T], ones[:], sq[:, e, b * T:(b + 1) * T],
                                        start=(e == 0 and b == 0), stop=(e == 1 and b == 1))
                    ins.then_inc(ssq_mm, 1)

            def product(t0, g0, n, set0, right, kts=4, o_wait=None, rate=0, u0=0, std=None):
                for i in steps(pe, n):
                    for u in range(2):
                        pe.wait_ge(pg_free, i * 2 + (g0 + u - 1))
                        for j in range(4):
                            if u == 0 and o_wait is not None:
                                pe.wait_ge(o_lo, o_wait + ((j + 1) * kts + 1) // 2)
                            feature_tile(i * 8 + (t0 + 4 * u + j), (t0 + j) % 2, (set0 + u) % 2, kts, kts * j, right,
                                         j, 3)
                        if rate == 2 or (rate == 1 and u == 1):
                            reduce_unit(i * rate + (u0 + (u if rate == 2 else 0)), std)

            def ffn(layer):
                o_n = O_NF0 if layer == 0 else O_NF1
                for kind, t0, g0, o0, n, u0, rate, ch, b0 in ffn_plan(layer):
                    set0 = g0 % 2
                    std = (S_NF0 if layer == 0 else S_NF1) + 1
                    if kind == "up":
                        product(t0, g0, n, set0, h2, 4, o_n, rate, u0, std)
                    else:
                        product(t0, g0, n, set0, a2, FFC[ch] // 2, o0, rate, u0, std)

            product(T_WOA, G_WOA, 2, 1, a2, 4, O_GLA, 2, U_WOA, S_NF0)
            sumsq(E_NF0, 8, U_FFN0, S_NF0)
            ffn(0)
            sumsq(E_NKV, 8, U_DKV, S_NKV)
            pe.wait_ge(pg_free, G_DKV)
            for j in range(4):
                pe.wait_ge(o_lo, O_NKV + 2 * (j + 1))
                feature_tile(T_DKV + j, (T_DKV + j) % 2, 1, 4, 4 * j, h2, j, 3)
            reduce_unit(U_DKV, S_NKV + 1)
            token_tile(T_KPE, T_KPE % 2, 0, NB, ROPE, 0, h2, True, True)
            sumsq(E_LKV, 2, U_PAIR, S_LKV)
            for j in range(4):
                pe.wait_ge(o_lo, O_NMX + 2 * (j + 1))
                feature_tile(T_DQ + j, (T_DQ + j) % 2, 1, 4, 4 * j, h2, j, 3)
            sumsq(E_LQ, 2, U_PAIR, S_LQ)
            pe.wait_ge(o_lo, O_LQ + 2)

            def project_q(pr):
                pe.wait_ge(pg_free, pr * 2 + (G_MLA - 1))
                token_tile(pr * 2 + T_MLA, T_MLA % 2, 0, LB, 2 * QKD, LB, a2, True, True)

            def project_kv(pr):
                pe.wait_ge(pg_free, pr * 2 + G_MLA)
                token_tile(pr * 2 + (T_MLA + 1), (T_MLA + 1) % 2, 1, LB, 2 * (NOPE + VD), 0, a2, True, True)

            project_q(0)
            project_kv(0)
            for pr, i, u in pairs(pe):
                nxt = not isinstance(pr, int) or pr < PAIRS - 1
                q, kv = b_q[u], b_kv[u]
                pe.wait_ge(bqk, pr * 2 + 1)
                for hh in range(2):
                    for tt in range(2):
                        pe.matmul(xo[:, 0, hh * T + tt * P:hh * T + (tt + 1) * P],
                                  q[:, tt, hh * QKD:hh * QKD + NOPE], ident[:], start=True, stop=True)
                for tt in range(2):
                    ins = pe.matmul(xo[:, 1, tt * P:(tt + 1) * P], b_qp[:, tt].rearrange("p h n -> p (h n)"), ident[:],
                                    start=True, stop=True)
                ins.then_inc(tq_ready, 1)
                pe.wait_ge(bqk, pr * 2 + 2)
                pe.wait_ge(o_hi, pr + O_MLA)
                for hh in range(2):
                    for tt in range(2):
                        pe.matmul(x3[:, hh * T + tt * P:hh * T + (tt + 1) * P],
                                  kv[:, tt, hh * 256:hh * 256 + NOPE], ident[:], start=True, stop=True)
                for tt in range(2):
                    ins = pe.matmul(xo[:, 1, T + tt * P:T + (tt + 1) * P], b_kp[:, tt].rearrange("p h n -> p (h n)"),
                                    ident[:], start=True, stop=True)
                ins.then_inc(tk_ready, 1)
                if nxt:
                    project_q(pr + 1)
                pe.wait_ge(te_act, pr + 1)
                pe.wait_ge(te_dve, pr + 1)
                for hh in range(2):
                    dst = (xo[:, 0, :], x3[:, :])[hh]
                    r0 = hh * ROPE
                    for qt, (c0, n) in enumerate(((0, P), (P, T))):
                        pe.matmul(dst[:, c0:c0 + n], b_qt[:, hh, qt * P:(qt + 1) * P], b_kt[:, hh, 0:n],
                                  start=True, stop=False)
                        ins = pe.matmul(dst[:, c0:c0 + n], b_rt[r0:r0 + ROPE, 0, qt * P:(qt + 1) * P],
                                        b_rt[r0:r0 + ROPE, 1, 0:n], start=False, stop=True)
                    ins.then_inc(s_ready, 1)
                if nxt:
                    project_kv(pr + 1)
                    reduce_unit(pr + U_PAIR, S_LQ + 1)
                for hh in range(2):
                    pe.wait_ge(p_ready, pr * 2 + hh + 1)
                    for b in range(3):
                        ins = pe.matmul(xo[:, 1 - hh, b * P:(b + 1) * P], b_p[:, hh, b * P:(b + 1) * P], ident[:],
                                        start=True, stop=True)
                    ins.then_inc(pt_ready, 1)
                for hh in range(2):
                    pe.wait_ge(pt_evac, pr * 2 + hh + 1)
                    v = [kv[:, kt, hh * 256 + NOPE:hh * 256 + NOPE + VD] for kt in range(2)]
                    pe.matmul(x3[:, hh * T:(hh + 1) * T], v[0], b_pt[:, hh, 0:T], start=True, stop=False,
                              skip_group_check=True)
                    ins = pe.matmul(x3[:, hh * T + P:(hh + 1) * T], v[1], b_pt[:, hh, T:3 * P], start=False,
                                    stop=True, skip_group_check=True)
                ins.then_inc(ob_ready, 1)
            product(T_WOB, G_WOB, 2, 0, h2, 4, O_MLA, 2, U_WOB, S_LQ + 1)
            sumsq(E_NF1, 8, U_FFN1, S_NF1)
            ffn(1)
            pe.wait_ge(pg_free, G_END)
            for g in range(8):
                if g >= 4:
                    pe.wait_ge(y_ev, g - 3)
                for b in range(4):
                    ins = pe.matmul(y_bank(g)[:, b * P:(b + 1) * P],
                                    xt[:, 4 * (g % 4) + b, (g // 4) * P:(g // 4 + 1) * P], ident[:], start=True, stop=True)
                ins.then_inc(y_tr, 1)


_INS = ["x", "c", "positions", "ada_w", "ada_b", "norm_mix", "norm_ffn", "gla_w_in", "gla_w_alpha", "gla_b_alpha",
        "gla_onorm", "gla_w_out", "mla_w_dq", "mla_q_lat_norm", "mla_w_uq", "mla_q_norm", "mla_w_out", "kv_ada_w",
        "kv_ada_b", "kv_norm", "kv_w_dkv", "kv_lat_norm", "kv_w_ukv", "kv_k_norm", "ffn_w_gu", "ffn_w_down"]


def kernel(**inputs):
    import concourse.bacc as bacc
    from concourse.bass_utils import run_bass_kernel_spmd

    nc = bacc.Bacc("TRN2", target_bir_lowering=False, num_devices=1)
    arrays, args = {}, []
    for name in _INS:
        a = np.ascontiguousarray(inputs[name])
        arrays["in_" + name] = a
        args.append(nc.dram_tensor("in_" + name, a.shape, mybir.dt.from_np(a.dtype), kind="ExternalInput").ap())
    args.append(nc.dram_tensor("out_0", (1, T, D), F32, kind="ExternalOutput").ap())
    trunk(nc, *args)
    r = run_bass_kernel_spmd(nc, [arrays], core_ids=[0])
    return r.results[0]["out_0"]
```

```python
from contextlib import ExitStack

import numpy as np

import concourse.bass as bass
from concourse import mybir

F32 = mybir.dt.float32
F32R = mybir.dt.float32r
I32 = mybir.dt.int32
ALU = mybir.AluOpType
ACT = mybir.ActivationFunctionType
AX = mybir.AxisListType

P = 128
D = 2048
T = 256
NB = D // P
KQ = NB // 4
HEADS_A = 4
DK, DV = D // 2 // HEADS_A, D // HEADS_A
QK_A = HEADS_A * DK
RANK = 16
TAU = 16.0
CH = 64
NCH = T // CH
HEADS_B = 16
NOPE, ROPE, VD = 128, 64, 128
QKD = NOPE + ROPE
HALF = ROPE // 2
PAIRS = HEADS_B // 2
LORA = 512
LB = LORA // P
FF = 5632
FFC = (8, 8, 6)
EPS = 1e-6
THETA = 10000.0
GW = 512
NEG = -1e30
TWO_PI = 2.0 * np.pi
PI_A = 6.28125
PI_B = 0.00193500518798828125
PI_C = float(TWO_PI - PI_A - PI_B)
MAGIC = 12582912.0

MOD0, MODKV, MOD1 = 0, 24, 32
C_NMIX, C_NFFN, C_KVN, C_ON, C_BA, C_QL, C_KL, C_QN, C_KN, C_QT, C_KT, C_END = \
    224, 256, 288, 304, 308, 316, 320, 324, 325, 326, 327, 328

T_LOW, T_GLA, T_WOA, T_FFN0 = 0, 1, 49, 65
T_DKV, T_KPE, T_DQ, T_MLA, T_WOB, T_FFN1, T_END = 201, 205, 206, 210, 226, 242, 378
G_LOW, G_GLA, G_WOA, G_FFN0, G_DKV, G_KPE, G_DQ, G_MLA, G_WOB, G_FFN1, G_END = 0, 1, 13, 17, 51, 52, 53, 54, 70, 74, 108
O_N0, O_GLA, O_NF0, O_FFN0, O_NKV, O_NMX, O_LKV, O_LQ, O_MLA, O_NF1, O_FFN1 = 0, 8, 16, 24, 46, 54, 62, 64, 66, 74, 82
E_N0, E_GLA, E_NF0, E_NKV, E_LKV, E_LQ, E_NF1 = 0, 8, 16, 24, 32, 34, 36
S_N0, S_GLA, S_NF0, S_NKV, S_LKV, S_LQ, S_NF1 = 0, 1, 5, 6, 7, 8, 9
FMA = {O_N0: 0, O_NF0: 8, O_NKV: 16, O_NMX: 24, O_LKV: 32, O_LQ: 34, O_NF1: 36}
U_GLA, U_WOA, U_FFN0, U_DKV, U_PAIR, U_WOB, U_FFN1, U_END = 8, 16, 20, 40, 41, 48, 52, 56


def whole(tiles):
    return tiles * 2


def tile_shape(t0, k, per):
    t = t0 + k
    if t == T_KPE:
        return NB, ROPE
    if T_MLA <= t < T_WOB and t % 2 == T_MLA % 2:
        return LB, 2 * QKD
    return 4, GW


def halves(k):
    return (0, (k + 1) // 2), ((k + 1) // 2, k)


def steps(eng, n, peel=False):
    m = n - 1 if peel else n
    if m > 1:
        with eng.Fori(0, m) as i:
            yield i
    else:
        yield from range(m)
    if peel:
        yield n - 1


def pairs(eng):
    with eng.Fori(0, PAIRS // 2 - 1) as i:
        for u in range(2):
            yield i * 2 + u, i, u
    for u in range(2):
        yield PAIRS - 2 + u, PAIRS // 2 - 1, u


def a_of(rate, u, j):
    if rate == 2:
        return u, j
    if rate == 1 and j % 2 == 0:
        return 0, 2 * u + j // 2
    return None


def a_of_head(pos):
    return None if pos % 3 == 2 else (pos // 6, pos % 6 - pos % 6 // 3)


def ffn_plan(layer):
    t, g, o, u = (T_FFN0, G_FFN0, O_FFN0, U_FFN0) if layer == 0 else (T_FFN1, G_FFN1, O_FFN1, U_FFN1)
    rates = ((1, 1, 1, 1, 2, 1), (1, 0, 0, 0, 0, 0))[layer]
    out, b = [], 0
    for c, n in enumerate(FFC):
        a = rates[2 * c]
        out.append(("up", t, g, o, n // 2, u, a, c, b))
        t, g, o, u = t + 4 * n, g + n, o + n, u + a * (n // 2)
        a = rates[2 * c + 1]
        out.append(("down", t, g, o - n, 2, u, a, c, b))
        t, g, u = t + 16, g + 4, u + a * 2
        b += 2 * n
    return out


def trunk(nc, x, c, positions, ada_w, ada_b, norm_mix, norm_ffn, gla_w_in, gla_w_alpha, gla_b_alpha, gla_onorm,
          gla_w_out, mla_w_dq, mla_q_lat_norm, mla_w_uq, mla_q_norm, mla_w_out, kv_ada_w, kv_ada_b, kv_norm,
          kv_w_dkv, kv_lat_norm, kv_w_ukv, kv_k_norm, ffn_w_gu, ffn_w_down, out):
    with ExitStack() as ctx:
        def sb(name, shape, dt=F32):
            return ctx.enter_context(nc.sbuf_tensor(name, shape, dt))

        def ps(name, shape):
            return ctx.enter_context(nc.psum_tensor(name, shape, F32))

        def sem(name):
            return ctx.enter_context(nc.semaphore(name))

        raw = sb("raw", [P, 4, 2048])
        whi = sb("whi", [P, 2, 2048], F32R)
        wlo = sb("wlo", [P, 2, 2048], F32R)
        adar = sb("adar", [P, 2, 4, GW])
        acc = sb("acc", [P, 2, GW])
        xt = sb("xt", [P, NB, T])
        hhi = sb("hhi", [P, NB, T], F32R)
        hlo = sb("hlo", [P, NB, T], F32R)
        ahi = sb("ahi", [P, NB, T], F32R)
        alo = sb("alo", [P, NB, T], F32R)
        work = sb("work", [P, 6912])
        cols = sb("cols", [P, C_END])
        mods = sb("mods", [P, 224])
        avec = sb("avec", [P, 2, NB])
        scol = sb("scol", [P, NB])
        ones = sb("ones", [P, P])
        ident = sb("ident", [P, P])
        rstd = sb("rstd", [P, T])
        sq = sb("sq", [P, 2, 2 * T])
        ht = sb("ht", [P, 2, 2 * T])
        mask = sb("mask", [P, 3, P])
        csin = sb("csin", [P, 2, 2, HALF])
        kpe = sb("kpe", [P, 2, ROPE])
        nrow = sb("nrow", [P, 64])
        posi = sb("posi", [P, 2], I32)
        cst = sb("cst", [P, 4])
        invf = sb("invf", [P, HALF])
        EPSC, ONEC, HPIC = cst[:, 0:1], cst[:, 1:2], cst[:, 2:3]
        COS, SIN = csin[:, 0], csin[:, 1]

        def wview(lo, hi, **dims):
            pat = {1: "p (a n) -> p a n", 2: "p (a b n) -> p a b n"}[len(dims)]
            return work[:, lo:hi].rearrange(pat, **dims)

        xio = wview(0, 4096, a=2)
        vrow = wview(4096, 4480, a=3)
        crow = work[0:NB, 4480:4608]
        a_qk = wview(0, 1024, a=4)
        a_v = wview(1024, 2048, a=2)
        a_sg = wview(2048, 3072, a=4)
        a_c = wview(3072, 3584, a=2)
        a_e = wview(3584, 4864, a=2)
        a_qd = wview(4864, 5376, a=2)
        a_att = wview(5376, 5888, a=2)
        a_l = a_e[:, :, 0:T]
        a_m = a_e[:, :, T:2 * T]
        alrt = work[0:RANK, 5920:6176]
        wah = work[0:RANK, 6176:6432]
        a_cs = nrow[:, 0:16].rearrange("p (s b n) -> p s b n", s=2, b=2)
        KOFF = [0, 64, 192, 384]
        f_s = wview(0, 1024, a=2)
        f_a = wview(1024, 2048, a=2)
        b_q = [v.rearrange("p (a n) -> p a n", a=2)
               for v in (work[:, 0:768], work[:, 6144:6912])]
        b_kv = [v.rearrange("p (a n) -> p a n", a=2)
                for v in (work[:, 768:1792], sq[:].rearrange("p a n -> p (a n)"))]
        b_qt = wview(1792, 2304, a=2)
        b_kt = wview(2304, 2816, a=2)
        b_rt = wview(2816, 3328, a=2)
        b_kp = wview(3328, 3584, a=2, b=2)
        b_qp = wview(5888, 6144, a=2, b=2)
        b_p = wview(3584, 4352, a=2)
        b_pt = wview(4352, 5120, a=2)
        b_sq = work[:, 5120:5888]
        b_o = ht[:, 1, :]
        latk = wview(0, 1024, a=4)
        latq = wview(1024, 2048, a=4)
        ang = wview(2048, 2112, a=2)
        angk = wview(2112, 2176, a=2)
        anga = wview(2176, 2240, a=2)
        posf = work[:, 2272:2274]
        kpf = work[0:ROPE, 2688:2944]
        krw = wview(2304, 2432, a=2)
        krt = wview(2432, 2688, a=4, b=2)
        b_st = nrow[:, 16:24]
        b_mx, b_sm = nrow[:, 24:28], nrow[:, 28:32]
        kss = nrow[:, 32:34]

        pg = ps("pg", [P, 2, 4, T])
        pt = pg[:, :, :, :].rearrange("p s (t b) n -> p s t (b n)", t=2)
        xo = ps("xo", [P, 2, 512])
        x2 = ps("x2", [P, 512])
        x3 = ps("x3", [P, 512])

        raw_ld = [sem(f"raw_ld{i}") for i in range(4)]
        ada_ld = [sem(f"ada_ld{i}") for i in range(4)]
        c_ld, par_ld, x_ld, pos_ld, wah_ld, out_st = sem("c_ld"), sem("par_ld"), sem("x_ld"), sem("pos_ld"), sem("wah_ld"), sem("out_st")
        hi_done, lo_done, mm_done, pg_free = sem("hi_done"), sem("lo_done"), sem("mm_done"), sem("pg_free")
        ada_used, ada_sum, modp_ready, mods_done = sem("ada_used"), sem("ada_sum"), sem("modp_ready"), sem("mods_done")
        cst_done, dcst_done = sem("cst_done"), sem("dcst_done")
        c_tr, tr_ready, tr_evac, s_silu = sem("c_tr"), sem("tr_ready"), sem("tr_evac"), sem("s_silu")
        sq_done, ssq_mm, std_done, rstd_done = sem("sq_done"), sem("ssq_mm"), sem("std_done"), sem("rstd_done")
        a_done, n_mul, n_fma, o_hi, o_lo = sem("a_done"), sem("n_mul"), sem("n_fma"), sem("o_hi"), sem("o_lo")
        oa_norm, kp_tr, kp_in = sem("oa_norm"), sem("kp_tr"), sem("kp_in")
        la_ready, la_act, la_used, la_dve, kexp, kq_ready = (sem("la_ready"), sem("la_act"), sem("la_used"),
                                                             sem("la_dve"), sem("kexp"), sem("kq_ready"))
        att_ready, att_evac, att_msk, sg_act, oa_ready, og_mul = (sem("att_ready"), sem("att_evac"), sem("att_msk"),
                                                                  sem("sg_act"), sem("oa_ready"), sem("og_mul"))
        f_silu = sem("f_silu")
        rot_c, rot_a, kp_rot, kp_ss = sem("rot_c"), sem("rot_a"), sem("kp_rot"), sem("kp_ss")
        q_rot, bsq, bst, bstd, brs, bqk = sem("q_rot"), sem("bsq"), sem("bst"), sem("bstd"), sem("brs"), sem("bqk")
        tq_ready, tk_ready, te_act = sem("tq_ready"), sem("tk_ready"), sem("te_act")
        s_ready, s_mx, s_exp, s_dve, s_rcp = sem("s_ready"), sem("s_mx"), sem("s_exp"), sem("s_dve"), sem("s_rcp")
        p_ready, pt_ready, pt_evac, ob_ready, ob_act = (sem("p_ready"), sem("pt_ready"), sem("pt_evac"),
                                                        sem("ob_ready"), sem("ob_act"))
        y_tr, y_ev = sem("y_tr"), sem("y_ev")

        def rows(w):
            return w.rearrange("(k p) n -> p k n", p=P)

        w_in, w_outa = rows(gla_w_in[0]), rows(gla_w_out[0])
        w_dq, w_uq, w_outb = rows(mla_w_dq[0]), rows(mla_w_uq[0]), rows(mla_w_out[0])
        w_dkv, w_ukv = rows(kv_w_dkv), rows(kv_w_ukv)
        w_gu = [rows(ffn_w_gu[i]) for i in range(2)]
        w_dn = [rows(ffn_w_down[i]) for i in range(2)]
        w_ada = {0: rows(ada_w[0]), 1: rows(kv_ada_w), 2: rows(ada_w[1])}

        def ada_src(unit0, rel):
            m, base = (0, MOD0) if unit0 < MODKV else (1, MODKV) if unit0 < MOD1 else (2, MOD1)
            return w_ada[m], (unit0 - base + rel) * GW

        def tile(buf, s, k, n):
            return buf[:, s, 0:k * n].rearrange("p (k n) -> p k n", k=k)

        def a_slot(j):
            return adar[:, j] if j < 2 else tile(raw, j, 4, GW)

        def acc_start(unit):
            return acc if unit % 2 == 0 else ht

        def h_slot(j):
            return (ht, sq)[j % 4 // 2][:, j % 2, :].rearrange("p (b n) -> p b n", b=2)

        def y_bank(g):
            return pt[:, g % 4 // 2, g % 2]

        def lines(v):
            return v.rearrange("(a n) -> a n", n=P)

        rowsets = [lines(ada_b[0]), lines(kv_ada_b), lines(ada_b[1]), lines(norm_mix[0]),
                   lines(norm_mix[1]), lines(norm_ffn[0]), lines(norm_ffn[1]), lines(kv_norm), lines(gla_onorm[0]),
                   lines(gla_b_alpha[0]), lines(mla_q_lat_norm[0]), lines(kv_lat_norm), lines(mla_q_norm[0][0:NOPE]),
                   lines(kv_k_norm[0:NOPE])]
        pieces, r = [], 0
        for v in rowsets:
            k = 0
            while k < v.shape[0]:
                m = min(v.shape[0] - k, P - r % P)
                pieces.append((v, k, m, r))
                k, r = k + m, r + m
        assert r == C_QT
        par_dmas = len(pieces) + 4

        block = ctx.enter_context(nc.Block())

        @block.sync
        def _(sp):
            def g_tile(t, s, pieces, first=False):
                if not first:
                    sp.wait_ge(lo_done, whole(t - 3))
                for dst, src in pieces:
                    sp.dma_start(dst, src).then_inc(raw_ld[s], 16)

            def by_k(s, w, k0, k, n, col):
                d = tile(raw, s, k, n)
                h = (k + 1) // 2
                return [(d[:, 0:h], w[:, k0:k0 + h, bass.ds(col, n)]),
                        (d[:, h:k], w[:, k0 + h:k0 + k, bass.ds(col, n)])]

            def by_half(s, w, k0, col_a, col_b):
                d = tile(raw, s, 4, GW)
                return [(d[:, :, 0:256], w[:, k0:k0 + 4, bass.ds(col_a, 256)]),
                        (d[:, :, 256:512], w[:, k0:k0 + 4, bass.ds(col_b, 256)])]

            def a_tile_start(unit, j):
                w, col = ada_src(0, unit)
                if unit:
                    sp.wait_ge(ada_used, unit * 16 + 4 * j - 12)
                for h in range(2):
                    k0 = 4 * j + 2 * h
                    sp.dma_start(a_slot(j)[:, 2 * h:2 * h + 2, :], w[:, k0:k0 + 2, col:col + GW]) \
                        .then_inc(ada_ld[j], 16)

            def a_tile(unit, src, j):
                w, col = src
                sp.wait_ge(ada_used, (unit * 4 + j - 1) * 4)
                for h in range(2):
                    k0 = 4 * j + 2 * h
                    sp.dma_start(adar[:, j % 2, 2 * h:2 * h + 2, :], w[:, k0:k0 + 2, bass.ds(col, GW)]) \
                        .then_inc(ada_ld[j % 2], 16)

            for u in range(8):
                for j in range(4):
                    a_tile_start(u, j)
                if u == 0:
                    sp.dma_start(xio, x[0].rearrange("(t p) n -> p t n", p=P)).then_inc(x_ld, 16)
                    g_tile(0, 0, by_k(0, w_in, 0, NB, RANK, 2 * QK_A + 2 * D), first=True)
            def a_with(u0, i, rate, hit):
                if hit is not None:
                    rel = i * rate + hit[0]
                    a_tile(rel + u0, ada_src(u0, rel), hit[1])

            def a_steps(n, rate):
                return range(n) if rate == 2 else steps(sp, n)

            def a_after(u0, i, n, rate, u, j):
                pos = 4 * u + j
                if pos:
                    a_with(u0, i, rate, a_of(rate, (pos - 1) // 4, (pos - 1) % 4))
                elif rate == 2 and i:
                    a_with(u0, i - 1, rate, a_of(rate, 1, 3))
                if pos == 7 and rate == 2 and i == n - 1:
                    a_with(u0, i, rate, a_of(rate, u, j))

            def a_after_head(h, pos):
                if pos:
                    a_with(U_GLA, h, 2, a_of_head(pos - 1))

            for n in range(3):
                if n:
                    sp.wait_ge(ada_used, 8 * 16 - 8 + 4 * n)
                g_tile(1 + n, 1 + n, by_half(1 + n, w_in, 4 * n, 0, QK_A), first=True)
                a_after_head(0, n)
            g_tile(4, 0, by_half(0, w_in, 12, 0, QK_A))
            a_after_head(0, 3)
            for g in (1, 2):
                for j in range(4):
                    t = 1 + 4 * g + j
                    g_tile(t, t % 4, by_k(t % 4, w_in, 4 * j, 4, GW, 2 * QK_A + (g - 1) * D))
                    a_after_head(0, 4 * g + j)
            with sp.Fori(1, HEADS_A) as h:
                for g in range(3):
                    for j in range(4):
                        t, s = h * 12 + (1 + 4 * g + j), (1 + j) % 4
                        if g == 0:
                            g_tile(t, s, by_half(s, w_in, 4 * j, h * DK, h * DK + QK_A))
                        else:
                            g_tile(t, s, by_k(s, w_in, 4 * j, 4, GW, h * DV + (2 * QK_A + (g - 1) * D)))
                        a_after_head(h, 4 * g + j)

            def square(w, t0, n, u0, rate):
                for i in a_steps(n, rate):
                    for u in range(2):
                        for j in range(4):
                            s = (t0 + j) % 4
                            g_tile(i * 8 + (t0 + 4 * u + j), s, by_k(s, w, 4 * j, 4, GW, (i * 2 + u) * GW))
                            a_after(u0, i, n, rate, u, j)

            square(w_outa, T_WOA, 2, U_WOA, 2)

            def ffn(layer):
                for kind, t0, g0, o0, n, u0, rate, ch, b0 in ffn_plan(layer):
                    for i in a_steps(n, rate):
                        for u in range(2):
                            for j in range(4):
                                s = (t0 + j) % 4
                                t = i * 8 + (t0 + 4 * u + j)
                                if kind == "up":
                                    col = (i * 2 + u) * 256 + b0 * P
                                    g_tile(t, s, by_half(s, w_gu[layer], 4 * j, col, col + FF))
                                else:
                                    k = FFC[ch] // 2
                                    g_tile(t, s, by_k(s, w_dn[layer], b0 + k * j, k, GW, (i * 2 + u) * GW))
                                a_after(u0, i, n, rate, u, j)

            ffn(0)
            for j in range(4):
                s = (T_DKV + j) % 4
                g_tile(T_DKV + j, s, by_k(s, w_dkv, 4 * j, 4, GW, 0))
            s = T_KPE % 4
            g_tile(T_KPE, s, by_k(s, w_dkv, 0, NB, ROPE, LORA))
            for j in range(4):
                s = (T_DQ + j) % 4
                g_tile(T_DQ + j, s, by_k(s, w_dq, 4 * j, 4, GW, 0))
                if j:
                    a_tile(U_DKV, ada_src(U_DKV, 0), j - 1)
            a_tile(U_DKV, ada_src(U_DKV, 0), 3)
            def mla_tile(i, k):
                s = (T_MLA + k) % 4
                w, n = ((w_uq, 2 * QKD), (w_ukv, 2 * (NOPE + VD)))[k % 2]
                g_tile(i * 4 + (T_MLA + k), s, by_k(s, w, 0, LB, n, (i * 2 + k // 2) * n))

            for k in range(4):
                mla_tile(0, k)
            for pr, i, u in pairs(sp):
                for m in range(2):
                    if not isinstance(pr, int):
                        mla_tile(i, 4 + 2 * u + m)
                    if not isinstance(pr, int) or pr < PAIRS - 1:
                        for j in (2 * m, 2 * m + 1):
                            a_tile(pr + U_PAIR, ada_src(U_PAIR, pr), j)
            square(w_outb, T_WOB, 2, U_WOB, 2)
            ffn(1)
            sp.wait_ge(y_ev, 8)
            sp.dma_start(out[0].rearrange("(t p) n -> p t n", p=P), xio).then_inc(out_st, 16)
            sp.wait_ge(out_st, 16)

        @block.gpsimd
        def _(pool):
            pool.memset(ident[:], 0.0).then_inc(cst_done, 1)
            pool.wait_ge(cst_done, 1)
            pool.affine_select(out=ident[:], in_=ident[:], compare_op=ALU.not_equal, fill=1.0, base=0,
                               pattern=[[-1, P]], channel_multiplier=1).then_inc(cst_done, 1)
            pool.memset(mask[:], 0.0).then_inc(cst_done, 1)
            pool.memset(a_att, 0.0).then_inc(cst_done, 1)
            for f in range(HALF):
                ins = pool.memset(invf[:, f:f + 1], float(np.float32(THETA) ** np.float32(-np.float32(f) / HALF)))
            ins.then_inc(cst_done, 1)
            pool.wait_ge(cst_done, 5)
            for b in (0, 2):
                ins = pool.affine_select(out=mask[:, b, :], in_=mask[:, b, :], compare_op=ALU.is_ge, fill=NEG, base=0,
                                         pattern=[[-1, P]], channel_multiplier=1)
            ins.then_inc(cst_done, 1)

            def lo_part(o, dst, src, hi):
                pool.wait_ge(o_hi, o + 1)
                pool.tensor_tensor(dst, src, hi.bitcast(F32), ALU.subtract).then_inc(o_lo, 1)

            def norm_lo(o0, n, hi, lo, b0=0):
                for j in range(n):
                    b = b0 + 2 * j
                    lo_part(o0 + j, lo[:, b:b + 2, :], h_slot(j), hi[:, b:b + 2, :])

            pool.dma_start(wah, gla_w_alpha[0][:, 0:DK]).then_inc(wah_ld, 16)
            norm_lo(O_N0, 8, hhi, hlo)

            def gla_mask_and_lo(h):
                pool.wait_ge(tr_evac, 5)
                pool.wait_ge(att_evac, h + 1)
                pool.affine_select(out=a_att[:, 0, 0:P], in_=a_att[:, 0, 0:P], compare_op=ALU.is_ge, fill=0.0, base=0,
                                   pattern=[[1, P]], channel_multiplier=-1)
                pool.affine_select(out=a_att[:, 1, P:T], in_=a_att[:, 1, P:T], compare_op=ALU.is_ge, fill=0.0, base=0,
                                   pattern=[[1, P]], channel_multiplier=-1).then_inc(att_msk, 1)
                for e in range(2):
                    lo_part(h * 2 + (O_GLA + e), alo[:, bass.ds(h * 4 + 2 * e, 2), :],
                            ht[:, e, :].rearrange("p (b n) -> p b n", b=2), ahi[:, bass.ds(h * 4 + 2 * e, 2), :])

            with pool.Fori(0, HEADS_A - 1) as h:
                pool.wait_ge(la_ready, h + 1)
                pool.dma_start(wah, gla_w_alpha[0][:, bass.ds(h * DK + DK, DK)]).then_inc(wah_ld, 16)
                gla_mask_and_lo(h)
            gla_mask_and_lo(HEADS_A - 1)

            def ffn(layer):
                for kind, t0, g0, o0, n, u0, rate, ch, b0 in ffn_plan(layer):
                    if kind == "up":
                        for i in steps(pool, n):
                            for u in range(2):
                                lo_part(i * 2 + (o0 + u), alo[:, bass.ds(i * 4 + 2 * u, 2), :],
                                        f_a[:, u, :].rearrange("p (b n) -> p b n", b=2),
                                        ahi[:, bass.ds(i * 4 + 2 * u, 2), :])

            norm_lo(O_NF0, 8, hhi, hlo)
            ffn(0)
            norm_lo(O_NKV, 8, ahi, alo)
            norm_lo(O_NMX, 8, hhi, hlo)

            def rotate(r1, r2, cos, sin, tmp, done, base):
                for k, (a, b) in enumerate(((r1, cos), (r2, sin), (r2, cos), (r1, sin))):
                    ins = pool.tensor_tensor(tmp[k], a, b, ALU.mult)
                ins.then_inc(done, 1)
                pool.wait_ge(done, base + 1)
                pool.tensor_tensor(r1, tmp[0], tmp[1], ALU.subtract)
                pool.tensor_tensor(r2, tmp[2], tmp[3], ALU.add).then_inc(done, 1)

            pool.wait_ge(kp_in, 1)
            pool.wait_ge(rot_a, 3)
            rotate(kpe[:, :, 0:HALF], kpe[:, :, HALF:ROPE], COS, SIN, [krt[:, k] for k in range(4)], kp_rot, 0)
            norm_lo(O_LKV, 2, ahi, alo, 0)
            norm_lo(O_LQ, 2, ahi, alo, LB)

            def rotate_q(pr, par):
                pool.wait_ge(pg_free, pr * 2 + (G_MLA + 1))
                q4 = b_q[par].rearrange("p t (h n) -> p t h n", h=2)
                cs = [z[:, :, None, :].broadcast_to([P, 2, 2, HALF]) for z in (COS, SIN)]
                tmp = [ht[:, 0, k * 128:(k + 1) * 128].rearrange("p (t h n) -> p t h n", t=2, h=2)
                       for k in range(4)]
                rotate(q4[:, :, :, NOPE:NOPE + HALF], q4[:, :, :, NOPE + HALF:QKD], cs[0], cs[1], tmp, q_rot, pr * 2)

            pool.wait_ge(o_lo, O_MLA)
            rotate_q(0, 0)
            for pr, i, u in pairs(pool):
                if not isinstance(pr, int) or pr < PAIRS - 1:
                    pool.wait_ge(q_rot, pr * 2 + 2)
                    rotate_q(pr + 1, (u + 1) % 2)
                lo_part(pr + O_MLA, hlo[:, bass.ds(pr * 2, 2), :], b_o.rearrange("p (b n) -> p b n", b=2),
                        hhi[:, bass.ds(pr * 2, 2), :])
            norm_lo(O_NF1, 8, hhi, hlo)
            ffn(1)

        @block.scalar
        def _(act):
            def hi(t, s4, s2, n4, free=True, k=4, n=GW):
                act.wait_ge(raw_ld[s4], n4 * 32 + 32)
                for h, (a, b) in enumerate(halves(k)):
                    if free:
                        act.wait_ge(mm_done, whole(t - 2) + (h + 1))
                    act.activation(whi[:, s2, h * 1024:h * 1024 + (b - a) * n], raw[:, s4, a * n:b * n], ACT.Copy).then_inc(hi_done, 1)

            def his(t0, per, i, first, count):
                for k in range(first, first + count):
                    hi(i * per + (t0 + k), (t0 + k) % 4, (t0 + k) % 2, i * (per // 4) + (t0 + k) // 4,
                       True, *tile_shape(t0, k, per))

            act.dma_start(crow, lines(c[0])).then_inc(c_ld, 16)
            act.wait_ge(c_tr, 1)
            act.activation(scol[:], x2[:, 0:NB], ACT.Silu).then_inc(s_silu, 1)
            for t in range(2):
                act.dma_start(posi[:, t:t + 1], positions[0, t * P:(t + 1) * P].rearrange("(p a) -> p a", a=1)) \
                    .then_inc(pos_ld, 16)
            for v, k, m, r in pieces:
                act.dma_start(vrow[r % P:r % P + m, r // P, :], v[k:k + m, :]).then_inc(par_ld, 16)
            for r, v in ((C_QT, mla_q_norm[0]), (C_KT, kv_k_norm)):
                for h in range(2):
                    act.dma_start(vrow[r % P:r % P + 1, r // P, ROPE * h:ROPE * (h + 1)],
                                  v[NOPE:QKD].rearrange("(a n) -> a n", a=1)).then_inc(par_ld, 16)

            def squares(e0, src, n):
                for j in range(n):
                    if e0 + j >= 2:
                        act.wait_ge(ssq_mm, e0 + j - 1)
                    act.activation(sq[:, j % 2, :].rearrange("p (b n) -> p b n", b=2), src[:, 2 * j:2 * j + 2, :],
                                   ACT.Square).then_inc(sq_done, 1)

            def std(e, depth, sums=x2):
                act.wait_ge(ssq_mm, e)
                act.activation(rstd[:], sums[:, 0:T], ACT.Sqrt, bias=EPSC, scale=1.0 / depth).then_inc(std_done, 1)

            def norm_hi(o0, n, dst, b0=0, first=0):
                for j in range(first, n):
                    act.wait_ge(n_fma, FMA[o0] + j + 1)
                    act.activation(dst[:, b0 + 2 * j:b0 + 2 * j + 2, :], h_slot(j), ACT.Copy).then_inc(o_hi, 1)

            act.wait_ge(tr_evac, 5)
            act.wait_ge(dcst_done, 3)
            squares(E_N0, xt, 8)
            std(E_N0 + 8, D)
            hi(0, 0, 0, 0, free=False, k=NB, n=RANK)
            norm_hi(O_N0, 8, hhi)
            hi(1, 1, 1, 0, free=False)

            with act.Fori(0, HEADS_A) as h:
                his(T_GLA, 12, h, 1, 1)
                act.wait_ge(la_ready, h + 1)
                for b in range(2):
                    ins = act.activation(a_l[:, b, :], x2[:, b * T:(b + 1) * T], ACT.Identity,
                                         bias=cols[:, bass.ds(h * 2 + (C_BA + b), 1)])
                ins.then_inc(la_act, 1)
                act.wait_ge(la_act, h * 4 + 1)
                act.activation(a_m, a_l, ACT.Abs).then_inc(la_act, 1)
                act.wait_ge(la_act, h * 4 + 2)
                act.activation(a_m, a_m, ACT.Exp, scale=-1.0).then_inc(la_act, 1)
                his(T_GLA, 12, h, 2, 1)
                act.wait_ge(la_act, h * 4 + 3)
                act.activation(a_m, a_m, ACT.Ln, bias=ONEC).then_inc(la_act, 1)
                his(T_GLA, 12, h, 3, 2)
                act.wait_ge(la_dve, h * 4 + 4)
                for n in range(NCH):
                    for b in range(2):
                        act.activation(a_e[:, b, KOFF[n]:KOFF[n] + CH * (n + 1)], a_c[:, b, 0:CH * (n + 1)], ACT.Exp,
                                       bias=a_cs[:, 0, b, n:n + 1], scale=1.0 / TAU)
                        ins = act.activation(a_qd[:, b, CH * n:CH * (n + 1)], a_c[:, b, CH * n:CH * (n + 1)], ACT.Exp,
                                             bias=a_cs[:, 1, b, n:n + 1], scale=-1.0 / TAU)
                ins.then_inc(kexp, 1)
                his(T_GLA, 12, h, 5, 8)
                act.wait_ge(mm_done, whole(h * 12 + (T_GLA + 12)))
                act.activation(a_sg, pg[:, 0], ACT.Sigmoid).then_inc(sg_act, 1)
                act.wait_ge(oa_ready, h + 1)
                for e in range(2):
                    act.wait_ge(ssq_mm, h * 2 + (E_GLA + e - 1))
                    act.activation(sq[:, e, :], xo[:, e, :], ACT.Square).then_inc(sq_done, 1)
                std(h * 2 + (E_GLA + 2), DV)
                for e in range(2):
                    act.wait_ge(og_mul, h * 2 + e + 1)
                    act.activation(ahi[:, bass.ds(h * 4 + 2 * e, 2), :],
                                   ht[:, e, :].rearrange("p (b n) -> p b n", b=2), ACT.Copy).then_inc(o_hi, 1)

            def plain(t0, n):
                for i in steps(act, n):
                    his(t0, 8, i, 1, 8)

            def with_squares(t0, g0, n, e0):
                for i in steps(act, n):
                    for u in range(2):
                        his(t0 + 4 * u, 8, i, 1, 4)
                        act.wait_ge(pg_free, i * 2 + (g0 + u + 1))
                        for e in range(2):
                            act.wait_ge(ssq_mm, i * 4 + (e0 + 2 * u + e - 1))
                            act.activation(sq[:, e, :].rearrange("p (b n) -> p b n", b=2),
                                           xt[:, bass.ds(i * 8 + (4 * u + 2 * e), 2), :], ACT.Square).then_inc(sq_done, 1)

            def ffn(layer):
                last_down = T_WOA + 16 if layer == 0 else T_WOB + 16
                for kind, t0, g0, o0, n, u0, rate, ch, b0 in ffn_plan(layer):
                    if kind == "down":
                        if layer == 1 and ch == 2:
                            for i in steps(act, n, peel=True):
                                his(t0, 8, i, 1, 7 if isinstance(i, int) and i == n - 1 else 8)
                        elif ch == 2:
                            with_squares(t0, g0, n, E_NKV)
                        else:
                            plain(t0, n)
                        last_down = t0 + 16
                        continue
                    act.wait_ge(mm_done, whole(last_down))
                    for i in steps(act, n):
                        for u in range(2):
                            his(t0 + 4 * u, 8, i, 1, 4)
                            act.wait_ge(mm_done, whole(i * 8 + (t0 + 4 * u + 4)))
                            act.activation(f_s[:, u, :].rearrange("p (b n) -> p b n", b=2),
                                           pg[:, (g0 + u) % 2, 0:2], ACT.Silu).then_inc(f_silu, 1)
                            act.wait_ge(pg_free, i * 2 + (g0 + u + 1))
                            act.activation(ahi[:, bass.ds(i * 4 + 2 * u, 2), :],
                                           f_a[:, u, :].rearrange("p (b n) -> p b n", b=2), ACT.Copy).then_inc(o_hi, 1)

            with_squares(T_WOA, G_WOA, 2, E_NF0)
            std(E_NF0 + 8, D, x3)
            norm_hi(O_NF0, 8, hhi)
            ffn(0)
            std(E_NKV + 8, D, x3)
            norm_hi(O_NKV, 8, ahi)
            his(T_DKV, 4, 0, 1, 1)
            for j in range(4):
                norm_hi(O_NMX, 2 * j + 2, hhi, first=2 * j)
                his(T_DKV, 4, 0, 2 + j, 1)
            act.wait_ge(pg_free, G_DKV + 1)
            act.wait_ge(o_lo, O_NMX + 8)
            squares(E_LKV, latk, 2)
            his(T_DQ, 4, 0, 1, 1)
            act.wait_ge(rot_c, 8)
            act.activation(SIN, ang, ACT.Sin).then_inc(rot_a, 1)
            act.activation(anga, ang, ACT.Abs).then_inc(rot_a, 1)
            act.wait_ge(rot_a, 2)
            act.activation(COS, anga, ACT.Sin, bias=HPIC, scale=-1.0).then_inc(rot_a, 1)
            his(T_DQ, 4, 0, 2, 1)
            std(E_LKV + 2, LORA)
            norm_hi(O_LKV, 2, ahi, 0)
            his(T_DQ, 4, 0, 3, 2)
            act.wait_ge(pg_free, G_DQ + 1)
            squares(E_LQ, latq, 2)
            std(E_LQ + 2, LORA)
            norm_hi(O_LQ, 2, ahi, LB)

            def square_q(pr, par):
                act.wait_ge(q_rot, pr * 2 + 2)
                act.activation(b_sq, b_q[par].rearrange("p t n -> p (t n)"), ACT.Square).then_inc(bsq, 1)

            def square_k(pr, par):
                act.wait_ge(pg_free, pr * 2 + (G_MLA + 2))
                act.wait_ge(bst, pr * 3 + 1)
                act.activation(b_sq[:, 0:512].rearrange("p (t h n) -> p t h n", t=2, h=2),
                               b_kv[par].rearrange("p t (h n) -> p t h n", h=2)[:, :, :, 0:NOPE], ACT.Square) \
                    .then_inc(bsq, 1)
                act.wait_ge(bst, pr * 3 + 3)
                act.activation(b_st, b_st, ACT.Sqrt, bias=EPSC, scale=1.0 / QKD).then_inc(bstd, 1)

            his(T_MLA, 4, 0, 1, 2)
            act.wait_ge(o_lo, O_MLA)
            square_q(0, 0)
            square_k(0, 0)
            his(T_MLA, 4, 0, 3, 1)
            for pr, i, u in pairs(act):
                nxt = not isinstance(pr, int) or pr < PAIRS - 1
                act.wait_ge(tq_ready, pr + 1)
                act.activation(b_qt.rearrange("p h n -> p (h n)"), xo[:, 0, :], ACT.Copy, scale=cols[:, C_QN:C_QN + 1])
                act.wait_ge(tk_ready, pr + 1)
                act.activation(b_kt.rearrange("p h n -> p (h n)"), x3[:], ACT.Copy, scale=cols[:, C_KN:C_KN + 1])
                act.activation(b_rt[:, 0, :], xo[:, 1, 0:T], ACT.Copy, scale=cols[:, C_QT:C_QT + 1])
                act.activation(b_rt[:, 1, :], xo[:, 1, T:2 * T], ACT.Copy, scale=cols[:, C_KT:C_KT + 1]) \
                    .then_inc(te_act, 1)
                if not isinstance(pr, int):
                    his(T_MLA + 2 * u, 4, i, 4, 1)
                elif not nxt:
                    his(T_WOB, 4, 0, 0, 1)
                if nxt:
                    square_q(pr + 1, (u + 1) % 2)
                for h in range(2):
                    act.wait_ge(s_mx, pr * 2 + h + 1)
                    for q, (a, b) in enumerate(((0, P), (P, 3 * P))):
                        ins = act.activation(b_p[:, h, a:b], b_p[:, h, a:b], ACT.Exp,
                                             bias=b_mx[:, 2 * h + q:2 * h + q + 1],
                                             accum_out=b_sm[:, 2 * h + q:2 * h + q + 1])
                    ins.then_inc(s_exp, 1)
                for h in range(2):
                    act.wait_ge(s_rcp, pr * 2 + h + 1)
                    for q, (a, b) in enumerate(((0, P), (P, 3 * P))):
                        ins = act.activation(b_p[:, h, a:b], b_p[:, h, a:b], ACT.Copy,
                                             scale=b_sm[:, 2 * h + q:2 * h + q + 1])
                    ins.then_inc(p_ready, 1)
                for h in range(2):
                    act.wait_ge(pt_ready, pr * 2 + h + 1)
                    act.activation(b_pt[:, h, :], xo[:, 1 - h, 0:3 * P], ACT.Copy).then_inc(pt_evac, 1)
                if nxt:
                    square_k(pr + 1, (u + 1) % 2)
                act.wait_ge(ob_ready, pr + 1)
                act.wait_ge(o_lo, pr + O_MLA)
                act.activation(b_o, x3[:], ACT.Copy).then_inc(ob_act, 1)
                act.wait_ge(ob_act, pr + 1)
                act.activation(hhi[:, bass.ds(pr * 2, 2), :], b_o.rearrange("p (b n) -> p b n", b=2), ACT.Copy) \
                    .then_inc(o_hi, 1)
                if not isinstance(pr, int):
                    his(T_MLA + 2 * u, 4, i, 5, 1)
            with_squares(T_WOB, G_WOB, 2, E_NF1)
            std(E_NF1 + 8, D, x3)
            norm_hi(O_NF1, 8, hhi)
            ffn(1)

        @block.vector
        def _(dve):
            def lo(t, s4, s2, k=4, n=GW):
                for h, (a, b) in enumerate(halves(k)):
                    dve.wait_ge(hi_done, whole(t) + (h + 1))
                    c0, c1 = h * 1024, h * 1024 + (b - a) * n
                    dve.tensor_tensor(wlo[:, s2, c0:c1], raw[:, s4, a * n:b * n], whi[:, s2, c0:c1].bitcast(F32),
                                      ALU.subtract).then_inc(lo_done, 1)

            def ada(unit, j, start=False):
                sums = acc_start(unit) if start else acc
                if start:
                    buf = a_slot(j)
                    dve.wait_ge(ada_ld[j], unit * 32 + 32)
                else:
                    buf = adar[:, j % 2]
                    dve.wait_ge(ada_ld[j % 2], (unit * 2 + j // 2 - 8) * 32 + 32)
                for q in range(4):
                    k = 4 * j + q
                    if k < 2:
                        if k == 0 and not (start and unit < 2):
                            dve.wait_ge(modp_ready, unit - 1 if start else unit)
                        dve.tensor_scalar(sums[:, k, :], buf[:, q, :], scol[:, k:k + 1], None, ALU.mult) \
                            .then_inc(ada_used, 1)
                    else:
                        dve.wait_ge(ada_used, unit * 16 + (k - 1))
                        dve.scalar_tensor_tensor(out=sums[:, k % 2, :], in0=buf[:, q, :], scalar=scol[:, k:k + 1],
                                                 in1=sums[:, k % 2, :], op0=ALU.mult, op1=ALU.add) \
                            .then_inc(ada_used, 1)
                if j == 3:
                    dve.wait_ge(ada_used, unit * 16 + 16)
                    dve.tensor_tensor(sums[:, 0, :], sums[:, 0, :], sums[:, 1, :], ALU.add).then_inc(ada_sum, 1)

            def mod(unit):
                dve.wait_ge(modp_ready, unit + 1)
                dve.tensor_tensor(mods[:, bass.ds(unit * 4, 4)], x2[:, 508:512], cols[:, bass.ds(unit * 4, 4)],
                                  ALU.add).then_inc(mods_done, 1)

            def los(t0, per, i, first, count, hits=(None,) * 4):
                for n, k in enumerate(range(first, first + count)):
                    lo(i * per + (t0 + k), (t0 + k) % 4, (t0 + k) % 2, *tile_shape(t0, k, per))
                    if hits[n] is not None:
                        ada(*hits[n])

            def a_hits(u0, i, rate, u):
                hits = [a_of(rate, u, j) for j in range(4)]
                return [hit and (i * rate + (u0 + hit[0]), hit[1]) for hit in hits]

            def mod_at(u0, i, rate, u):
                if rate == 2 or (rate == 1 and u == 1):
                    mod(i * rate + (u0 + (u if rate == 2 else 0)))

            dve.memset(ones[:], 1.0).then_inc(dcst_done, 1)
            dve.memset(cst[:, 0:1], EPS)
            dve.memset(cst[:, 1:2], 1.0)
            dve.memset(cst[:, 2:3], float(np.pi / 2)).then_inc(dcst_done, 1)
            dve.memset(nrow[:], 0.0).then_inc(dcst_done, 1)
            def gain(n, unit0, gcol):
                dve.scalar_tensor_tensor(out=avec[:, n % 2, :], in0=mods[:, 4 * unit0:4 * unit0 + NB], scalar=1.0,
                                         in1=cols[:, gcol:gcol + NB], op0=ALU.add, op1=ALU.mult).then_inc(a_done, 1)
                dve.wait_ge(a_done, n + 1)

            def recip(s):
                dve.wait_ge(std_done, s + 1)
                dve.reciprocal(rstd[:], rstd[:]).then_inc(rstd_done, 1)
                dve.wait_ge(rstd_done, s + 1)

            def norm_apply(o0, n, src, a, shift, first=0):
                for j in range(first, n):
                    o, m = o0 + j, FMA[o0] + j
                    if j >= 4:
                        dve.wait_ge(o_lo, o - 3)
                    elif j == 0 and o0:
                        dve.wait_ge(o_lo, o0)
                    v = h_slot(j)
                    dve.tensor_tensor(v, src[:, 2 * j:2 * j + 2, :], rstd[:, None, :].broadcast_to([P, 2, T]),
                                      ALU.mult).then_inc(n_mul, 1)
                    dve.wait_ge(n_mul, m + 1)
                    for b in range(2):
                        k = 2 * j + b
                        if shift is None:
                            ins = dve.tensor_scalar(v[:, b, :], v[:, b, :], a[:, k:k + 1], None, ALU.mult)
                        else:
                            ins = dve.tensor_scalar(v[:, b, :], v[:, b, :], a[:, k:k + 1], shift[:, k:k + 1],
                                                    ALU.mult, ALU.add)
                    ins.then_inc(n_fma, 1)

            dve.wait_ge(s_silu, 1)
            for j in range(4):
                ada(0, j, start=True)
            dve.wait_ge(tr_ready, 1)
            dve.tensor_copy(cols[:], x3[:, 0:C_END]).then_inc(tr_evac, 1)
            for g in range(4):
                dve.wait_ge(tr_ready, g + 2)
                dve.tensor_copy(xt[:, 4 * g:4 * g + 4, :], pg[:, g % 2]).then_inc(tr_evac, 1)
            for u in range(1, 8):
                for j in range(4):
                    ada(u, j, start=True)
                    if j == 0:
                        mod(u - 1)
            recip(S_N0)
            mod(7)
            dve.wait_ge(mods_done, 8)
            gain(0, 4, C_NMIX)
            lo(0, 0, 0, NB, RANK)
            norm_apply(O_N0, 8, xt, avec[:, 0, :], mods[:, 0:NB])
            lo(1, 1, 1)
            dve.wait_ge(mm_done, whole(1))
            dve.tensor_copy(alrt, pg[0:RANK, 1, 0, :]).then_inc(pg_free, 1)

            with dve.Fori(0, HEADS_A) as h:
                def los_head(first, count):
                    for pos in range(first, first + count):
                        hit = a_of_head(pos)
                        los(T_GLA, 12, h, pos + 1, 1, (hit and (h * 2 + (U_GLA + hit[0]), hit[1]),))

                los_head(0, 2)
                dve.wait_ge(la_act, h * 4 + 4)
                dve.tensor_scalar(a_l, a_l, -1.0, 0.0, ALU.mult, ALU.max).then_inc(la_used, 1)
                dve.wait_ge(la_used, h + 1)
                dve.tensor_tensor(a_l, a_l, a_m, ALU.add).then_inc(la_dve, 1)
                dve.wait_ge(la_dve, h * 4 + 1)
                for b in range(2):
                    dve.tensor_tensor_scan(a_c[:, b, :], ones[:, 0:1].broadcast_to([P, T]), a_l[:, b, :], 0.0, ALU.mult, ALU.add) \
                        .then_inc(la_dve, 1)
                dve.wait_ge(la_dve, h * 4 + 3)
                for s in range(2):
                    ins = dve.tensor_scalar(a_cs[:, s, :, 1:NCH], a_c[:, :, CH - 1:T - CH:CH],
                                            (-1.0 / TAU, 1.0 / TAU)[s], None, ALU.mult)
                ins.then_inc(la_dve, 1)
                los_head(2, 2)
                dve.wait_ge(mm_done, whole(h * 12 + (T_GLA + 4)))
                dve.tensor_copy(a_qk, pg[:, 0]).then_inc(pg_free, 1)
                los_head(4, 1)
                dve.wait_ge(kexp, h + 1)
                dve.wait_ge(pg_free, h * 3 + 2)
                for n in range(NCH):
                    v = a_e[:, :, KOFF[n]:KOFF[n] + CH * (n + 1)]
                    dve.tensor_tensor(v, v, a_qk[:, 2:4, 0:CH * (n + 1)], ALU.mult)
                dve.scalar_tensor_tensor(out=a_qd, in0=a_qk[:, 0:2, :], scalar=float(DK) ** -0.5, in1=a_qd,
                                         op0=ALU.mult, op1=ALU.mult).then_inc(kq_ready, 1)
                los_head(5, 1)
                mod(h * 2 + U_GLA)
                los_head(6, 2)
                dve.wait_ge(mm_done, whole(h * 12 + (T_GLA + 8)))
                dve.tensor_copy(a_v, pt[:, 1]).then_inc(pg_free, 1)
                los_head(8, 1)
                dve.wait_ge(att_ready, h + 1)
                dve.tensor_copy(a_att[0:CH, 0, 0:CH], x3[0:CH, 0:CH])
                dve.tensor_copy(a_att[:, 0, CH:T], x3[:, CH:T])
                dve.tensor_copy(a_att[0:CH, 1, P:P + CH], x3[0:CH, T + P:T + P + CH])
                dve.tensor_copy(a_att[:, 1, P + CH:T], x3[:, T + P + CH:2 * T]).then_inc(att_evac, 1)
                los_head(9, 3)
                mod(h * 2 + (U_GLA + 1))
                dve.wait_ge(sg_act, h + 1)
                dve.tensor_tensor(a_sg, a_sg, pg[:, 0], ALU.mult).then_inc(pg_free, 1)
                recip_h = h + (S_GLA + 1)
                dve.wait_ge(std_done, recip_h)
                dve.reciprocal(rstd[:], rstd[:]).then_inc(rstd_done, 1)
                dve.wait_ge(rstd_done, recip_h)
                dve.wait_ge(pg_free, h * 3 + (G_GLA + 3))
                for e in range(2):
                    dve.wait_ge(o_lo, h * 2 + (O_GLA + e - 1))
                    for b in range(2):
                        k = 2 * e + b
                        ins = dve.scalar_tensor_tensor(out=ht[:, e, b * T:(b + 1) * T], in0=xo[:, e, b * T:(b + 1) * T],
                                                       scalar=cols[:, C_ON + k:C_ON + k + 1], in1=rstd[:],
                                                       op0=ALU.mult, op1=ALU.mult)
                    ins.then_inc(oa_norm, 1)
                    dve.wait_ge(oa_norm, h * 2 + e + 1)
                    dve.tensor_tensor(ht[:, e, :], ht[:, e, :],
                                      a_sg[:, 2 * e:2 * e + 2, :].rearrange("p b n -> p (b n)"), ALU.mult) \
                        .then_inc(og_mul, 1)

            def residual(t, g, set_, blk, gate):
                dve.wait_ge(mm_done, whole(t))
                for b in range(4):
                    ins = dve.scalar_tensor_tensor(out=xt[:, bass.ds(blk + b, 1), :].rearrange("p b n -> p (b n)"),
                                                   in0=pg[:, set_, b, :], scalar=mods[:, bass.ds(gate + b, 1)],
                                                   in1=xt[:, bass.ds(blk + b, 1), :].rearrange("p b n -> p (b n)"),
                                                   op0=ALU.mult, op1=ALU.add)
                ins.then_inc(pg_free, 1)

            def down(t0, g0, n, set0, gate_unit, rate=0, u0=0, peel=False):
                dve.wait_ge(pg_free, g0)
                dve.wait_ge(mods_done, gate_unit + 4)
                for i in steps(dve, n, peel):
                    for u in range(2):
                        last = peel and isinstance(i, int) and i == n - 1 and u == 1
                        los(t0 + 4 * u, 8, i, 1, 3 if last else 4, a_hits(u0, i, rate, u))
                        residual(i * 8 + (t0 + 4 * u + 4), None, (set0 + u) % 2, i * 8 + 4 * u,
                                 i * 8 + (4 * gate_unit + 4 * u))
                        mod_at(u0, i, rate, u)

            def ffn(layer):
                base = MOD0 if layer == 0 else MOD1
                for kind, t0, g0, o0, n, u0, rate, ch, b0 in ffn_plan(layer):
                    set0 = g0 % 2
                    if kind == "down":
                        down(t0, g0, n, set0, base + 20, rate, u0, peel=(layer == 1 and ch == 2))
                        continue
                    for i in steps(dve, n):
                        for u in range(2):
                            los(t0 + 4 * u, 8, i, 1, 4, a_hits(u0, i, rate, u))
                            dve.wait_ge(f_silu, i * 2 + (o0 + u + 1 - (O_FFN0, O_FFN1 - FF // T)[layer]))
                            dve.wait_ge(o_lo, i * 2 + (o0 + u - 1))
                            dve.tensor_tensor(f_a[:, u, :].rearrange("p (b n) -> p b n", b=2),
                                              f_s[:, u, :].rearrange("p (b n) -> p b n", b=2),
                                              pg[:, (set0 + u) % 2, 2:4], ALU.mult).then_inc(pg_free, 1)
                            mod_at(u0, i, rate, u)

            down(T_WOA, G_WOA, 2, 1, MOD0 + 8, 2, U_WOA)
            dve.wait_ge(mods_done, 20)
            gain(1, 16, C_NFFN)
            recip(S_NF0)
            norm_apply(O_NF0, 8, xt, avec[:, 1, :], mods[:, 12 * 4:12 * 4 + NB])
            ffn(0)
            dve.wait_ge(mods_done, U_DKV)
            gain(2, MODKV + 4, C_KVN)
            recip(S_NKV)
            norm_apply(O_NKV, 8, xt, avec[:, 0, :], mods[:, 4 * MODKV:4 * MODKV + NB])
            gain(3, MOD1 + 4, C_NMIX + NB)
            los(T_DKV, 4, 0, 1, 1)
            for j in range(4):
                norm_apply(O_NMX, 2 * j + 2, xt, avec[:, 1, :], mods[:, 4 * MOD1:4 * MOD1 + NB], first=2 * j)
                los(T_DKV, 4, 0, 2 + j, 1)
            dve.wait_ge(mm_done, whole(T_DKV + 4))
            dve.tensor_copy(latk, pg[:, 1]).then_inc(pg_free, 1)
            dve.wait_ge(mm_done, whole(T_KPE + 1))
            dve.tensor_copy(kpf, pg[0:ROPE, 0, 0, :]).then_inc(pg_free, 1)
            los(T_DQ, 4, 0, 1, 1, [(U_DKV, 0)])
            dve.wait_ge(pos_ld, 32)
            dve.wait_ge(cst_done, 6)
            dve.tensor_copy(posf, posi[:]).then_inc(rot_c, 1)
            dve.wait_ge(rot_c, 1)
            for t in range(2):
                ins = dve.tensor_scalar(ang[:, t, :], invf[:, 0:HALF], posf[:, t:t + 1], None, ALU.mult)
            ins.then_inc(rot_c, 1)
            dve.wait_ge(rot_c, 2)
            dve.tensor_scalar(angk, ang, float(1.0 / TWO_PI), MAGIC, ALU.mult, ALU.add).then_inc(rot_c, 1)
            dve.wait_ge(rot_c, 3)
            dve.tensor_scalar(angk, angk, MAGIC, None, ALU.subtract).then_inc(rot_c, 1)
            for k, part in enumerate((PI_A, PI_B, PI_C)):
                dve.wait_ge(rot_c, 4 + k)
                dve.scalar_tensor_tensor(out=ang, in0=angk, scalar=-part, in1=ang, op0=ALU.mult, op1=ALU.add) \
                    .then_inc(rot_c, 1)
            dve.wait_ge(rot_c, 7)
            dve.tensor_scalar(ang, ang, 3.1415925, -3.1415925, ALU.min, ALU.max).then_inc(rot_c, 1)
            dve.wait_ge(kp_tr, 1)
            dve.tensor_copy(kpe[:], x3[:, 0:2 * ROPE].rearrange("p (t n) -> p t n", t=2)).then_inc(kp_in, 1)
            los(T_DQ, 4, 0, 2, 1, [(U_DKV, 1)])
            recip(S_LKV)
            norm_apply(O_LKV, 2, latk, cols[:, C_KL:C_KL + LB], None)
            los(T_DQ, 4, 0, 3, 2, [(U_DKV, 2), (U_DKV, 3)])
            dve.wait_ge(kp_rot, 2)
            dve.tensor_tensor(krw, kpe[:], kpe[:], ALU.mult).then_inc(kp_ss, 1)
            dve.wait_ge(kp_ss, 1)
            dve.tensor_reduce(kss, krw, AX.X, ALU.add).then_inc(kp_ss, 1)
            dve.wait_ge(mm_done, whole(T_DQ + 4))
            dve.tensor_copy(latq, pg[:, 1]).then_inc(pg_free, 1)
            mod(U_DKV)
            recip(S_LQ)
            norm_apply(O_LQ, 2, latq, cols[:, C_QL:C_QL + LB], None)
            dve.wait_ge(kp_ss, 2)

            def bring_q(pr, par):
                dve.wait_ge(mm_done, whole(pr * 2 + (T_MLA + 1)))
                dve.tensor_copy(b_q[par], pt[:, 0, :, 0:2 * QKD]).then_inc(pg_free, 1)

            def bring_kv(pr, par):
                dve.wait_ge(mm_done, whole(pr * 2 + (T_MLA + 2)))
                dve.tensor_copy(b_kv[par], pt[:, 1]).then_inc(pg_free, 1)

            def sum_q(pr):
                dve.wait_ge(bsq, pr * 2 + 1)
                dve.tensor_reduce(b_st[:, 0:4], b_sq.rearrange("p (a n) -> p a n", a=4), AX.X, ALU.add) \
                    .then_inc(bst, 1)

            def sum_k(pr):
                dve.wait_ge(bsq, pr * 2 + 2)
                dve.tensor_reduce(b_st[:, 4:8], b_sq[:, 0:512].rearrange("p (a n) -> p a n", a=4), AX.X, ALU.add) \
                    .then_inc(bst, 1)
                dve.wait_ge(bst, pr * 3 + 2)
                k_st = b_st[:, 4:8].rearrange("p (t h) -> p t h", t=2)
                dve.tensor_tensor(k_st, k_st, kss[:, :, None].broadcast_to([P, 2, 2]), ALU.add).then_inc(bst, 1)

            def scale_qk(pr, par):
                dve.wait_ge(bstd, pr + 1)
                dve.reciprocal(b_st, b_st).then_inc(brs, 1)
                dve.wait_ge(brs, pr + 1)
                q4 = b_q[par].rearrange("p t (h n) -> p t h n", h=2)
                k4 = b_kv[par].rearrange("p t (h n) -> p t h n", h=2)[:, :, :, 0:NOPE]
                r4 = b_st.rearrange("p (a t h) -> p a t h", a=2, t=2)
                dve.tensor_tensor(b_qp, q4[:, :, :, NOPE:QKD], r4[:, 0, :, :, None].broadcast_to([P, 2, 2, ROPE]),
                                  ALU.mult)
                q4 = q4[:, :, :, 0:NOPE]
                dve.tensor_tensor(q4, q4, r4[:, 0, :, :, None].broadcast_to([P, 2, 2, NOPE]), ALU.mult) \
                    .then_inc(bqk, 1)
                dve.tensor_tensor(k4, k4, r4[:, 1, :, :, None].broadcast_to([P, 2, 2, NOPE]), ALU.mult)
                dve.tensor_tensor(b_kp, kpe[:, :, None, :].broadcast_to([P, 2, 2, ROPE]),
                                  r4[:, 1, :, :, None].broadcast_to([P, 2, 2, ROPE]), ALU.mult).then_inc(bqk, 1)

            los(T_MLA, 4, 0, 1, 1)
            bring_q(0, 0)
            los(T_MLA, 4, 0, 2, 1)
            ada(U_PAIR, 0)
            bring_kv(0, 0)
            sum_q(0)
            sum_k(0)
            ada(U_PAIR, 1)
            scale_qk(0, 0)
            los(T_MLA, 4, 0, 3, 1)
            for pr, i, u in pairs(dve):
                nxt = not isinstance(pr, int) or pr < PAIRS - 1
                if nxt:
                    bring_q(pr + 1, (u + 1) % 2)
                    ada(pr + U_PAIR, 2)
                for h in range(2):
                    s = (xo[:, 0, 0:3 * P], x3[:, 0:3 * P])[h]
                    d0 = pr * 4 + 2 * h
                    dve.wait_ge(s_ready, pr * 2 + h + 1)
                    dve.scalar_tensor_tensor(out=b_p[:, h, :], in0=s, scalar=float(QKD) ** -0.5,
                                             in1=mask[:].rearrange("p b n -> p (b n)"), op0=ALU.mult,
                                             op1=ALU.add).then_inc(s_dve, 1)
                    dve.wait_ge(s_dve, d0 + 1)
                    dve.tensor_reduce(b_mx[:, 2 * h:2 * h + 1], b_p[:, h, 0:P], AX.X, ALU.max)
                    dve.tensor_reduce(b_mx[:, 2 * h + 1:2 * h + 2], b_p[:, h, P:3 * P], AX.X, ALU.max) \
                        .then_inc(s_dve, 1)
                    dve.wait_ge(s_dve, d0 + 2)
                    dve.tensor_scalar(b_mx[:, 2 * h:2 * h + 2], b_mx[:, 2 * h:2 * h + 2], -1.0, None, ALU.mult) \
                        .then_inc(s_mx, 1)
                for h in range(2):
                    dve.wait_ge(s_exp, pr * 2 + h + 1)
                    dve.reciprocal(b_sm[:, 2 * h:2 * h + 2], b_sm[:, 2 * h:2 * h + 2]).then_inc(s_rcp, 1)
                if nxt:
                    sum_q(pr + 1)
                    bring_kv(pr + 1, (u + 1) % 2)
                    ada(pr + U_PAIR, 3)
                    sum_k(pr + 1)
                    scale_qk(pr + 1, (u + 1) % 2)
                if not isinstance(pr, int):
                    los(T_MLA + 2 * u, 4, i, 4, 1)
                elif not nxt:
                    los(T_WOB, 4, 0, 0, 1)
                if nxt:
                    mod(pr + U_PAIR)
                if not isinstance(pr, int):
                    ada(pr + (U_PAIR + 1), 0)
                    ada(pr + (U_PAIR + 1), 1)
                    los(T_MLA + 2 * u, 4, i, 5, 1)
            down(T_WOB, G_WOB, 2, 0, MOD1 + 8, 2, U_WOB)
            dve.wait_ge(mods_done, 52)
            gain(4, MOD1 + 16, C_NFFN + NB)
            recip(S_NF1)
            norm_apply(O_NF1, 8, xt, avec[:, 0, :], mods[:, 4 * (MOD1 + 12):4 * (MOD1 + 12) + NB])
            ffn(1)
            for g in range(8):
                dve.wait_ge(y_tr, g + 1)
                dve.tensor_copy(xio[:, g // 4, (g % 4) * 512:(g % 4 + 1) * 512], y_bank(g)).then_inc(y_ev, 1)

        @block.tensor
        def _(pe):
            def split3(dst, w, x_, start, stop):
                (w_h, w_l), (x_h, x_l) = w, x_
                pe.matmul(dst, w_h, x_h, start=start, stop=False, skip_group_check=True)
                pe.matmul(dst, w_h, x_l, start=False, stop=False, skip_group_check=True)
                return pe.matmul(dst, w_l, x_h, start=False, stop=stop, skip_group_check=True)

            def feature_tile(t, s2, set_, kts, k0, right, j, last_j):
                r_hi, r_lo = right
                for h, (ka, kb) in enumerate(halves(kts)):
                    pe.wait_ge(lo_done, whole(t) + (h + 1))
                    for k in range(ka, kb):
                        for b in range(4):
                            c0 = h * 1024 + (k - ka) * GW + b * P
                            ins = split3(pg[:, set_, b, :], (whi[:, s2, c0:c0 + P], wlo[:, s2, c0:c0 + P]),
                                         (r_hi[:, k0 + k, :], r_lo[:, k0 + k, :]),
                                         start=(j == 0 and k == 0 and b % 2 == 0), stop=(j == last_j and k == kts - 1))
                    ins.then_inc(mm_done, 1)

            def token_tile(t, s2, set_, kts, n, k0, left, first, last):
                l_hi, l_lo = left
                for h, (ka, kb) in enumerate(halves(kts)):
                    pe.wait_ge(lo_done, whole(t) + (h + 1))
                    for k in range(ka, kb):
                        c0 = h * 1024 + (k - ka) * n
                        for tt in range(2):
                            w_h, w_l = whi[:, s2, c0:c0 + n], wlo[:, s2, c0:c0 + n]
                            a_h = l_hi[:, k0 + k, tt * P:(tt + 1) * P]
                            a_lw = l_lo[:, k0 + k, tt * P:(tt + 1) * P]
                            ins = split3(pt[:, set_, tt, 0:n], (a_h, a_lw), (w_h, w_l),
                                         start=(first and k == 0), stop=(last and k == kts - 1))
                    ins.then_inc(mm_done, 1)

            def narrow_tile(t, s2, dst, n, right, o_wait):
                r_hi, r_lo = right
                for h, (ka, kb) in enumerate(halves(NB)):
                    pe.wait_ge(lo_done, whole(t) + (h + 1))
                    pe.wait_ge(o_lo, o_wait + kb // 2)
                    for k in range(ka, kb):
                        c0 = h * 1024 + (k - ka) * n
                        ins = split3(dst, (whi[:, s2, c0:c0 + n], wlo[:, s2, c0:c0 + n]), (r_hi[:, k, :], r_lo[:, k, :]),
                                     start=(k == 0), stop=(k == NB - 1))
                    ins.then_inc(mm_done, 1)

            def reduce_unit(unit, std, sums=acc):
                pe.wait_ge(ada_sum, unit + 1)
                if not isinstance(unit, int) or unit:
                    pe.wait_ge(mods_done, unit)
                if std is not None:
                    pe.wait_ge(std_done, std)
                for b in range(4):
                    ins = pe.matmul(x2[:, 508 + b:509 + b], sums[:, 0, b * P:(b + 1) * P], ones[:, 0:1],
                                    start=True, stop=True)
                ins.then_inc(modp_ready, 1)

            def sumsq(e0, n, units, s):
                if units:
                    pe.wait_ge(mods_done, units)
                    pe.wait_ge(std_done, s)
                for j in range(n):
                    pe.wait_ge(sq_done, e0 + j + 1)
                    for b in range(2):
                        ins = pe.matmul(x2[:, 0:T], ones[:], sq[:, j % 2, b * T:(b + 1) * T],
                                        start=(j == 0 and b == 0), stop=(j == n - 1 and b == 1))
                    ins.then_inc(ssq_mm, 1)

            pe.wait_ge(cst_done, 2)
            pe.wait_ge(c_ld, 16)
            pe.matmul(x2[:, 0:NB], crow, ident[0:NB, 0:NB], start=True, stop=True).then_inc(c_tr, 1)
            pe.wait_ge(par_ld, par_dmas * 16)
            for k in range(3):
                n = min(P, C_END - k * P)
                ins = pe.matmul(x3[:, k * P:k * P + n], vrow[0:n, k, :], ident[0:n, 0:n], start=True, stop=True)
            ins.then_inc(tr_ready, 1)
            pe.wait_ge(x_ld, 16)
            for g in range(4):
                if g >= 2:
                    pe.wait_ge(tr_evac, g)
                for b in range(4):
                    for tt in range(2):
                        ins = pe.matmul(pg[:, g % 2, b, tt * P:(tt + 1) * P],
                                        xio[:, tt, (4 * g + b) * P:(4 * g + b + 1) * P], ident[:], start=True, stop=True)
                ins.then_inc(tr_ready, 1)
            pe.wait_ge(dcst_done, 1)
            pe.wait_ge(s_silu, 1)
            reduce_unit(0, None, acc_start(0))
            pe.wait_ge(mods_done, 1)
            sumsq(E_N0, 8, 0, 0)
            for u in range(1, 8):
                reduce_unit(u, 1, acc_start(u))

            h2 = (hhi, hlo)
            a2 = (ahi, alo)
            pe.wait_ge(tr_evac, 5)
            narrow_tile(0, 0, pg[0:RANK, 1, 0, :], RANK, h2, O_N0)
            pe.wait_ge(pg_free, G_LOW + 1)

            with pe.Fori(0, HEADS_A) as h:
                pe.wait_ge(wah_ld, h * 16 + 16)
                pe.wait_ge(std_done, h + S_GLA)
                pe.wait_ge(mods_done, h * 2 + U_GLA)
                for b in range(2):
                    ins = pe.matmul(x2[:, b * T:(b + 1) * T], wah[:, b * P:(b + 1) * P], alrt, start=True, stop=True)
                ins.then_inc(la_ready, 1)
                pe.wait_ge(pg_free, h * 3 + G_GLA)
                for j in range(4):
                    feature_tile(h * 12 + (T_GLA + j), (T_GLA + j) % 2, 0, 4, 4 * j, h2, j, 3)
                pe.wait_ge(pg_free, h * 3 + G_GLA)
                for j in range(4):
                    token_tile(h * 12 + (T_GLA + 4 + j), (T_GLA + j) % 2, 1, 4, GW, 4 * j, h2, j == 0, j == 3)
                    if j == 0:
                        pe.wait_ge(la_act, h * 4 + 1)
                        reduce_unit(h * 2 + U_GLA, None)
                pe.wait_ge(kq_ready, h + 1)
                for n in range(NCH):
                    for kt in range((n + 2) // 2):
                        m = min(P, CH * (n + 1) - kt * P)
                        for b in range(2):
                            c0 = KOFF[n] + kt * P
                            ins = pe.matmul(x3[0:m, kt * T + CH * n:kt * T + CH * (n + 1)], a_e[:, b, c0:c0 + m],
                                            a_qd[:, b, CH * n:CH * (n + 1)], start=(b == 0), stop=(b == 1))
                ins.then_inc(att_ready, 1)
                pe.wait_ge(pg_free, h * 3 + (G_GLA + 1))
                for j in range(4):
                    feature_tile(h * 12 + (T_GLA + 8 + j), (T_GLA + j) % 2, 0, 4, 4 * j, h2, j, 3)
                    if j == 2:
                        reduce_unit(h * 2 + (U_GLA + 1), None)
                pe.wait_ge(att_msk, h + 1)
                pe.wait_ge(o_hi, h * 2 + O_GLA)
                for b in range(4):
                    v = [a_v[:, kt, b * P:(b + 1) * P] for kt in range(2)]
                    o = xo[:, b // 2, (b % 2) * T:(b % 2 + 1) * T]
                    pe.matmul(o, v[0], a_att[:, 0, :], start=True, stop=False, skip_group_check=True)
                    ins = pe.matmul(o[:, P:T], v[1], a_att[:, 1, P:T], start=False, stop=True, skip_group_check=True)
                ins.then_inc(oa_ready, 1)
                pe.wait_ge(mods_done, h * 2 + (U_GLA + 2))
                for e in range(2):
                    pe.wait_ge(sq_done, h * 2 + (E_GLA + e + 1))
                    for b in range(2):
                        ins = pe.matmul(x2[:, 0:T], ones[:], sq[:, e, b * T:(b + 1) * T],
                                        start=(e == 0 and b == 0), stop=(e == 1 and b == 1))
                    ins.then_inc(ssq_mm, 1)

            def sum_group(g, e0, s):
                if g == 0:
                    pe.wait_ge(std_done, s)
                for e in range(2):
                    pe.wait_ge(sq_done, e0 + 2 * g + e + 1)
                    for b in range(2):
                        ins = pe.matmul(x3[:, 0:T], ones[:], sq[:, e, b * T:(b + 1) * T],
                                        start=(g == 0 and e == 0 and b == 0), stop=(g == 3 and e == 1 and b == 1))
                    ins.then_inc(ssq_mm, 1)

            def product(t0, g0, n, set0, right, kts=4, o_wait=None, rate=0, u0=0, std=None, sums=None):
                for i in steps(pe, n) if sums is None else range(n):
                    for u in range(2):
                        pe.wait_ge(pg_free, i * 2 + (g0 + u - 1))
                        for j in range(4):
                            if u == 0 and o_wait is not None:
                                pe.wait_ge(o_lo, o_wait + ((j + 1) * kts + 1) // 2)
                            feature_tile(i * 8 + (t0 + 4 * u + j), (t0 + j) % 2, (set0 + u) % 2, kts, kts * j, right,
                                         j, 3)
                            if sums is not None and j == 1 and 2 * i + u > 0:
                                sum_group(2 * i + u - 1, *sums)
                        if rate == 2 or (rate == 1 and u == 1):
                            reduce_unit(i * rate + (u0 + (u if rate == 2 else 0)), std)
                if sums is not None:
                    sum_group(2 * n - 1, *sums)

            def ffn(layer):
                o_n = O_NF0 if layer == 0 else O_NF1
                for kind, t0, g0, o0, n, u0, rate, ch, b0 in ffn_plan(layer):
                    set0 = g0 % 2
                    std = (S_NF0 if layer == 0 else S_NF1) + 1
                    if kind == "up":
                        product(t0, g0, n, set0, h2, 4, o_n, rate, u0, std)
                    else:
                        product(t0, g0, n, set0, a2, FFC[ch] // 2, o0, rate, u0, std,
                                (E_NKV, S_NKV) if layer == 0 and ch == 2 else None)

            product(T_WOA, G_WOA, 2, 1, a2, 4, O_GLA, 2, U_WOA, S_NF0, (E_NF0, S_NF0))
            ffn(0)
            pe.wait_ge(pg_free, G_DKV)
            for j in range(4):
                pe.wait_ge(o_lo, O_NKV + 2 * (j + 1))
                feature_tile(T_DKV + j, (T_DKV + j) % 2, 1, 4, 4 * j, a2, j, 3)
            narrow_tile(T_KPE, T_KPE % 2, pg[0:ROPE, 0, 0, :], ROPE, a2, O_NKV)
            pe.wait_ge(pg_free, G_DKV + 1)
            for j in range(4):
                pe.wait_ge(o_lo, O_NMX + 2 * (j + 1))
                feature_tile(T_DQ + j, (T_DQ + j) % 2, 1, 4, 4 * j, h2, j, 3)
                if j == 0:
                    pe.wait_ge(pg_free, G_KPE + 1)
                    for tt in range(2):
                        ins = pe.matmul(x3[:, tt * ROPE:(tt + 1) * ROPE], kpf[:, tt * P:(tt + 1) * P],
                                        ident[0:ROPE, 0:ROPE], start=True, stop=True)
                    ins.then_inc(kp_tr, 1)
                if j == 1:
                    sumsq(E_LKV, 2, U_DKV, S_LKV)
            reduce_unit(U_DKV, S_LKV + 1)
            sumsq(E_LQ, 2, U_PAIR, S_LQ)
            pe.wait_ge(o_lo, O_LQ + 2)

            def project_q(pr):
                pe.wait_ge(pg_free, pr * 2 + (G_MLA - 1))
                token_tile(pr * 2 + T_MLA, T_MLA % 2, 0, LB, 2 * QKD, LB, a2, True, True)

            def project_kv(pr):
                pe.wait_ge(pg_free, pr * 2 + G_MLA)
                token_tile(pr * 2 + (T_MLA + 1), (T_MLA + 1) % 2, 1, LB, 2 * (NOPE + VD), 0, a2, True, True)

            project_q(0)
            project_kv(0)
            for pr, i, u in pairs(pe):
                nxt = not isinstance(pr, int) or pr < PAIRS - 1
                q, kv = b_q[u], b_kv[u]
                pe.wait_ge(bqk, pr * 2 + 1)
                for hh in range(2):
                    for tt in range(2):
                        pe.matmul(xo[:, 0, hh * T + tt * P:hh * T + (tt + 1) * P],
                                  q[:, tt, hh * QKD:hh * QKD + NOPE], ident[:], start=True, stop=True)
                for tt in range(2):
                    ins = pe.matmul(xo[:, 1, tt * P:(tt + 1) * P], b_qp[:, tt].rearrange("p h n -> p (h n)"), ident[:],
                                    start=True, stop=True)
                ins.then_inc(tq_ready, 1)
                pe.wait_ge(bqk, pr * 2 + 2)
                pe.wait_ge(o_hi, pr + O_MLA)
                for hh in range(2):
                    for tt in range(2):
                        pe.matmul(x3[:, hh * T + tt * P:hh * T + (tt + 1) * P],
                                  kv[:, tt, hh * 256:hh * 256 + NOPE], ident[:], start=True, stop=True)
                for tt in range(2):
                    ins = pe.matmul(xo[:, 1, T + tt * P:T + (tt + 1) * P], b_kp[:, tt].rearrange("p h n -> p (h n)"),
                                    ident[:], start=True, stop=True)
                ins.then_inc(tk_ready, 1)
                if nxt:
                    project_q(pr + 1)
                pe.wait_ge(te_act, pr + 1)
                for hh in range(2):
                    dst = (xo[:, 0, :], x3[:, :])[hh]
                    r0 = hh * ROPE
                    for qt, (c0, n) in enumerate(((0, P), (P, T))):
                        pe.matmul(dst[:, c0:c0 + n], b_qt[:, hh, qt * P:(qt + 1) * P], b_kt[:, hh, 0:n],
                                  start=True, stop=False)
                        ins = pe.matmul(dst[:, c0:c0 + n], b_rt[r0:r0 + ROPE, 0, qt * P:(qt + 1) * P],
                                        b_rt[r0:r0 + ROPE, 1, 0:n], start=False, stop=True)
                    ins.then_inc(s_ready, 1)
                if nxt:
                    project_kv(pr + 1)
                for hh in range(2):
                    pe.wait_ge(p_ready, pr * 2 + hh + 1)
                    for b in range(3):
                        ins = pe.matmul(xo[:, 1 - hh, b * P:(b + 1) * P], b_p[:, hh, b * P:(b + 1) * P], ident[:],
                                        start=True, stop=True)
                    ins.then_inc(pt_ready, 1)
                for hh in range(2):
                    pe.wait_ge(pt_evac, pr * 2 + hh + 1)
                    v = [kv[:, kt, hh * 256 + NOPE:hh * 256 + NOPE + VD] for kt in range(2)]
                    pe.matmul(x3[:, hh * T:(hh + 1) * T], v[0], b_pt[:, hh, 0:T], start=True, stop=False,
                              skip_group_check=True)
                    ins = pe.matmul(x3[:, hh * T + P:(hh + 1) * T], v[1], b_pt[:, hh, T:3 * P], start=False,
                                    stop=True, skip_group_check=True)
                ins.then_inc(ob_ready, 1)
                if nxt:
                    reduce_unit(pr + U_PAIR, S_LQ + 1)
            product(T_WOB, G_WOB, 2, 0, h2, 4, O_MLA, 2, U_WOB, S_LQ + 1, (E_NF1, S_NF1))
            ffn(1)
            pe.wait_ge(pg_free, G_END)
            for g in range(8):
                if g >= 4:
                    pe.wait_ge(y_ev, g - 3)
                for b in range(4):
                    ins = pe.matmul(y_bank(g)[:, b * P:(b + 1) * P],
                                    xt[:, 4 * (g % 4) + b, (g // 4) * P:(g // 4 + 1) * P], ident[:], start=True, stop=True)
                ins.then_inc(y_tr, 1)


_INS = ["x", "c", "positions", "ada_w", "ada_b", "norm_mix", "norm_ffn", "gla_w_in", "gla_w_alpha", "gla_b_alpha",
        "gla_onorm", "gla_w_out", "mla_w_dq", "mla_q_lat_norm", "mla_w_uq", "mla_q_norm", "mla_w_out", "kv_ada_w",
        "kv_ada_b", "kv_norm", "kv_w_dkv", "kv_lat_norm", "kv_w_ukv", "kv_k_norm", "ffn_w_gu", "ffn_w_down"]


def kernel(**inputs):
    import concourse.bacc as bacc
    from concourse.bass_utils import run_bass_kernel_spmd

    nc = bacc.Bacc("TRN2", target_bir_lowering=False, num_devices=1)
    arrays, args = {}, []
    for name in _INS:
        a = np.ascontiguousarray(inputs[name])
        arrays["in_" + name] = a
        args.append(nc.dram_tensor("in_" + name, a.shape, mybir.dt.from_np(a.dtype), kind="ExternalInput").ap())
    args.append(nc.dram_tensor("out_0", (1, T, D), F32, kind="ExternalOutput").ap())
    trunk(nc, *args)
    r = run_bass_kernel_spmd(nc, [arrays], core_ids=[0])
    return r.results[0]["out_0"]
```
